# Optimizing a Trainium2 kernel written in Bass

```python
import math
import jax
import jax.numpy as jnp
from jax import lax
import numpy as np

D_MODEL = 1024
BATCH = 1
SEQ = 256
DEPTH = 2

HEAD_DIM = 64
ROPE_DIM = HEAD_DIM // 4
ROPE_THETA = 500000.0
NORM_EPS = 1e-6
Q_BLOCK = 128

A_HEADS = D_MODEL // 128
A_WIDTH = A_HEADS * HEAD_DIM
A_PATTERNS = ((128, 1), (512, 4), (2048, 16))

B_WIDTH = D_MODEL - A_WIDTH
B_GROUP = 16
B_GROUPS = B_WIDTH // B_GROUP
B_STATE = 64
DT_MIN = 1e-3
DT_MAX = 1e-1

C_HEADS = D_MODEL // HEAD_DIM
C_NOPE = HEAD_DIM - ROPE_DIM
C_VDIM = HEAD_DIM
C_LATENT = D_MODEL // 4
IDX_HEADS = 8
IDX_DIM = 64
TOPK_MAX = 256
C_SPLITS = (C_HEADS * ROPE_DIM, C_HEADS * C_NOPE, C_LATENT, ROPE_DIM, IDX_HEADS * IDX_DIM, IDX_DIM)
C_IN = sum(C_SPLITS) + IDX_HEADS

FF_DENSE = ((8 * D_MODEL // 3 + 127) // 128) * 128
N_EXPERTS = 8
TOP_K_EXPERTS = 2
FF_EXPERT = 7 * D_MODEL // 2

kernel_name = 'hybrid_dilated_s5_dsa_moe_adaln'

def rms_norm(x, g):
    xf = x.astype(jnp.float32)
    y = xf * lax.rsqrt(jnp.mean(xf * xf, axis=-1, keepdims=True) + NORM_EPS)
    return (y * g.astype(jnp.float32)).astype(x.dtype)

def modulate(x, shift, scale):
    return x * (1 + scale[:, None, :]) + shift[:, None, :]

def rope_tables(seq):
    pos = jnp.arange(seq, dtype=jnp.float32)
    inv = ROPE_THETA ** (-jnp.arange(0, ROPE_DIM, 2, dtype=jnp.float32) / ROPE_DIM)
    ang = pos[:, None] * inv[None, :]
    return jnp.cos(ang), jnp.sin(ang)

def apply_rope(x, cos, sin):
    half = ROPE_DIM // 2
    xf = x.astype(jnp.float32)
    x1, x2, rest = xf[..., :half], xf[..., half:ROPE_DIM], xf[..., ROPE_DIM:]
    cs, sn = cos[:, None, :], sin[:, None, :]
    out = jnp.concatenate([x1 * cs - x2 * sn, x2 * cs + x1 * sn, rest], axis=-1)
    return out.astype(x.dtype)

def to_blocks(a):
    bn, s = a.shape[:2]
    return jnp.moveaxis(a.reshape((bn, s // Q_BLOCK, Q_BLOCK) + a.shape[2:]), 1, 0)

def from_blocks(a):
    a = jnp.moveaxis(a, 0, 1)
    return a.reshape((a.shape[0], a.shape[1] * a.shape[2]) + a.shape[3:])

def gather_rows(a, idx):
    return jax.vmap(lambda ab, ib: ab[ib])(a, idx)

def swiglu(u, w_gate, w_up, w_down):
    return (jax.nn.silu(u @ w_gate) * (u @ w_up)) @ w_down

def dilated_attention(q, k, v):
    bn, s, h, dh = q.shape
    f32 = jnp.float32
    scale = dh ** -0.5

    def block(args):
        blk, qb = args
        t = blk * Q_BLOCK + jnp.arange(Q_BLOCK)
        qf = qb.astype(f32) * scale
        ms, ls, os_ = [], [], []
        for window, dil in A_PATTERNS:
            n_keys = window // dil + 1
            src = t[:, None] - dil * jnp.arange(n_keys)[None, :]
            valid = src >= 0
            src = jnp.maximum(src, 0)
            kg = jnp.take(k, src, axis=1).astype(f32)
            vg = jnp.take(v, src, axis=1).astype(f32)
            sc = jnp.einsum('bqhd,bqnhd->bhqn', qf, kg)
            sc = jnp.where(valid[None, None], sc, -jnp.inf)
            m = jnp.max(sc, axis=-1)
            p = jnp.exp(sc - m[..., None])
            ms.append(m)
            ls.append(jnp.sum(p, axis=-1))
            os_.append(jnp.einsum('bhqn,bqnhd->bhqd', p, vg))
        m_st = jnp.stack(ms)
        wts = jnp.exp(m_st - jnp.max(m_st, axis=0, keepdims=True))
        den = jnp.sum(wts * jnp.stack(ls), axis=0)
        num = jnp.einsum('gbhq,gbhqd->bhqd', wts, jnp.stack(os_))
        out = num / den[..., None]
        return jnp.swapaxes(out, 1, 2).astype(q.dtype)

    out = lax.map(block, (jnp.arange(s // Q_BLOCK), to_blocks(q)))
    return from_blocks(out)

def _complex_affine_combine(e1, e2):
    a1r, a1i, b1r, b1i = e1
    a2r, a2i, b2r, b2i = e2
    ar = a2r * a1r - a2i * a1i
    ai = a2r * a1i + a2i * a1r
    br = a2r * b1r - a2i * b1i + b2r
    bi = a2r * b1i + a2i * b1r + b2i
    return ar, ai, br, bi

def s5_mixer(u, a_re, a_im, log_dt, b_re, b_im, c_re, c_im, d_skip, w_glu, b_glu):
    bn, s, _ = u.shape
    f32 = jnp.float32
    ug = u.reshape(bn, s, B_GROUPS, B_GROUP).astype(f32)
    dt = jnp.exp(log_dt.astype(f32))[:, None]
    lr, li = a_re.astype(f32), a_im.astype(f32)
    mag = jnp.exp(lr * dt)
    abar_r = mag * jnp.cos(li * dt)
    abar_i = mag * jnp.sin(li * dt)
    den = lr * lr + li * li
    nr = abar_r - 1.0
    fr = (nr * lr + abar_i * li) / den
    fi = (abar_i * lr - nr * li) / den
    br, bi = b_re.astype(f32), b_im.astype(f32)
    bbar_r = fr[..., None] * br - fi[..., None] * bi
    bbar_i = fr[..., None] * bi + fi[..., None] * br
    bu_r = jnp.einsum('bsgc,gpc->bsgp', ug, bbar_r)
    bu_i = jnp.einsum('bsgc,gpc->bsgp', ug, bbar_i)
    full = bu_r.shape
    _, _, xr, xi = lax.associative_scan(
        _complex_affine_combine,
        (jnp.broadcast_to(abar_r, full), jnp.broadcast_to(abar_i, full), bu_r, bu_i),
        axis=1)
    y = (jnp.einsum('bsgp,gcp->bsgc', xr, c_re.astype(f32))
         - jnp.einsum('bsgp,gcp->bsgc', xi, c_im.astype(f32))
         + d_skip.astype(f32) * ug)
    y = jax.nn.gelu(y.reshape(bn, s, B_WIDTH)).astype(u.dtype)
    return y * jax.nn.sigmoid(y @ w_glu + b_glu)

def even_mixer(u, cos, sin, w_in, w_out, a_re, a_im, log_dt, b_re, b_im, c_re, c_im,
               d_skip, w_glu, b_glu):
    bn, s, _ = u.shape
    proj = u @ w_in
    q, k, v, s_in = jnp.split(proj, [A_WIDTH, 2 * A_WIDTH, 3 * A_WIDTH], axis=-1)
    shp = (bn, s, A_HEADS, HEAD_DIM)
    q = apply_rope(q.reshape(shp), cos, sin)
    k = apply_rope(k.reshape(shp), cos, sin)
    v = v.reshape(shp)
    y_a = dilated_attention(q, k, v).reshape(bn, s, A_WIDTH)
    y_b = s5_mixer(s_in, a_re, a_im, log_dt, b_re, b_im, c_re, c_im, d_skip, w_glu, b_glu)
    return jnp.concatenate([y_a, y_b], axis=-1) @ w_out

def dsa_mixer(u, cos, sin, w_in, w_out, g_kv, w_uk, w_uv):
    bn, s, _ = u.shape
    f32 = jnp.float32
    topk = min(TOPK_MAX, s // 4)
    proj = u @ w_in
    cuts = [int(v) for v in np.cumsum(C_SPLITS)]
    q_r, q_n, ckv, k_r, q_i, k_i, w_i = jnp.split(proj, cuts, axis=-1)
    q_r = apply_rope(q_r.reshape(bn, s, C_HEADS, ROPE_DIM), cos, sin)
    q_n = q_n.reshape(bn, s, C_HEADS, C_NOPE)
    ckv = rms_norm(ckv, g_kv)
    k_r = apply_rope(k_r.reshape(bn, s, 1, ROPE_DIM), cos, sin)[:, :, 0]
    q_i = apply_rope(q_i.reshape(bn, s, IDX_HEADS, IDX_DIM), cos, sin)
    k_i = apply_rope(k_i.reshape(bn, s, 1, IDX_DIM), cos, sin)[:, :, 0]
    w_i = w_i * IDX_HEADS ** -0.5
    key_pos = jnp.arange(s)

    def block(args):
        blk, qr_b, qn_b, qi_b, wi_b = args
        t = blk * Q_BLOCK + jnp.arange(Q_BLOCK)
        logits = jnp.einsum('bqhd,bsd->bqhs', qi_b.astype(f32), k_i.astype(f32)) * IDX_DIM ** -0.5
        score = jnp.einsum('bqh,bqhs->bqs', wi_b.astype(f32), jax.nn.relu(logits))
        causal = key_pos[None, :] <= t[:, None]
        score = jnp.where(causal[None], score, -jnp.inf)
        _, idx = lax.top_k(score, topk)
        valid = idx <= t[None, :, None]
        ckv_g = gather_rows(ckv, idx).astype(f32)
        kr_g = gather_rows(k_r, idx).astype(f32)
        q_lat = jnp.einsum('bqhn,chn->bqhc', qn_b.astype(f32), w_uk.astype(f32))
        sc = (jnp.einsum('bqhc,bqkc->bhqk', q_lat, ckv_g)
              + jnp.einsum('bqhr,bqkr->bhqk', qr_b.astype(f32), kr_g)) * HEAD_DIM ** -0.5
        sc = jnp.where(valid[:, None], sc, -jnp.inf)
        p = jax.nn.softmax(sc, axis=-1)
        o_lat = jnp.einsum('bhqk,bqkc->bqhc', p, ckv_g)
        return jnp.einsum('bqhc,chd->bqhd', o_lat, w_uv.astype(f32)).astype(u.dtype)

    out = lax.map(block, (jnp.arange(s // Q_BLOCK), to_blocks(q_r), to_blocks(q_n),
                          to_blocks(q_i), to_blocks(w_i)))
    out = from_blocks(out).reshape(bn, s, C_HEADS * C_VDIM)
    return out @ w_out

def moe_swiglu(u, w_router, b_router, w_gate, w_up, w_down):
    bn, s, d = u.shape
    f32 = jnp.float32
    tok = u.reshape(bn * s, d)
    logits = tok.astype(f32) @ w_router.astype(f32) + b_router.astype(f32)
    top_val, top_idx = lax.top_k(logits, TOP_K_EXPERTS)
    gates = jax.nn.softmax(top_val, axis=-1)
    combine = jnp.einsum('tk,tke->te', gates, jax.nn.one_hot(top_idx, N_EXPERTS, dtype=f32))
    out = jnp.zeros((bn * s, d), f32)
    for e in range(N_EXPERTS):
        out = out + combine[:, e:e + 1] * swiglu(tok, w_gate[e], w_up[e], w_down[e]).astype(f32)
    return out.astype(u.dtype).reshape(bn, s, d)

def setup_inputs(seed: int = 0) -> dict:
    key = jax.random.key(seed)
    keys = iter(jax.random.split(key, 48))
    f32 = jnp.float32

    def nrm(shape, scale):
        return jax.random.normal(next(keys), shape, f32) * scale

    def gain(shape):
        return 1.0 + nrm(shape, 0.05)

    ne, no = (DEPTH + 1) // 2, DEPTH // 2
    d = D_MODEL
    n_idx = jnp.arange(B_STATE, dtype=f32)
    log_dt = math.log(DT_MIN) + jax.random.uniform(next(keys), (ne, B_GROUPS), f32) * (
        math.log(DT_MAX) - math.log(DT_MIN))
    return {
        'x': nrm((BATCH, SEQ, d), 1.0),
        'c': nrm((BATCH, d), 1.0),
        'w_ada': nrm((DEPTH, d, 6 * d), 0.5 * d ** -0.5),
        'b_ada': nrm((DEPTH, 6 * d), 0.02),
        'g_mix': gain((DEPTH, d)),
        'g_ffn': gain((DEPTH, d)),
        'g_final': gain((d,)),
        'e_w_in': nrm((ne, d, 3 * A_WIDTH + B_WIDTH), d ** -0.5),
        'e_w_out': nrm((ne, A_WIDTH + B_WIDTH, d), (A_WIDTH + B_WIDTH) ** -0.5),
        's5_a_re': -0.5 * jnp.exp(nrm((ne, B_GROUPS, B_STATE), 0.05)),
        's5_a_im': math.pi * n_idx + nrm((ne, B_GROUPS, B_STATE), 0.01),
        's5_log_dt': log_dt,
        's5_b_re': nrm((ne, B_GROUPS, B_STATE, B_GROUP), (2 * B_GROUP) ** -0.5),
        's5_b_im': nrm((ne, B_GROUPS, B_STATE, B_GROUP), (2 * B_GROUP) ** -0.5),
        's5_c_re': nrm((ne, B_GROUPS, B_GROUP, B_STATE), (2 * B_STATE) ** -0.5),
        's5_c_im': nrm((ne, B_GROUPS, B_GROUP, B_STATE), (2 * B_STATE) ** -0.5),
        's5_d': nrm((ne, B_GROUPS, B_GROUP), 1.0),
        's5_w_glu': nrm((ne, B_WIDTH, B_WIDTH), B_WIDTH ** -0.5),
        's5_b_glu': nrm((ne, B_WIDTH), 0.02),
        'ff_w_gate': nrm((ne, d, FF_DENSE), d ** -0.5),
        'ff_w_up': nrm((ne, d, FF_DENSE), d ** -0.5),
        'ff_w_down': nrm((ne, FF_DENSE, d), FF_DENSE ** -0.5),
        'o_w_in': nrm((no, d, C_IN), d ** -0.5),
        'o_w_out': nrm((no, C_HEADS * C_VDIM, d), (C_HEADS * C_VDIM) ** -0.5),
        'mla_g_kv': gain((no, C_LATENT)),
        'mla_w_uk': nrm((no, C_LATENT, C_HEADS, C_NOPE), C_LATENT ** -0.5),
        'mla_w_uv': nrm((no, C_LATENT, C_HEADS, C_VDIM), C_LATENT ** -0.5),
        'moe_w_router': nrm((no, d, N_EXPERTS), d ** -0.5),
        'moe_b_router': nrm((no, N_EXPERTS), 0.01),
        'moe_w_gate': nrm((no, N_EXPERTS, d, FF_EXPERT), d ** -0.5),
        'moe_w_up': nrm((no, N_EXPERTS, d, FF_EXPERT), d ** -0.5),
        'moe_w_down': nrm((no, N_EXPERTS, FF_EXPERT, d), FF_EXPERT ** -0.5),
    }

def reference(x, c, w_ada, b_ada, g_mix, g_ffn, g_final,
              e_w_in, e_w_out, s5_a_re, s5_a_im, s5_log_dt, s5_b_re, s5_b_im,
              s5_c_re, s5_c_im, s5_d, s5_w_glu, s5_b_glu,
              ff_w_gate, ff_w_up, ff_w_down,
              o_w_in, o_w_out, mla_g_kv, mla_w_uk, mla_w_uv,
              moe_w_router, moe_b_router, moe_w_gate, moe_w_up, moe_w_down):
    s = x.shape[1]
    cos, sin = rope_tables(s)
    c_act = jax.nn.silu(c.astype(jnp.float32))
    h = x
    for layer in range(DEPTH):
        mod = (c_act @ w_ada[layer].astype(jnp.float32)
               + b_ada[layer].astype(jnp.float32)).astype(x.dtype)
        sh_m, sc_m, gt_m, sh_f, sc_f, gt_f = jnp.split(mod, 6, axis=-1)
        i = layer // 2
        u = modulate(rms_norm(h, g_mix[layer]), sh_m, sc_m)
        if layer % 2 == 0:
            y = even_mixer(u, cos, sin, e_w_in[i], e_w_out[i], s5_a_re[i], s5_a_im[i],
                           s5_log_dt[i], s5_b_re[i], s5_b_im[i], s5_c_re[i], s5_c_im[i],
                           s5_d[i], s5_w_glu[i], s5_b_glu[i])
        else:
            y = dsa_mixer(u, cos, sin, o_w_in[i], o_w_out[i], mla_g_kv[i], mla_w_uk[i], mla_w_uv[i])
        h = h + gt_m[:, None, :] * y
        u = modulate(rms_norm(h, g_ffn[layer]), sh_f, sc_f)
        if layer % 2 == 0:
            y = swiglu(u, ff_w_gate[i], ff_w_up[i], ff_w_down[i])
        else:
            y = moe_swiglu(u, moe_w_router[i], moe_b_router[i], moe_w_gate[i], moe_w_up[i], moe_w_down[i])
        h = h + gt_f[:, None, :] * y
    return rms_norm(h, g_final)


_drawn_inputs = setup_inputs


def setup_inputs(seed=0):
    import zlib

    import numpy as np

    out = dict(_drawn_inputs(seed))
    spreads = {}
    factors = {'g_mix': 2.952,
     's5_a_re': 64.0,
     's5_a_im': 49.352,
     's5_log_dt': 52.592,
     's5_b_re': 64.0,
     's5_b_im': 47.48,
     's5_c_re': 59.352,
     's5_c_im': 64.0,
     's5_b_glu': 8.0,
     'mla_g_kv': 5.465,
     'moe_b_router': 38.776}
    for name, (base, spread) in spreads.items():
        noise = np.random.default_rng([zlib.crc32(name.encode()), seed]).standard_normal(out[name].shape)
        drawn = base * np.exp(spread * noise) if base else spread * noise
        out[name] = jnp.asarray(drawn.astype(out[name].dtype))
    for name, factor in factors.items():
        out[name] = (out[name] * factor).astype(out[name].dtype)
    return out
```

```python
import numpy as np
from contextlib import ExitStack

import concourse.bass as bass
from concourse import mybir

F32 = mybir.dt.float32
U32 = mybir.dt.uint32
I32 = mybir.dt.int32
ALU = mybir.AluOpType
ACT = mybir.ActivationFunctionType
AX = mybir.AxisListType

P = 128
D = 1024
S = 256
NT = S // P
KD = D // P
EPS = 1e-6
HD = 64
ROPE = HD // 4
HALF = ROPE // 2
SC = HD ** -0.5
A_HEADS = 8
A_W = A_HEADS * HD
G_S5, P_S5, C_S5 = 32, 64, 16
NCH = G_S5 * P_S5 // P
C_HEADS = 16
NOPE = HD - ROPE
LAT = D // 4
IH = 8
TOPK = min(256, S // 4)
FF = 2816
FB = 8
FW = FF // FB
FT = [(0, P), (P, P), (2 * P, FW - 2 * P)]
E = 8
FE = 3584
MB = FE // 512
SLOT = 4096
NS0, NS1 = 5, 7
ADA0, ADA1 = 512, 384
NA0, NA1 = 6 * D // ADA0, 6 * D // ADA1
KEYS = [P, 2 * P]
KOFF = [0, P]
KW = sum(KEYS)
BIG = 1e30
NEG = -3e38
ROUND = 12582912.0
PI = 3.1415925
OVER = P
TWO_PI = (6.28125, 0.0019353071693331, 1.0253131677018246e-11)

C_ID, C_ONE, C_TRI = 0, P, 2 * P
C_IOTA = 3 * P
C_CNT = C_IOTA + S
C_NEG = C_CNT + KW
C_CAU = C_NEG + KW
C_CB = C_CAU + KW
C_COS = C_CB + KW
C_SIN = C_COS + NT * HALF
C_HM = C_SIN + NT * HALF
C_TOK = C_HM + 2
NC = C_TOK + 2


def constants():
    c = np.zeros((P, NC), np.float32)
    p = np.arange(P)
    c[:, C_ID:C_ID + P] = np.eye(P)
    c[:, C_ONE:C_ONE + P] = 1
    c[:, C_TRI:C_TRI + P] = p[:, None] < p[None, :]
    c[:, C_IOTA:C_IOTA + S] = np.arange(S)
    for t in range(NT):
        d = (t * P + p)[:, None] - np.arange(KEYS[t])[None, :]
        n = (d >= 0) * ((d <= 128) * 1 + (d % 4 == 0) * 1 + (d % 16 == 0) * 1)
        a, b = KOFF[t], KOFF[t] + KEYS[t]
        c[:, C_CNT + a:C_CNT + b] = n
        c[:, C_NEG + a:C_NEG + b] = np.where(n == 0, -BIG, 0)
        c[:, C_CAU + a:C_CAU + b] = d >= 0
        c[:, C_CB + a:C_CB + b] = np.where(d >= 0, 0, NEG)
        inv = np.float32(500000.0) ** (-np.arange(0, ROPE, 2, dtype=np.float32) / np.float32(ROPE))
        ang = (t * P + p).astype(np.float32)[:, None] * inv.astype(np.float32)[None, :]
        c[:, C_COS + t * HALF:C_COS + (t + 1) * HALF] = np.cos(ang.astype(np.float64))
        c[:, C_SIN + t * HALF:C_SIN + (t + 1) * HALF] = np.sin(ang.astype(np.float64))
        c[:, C_TOK + t] = t * P + p
        c[:, C_HM + t] = (p // C_S5) % 2 == t
    return c


class Steps:

    def __init__(self, eng, sem):
        self.eng, self.sem, self.n = eng, sem, 0

        self.reg, self.per, self.at = None, 0, 0

    def __call__(self, ins):
        ins.then_inc(self.sem, 1)
        self.n += 1
        return ins

    def wait(self):
        if self.reg is None:
            self.eng.wait_ge(self.sem, self.n)
        else:
            self.eng.wait_ge(self.sem, self.reg * self.per + self.n)

    def enter(self, reg, first, per):
        self.reg, self.per, self.at = reg, per, self.n
        self.n -= first * per

    def leave(self, first, turns):
        assert self.n + first * self.per == self.at + self.per, (self.n, self.at, self.per)
        self.n = self.at + turns * self.per
        self.reg = None


def trunk(nc, A, out):
    ctx = ExitStack()
    with ctx:
        def sb(name, shape, dt=F32):
            return ctx.enter_context(nc.sbuf_tensor(name, shape, dt))

        def sem(name):
            return ctx.enter_context(nc.semaphore(name))

        cst = sb("cst", [P, NC])
        h = sb("h", [P, NT, D])
        uT = sb("uT", [P, KD, S])
        ada = sb("ada", [P, 6 * D])
        gate_row = sb("gate_row", [P, 2, D])
        ring = sb("ring", [P, NS0, SLOT])
        wide = sb("wide", [P, NS1 - NS0, SLOT])
        work = sb("work", [P, 9700])
        c_col = sb("c_col", [P, KD])
        g_col = sb("g_col", [P, 4, KD])
        mod_a = sb("mod_a", [P, 2, KD])
        mod_b = sb("mod_b", [P, 2, KD])
        stat = sb("stat", [P, 24])
        eps = sb("eps", [P, 1])

        ps = [ctx.enter_context(nc.psum_tensor(f"ps{i}", [P, 512], F32)) for i in range(8)]

        ident = cst[:, C_ID:C_ID + P]
        ones = cst[:, C_ONE:C_ONE + P]
        tri = cst[:, C_TRI:C_TRI + P]

        def iota(n):
            return cst[:, C_IOTA:C_IOTA + n]

        def cos(t, heads):
            return cst[:, C_COS + t * HALF:C_COS + (t + 1) * HALF].unsqueeze(1).broadcast_to([P, heads, HALF])

        def sin(t, heads):
            return cst[:, C_SIN + t * HALF:C_SIN + (t + 1) * HALF].unsqueeze(1).broadcast_to([P, heads, HALF])

        class Region:

            def __init__(self, buf, size, at=0):
                self.buf, self.size, self.at = buf, size, at

            def take(self, *shape):
                n = int(np.prod(shape))
                a = self.buf[:, self.at:self.at + n]
                self.at += n
                assert self.at <= self.size, self.at
                if len(shape) == 1:
                    return a
                names = "abcd"[:len(shape)]
                return a.rearrange(f"p ({' '.join(names)}) -> p {' '.join(names)}",
                                   **{x: s for x, s in zip(names, shape)})

        flat_uT = uT[:, :, :].rearrange("p a b -> p (a b)")
        rope_buf = work[:, 9444:9700].rearrange("p (a h d) -> p a h d", a=2, h=C_HEADS)
        W0 = Region(work, 9444)
        hn = W0.take(NT, D)
        qk_tok = hn
        s5_y = W0.take(4, S)
        s5_p = W0.take(24, NCH)
        s5_bT = W0.take(2, 4, P)
        s5_cT = W0.take(3, 4, P)
        s5_tmp = W0.take(NCH, P)
        s5_v = W0.take(2, S)
        s5_small = W0.take(10)
        s5_rb = W0.take(192)
        WA = Region(ada, 6 * D)
        qT = WA.take(4, S)
        kT = WA.take(4, S)
        v_tok = WA.take(NT, A_W)
        s_inT = WA.take(4, S)
        catT = WA.take(KD, S)
        tmp_flat = s5_tmp.rearrange("p a b -> p (a b)")
        rotA = tmp_flat[:, 0:512].rearrange("p (a b) -> p a b", a=2)
        rotB = tmp_flat[:, 512:1024].rearrange("p (a b) -> p a b", a=2)
        zbuf = tmp_flat[:, 1024:2048].rearrange("p (n a b) -> p n a b", n=2, a=2)
        post = hn.rearrange("p t (n a b) -> p t n a b", n=2, a=2)
        WU = Region(flat_uT, KD * S)
        sm = WU.take(2, KW)
        pT = WU.take(2, KW)
        phase = wide[:, :, :].rearrange("p a (b c) -> p a b c", b=NCH)

        b_in = flat_uT[:, 0:512].rearrange("p (a b c) -> p a b c", a=2, b=NCH)
        c_in = flat_uT[:, 512:1024].rearrange("p (a b c) -> p a b c", a=2, b=4)
        b_pad = flat_uT[:, 1024:2048].rearrange("p (a b c) -> p a b c", a=2, b=4)
        c_pad = hn.rearrange("p t (b c) -> p t b c", b=8)
        s5_d = sb("s5_d", [P, 4])
        s5_bg = sb("s5_bg", [P, 4])

        (LR, LI, LDT, DT, X1, ANG, MAG, KK, TT, RR, RH, SN, SH, CS, AR, AI, NR, DEN, RDEN, FR, FI,
         ER, EI, T2) = range(24)

        consts_in = sem("consts_in")
        x_in = sem("x_in")
        vec_in = sem("vec_in")
        s5_in = sem("s5_in")
        bias_in = sem("bias_in")
        late_in = sem("late_in")
        fill = [sem(f"slot{i}_filled") for i in range(NS1)]
        weights_used = sem("weights_used")
        ada_used = sem("ada_used")
        dve_steps, act_steps, pool_steps = sem("dve_steps"), sem("act_steps"), sem("pool_steps")
        c_ready = sem("c_ready")
        ada_zeroed = sem("ada_zeroed")
        mod_summed = sem("mod_summed")
        mod_ready = sem("mod_ready")
        gate_ready = sem("gate_ready")
        h_ready = sem("h_ready")
        rms_ready = sem("rms_ready")
        hn_ready = sem("hn_ready")
        hnT_done = sem("hnT_done")
        uT_ready = sem("uT_ready")
        mix_out_done = sem("mix_out_done")
        out_stored = sem("out_stored")

        tables_ready = sem("tables_ready")
        y_final = sem("y_final")
        ckv_ready = sem("ckv_ready")
        ckvT_done = sem("ckvT_done")
        ckvT_ready = sem("ckvT_ready")
        kv_done = sem("kv_done")
        kn_ready = sem("kn_ready")
        v_ready = sem("v_ready")
        idxT_done = sem("idxT_done")
        idxT_ready = sem("idxT_ready")
        logit_done = sem("logit_done")
        relu_ready = sem("relu_ready")
        score_added = sem("score_added")
        mask_ready = sem("mask_ready")
        router_done = sem("router_done")
        gap_ready = sem("gap_ready")
        gap_exp = sem("gap_exp")
        member_ready = sem("member_ready")
        pos_done = sem("pos_done")
        sel_ready = sem("sel_ready")
        gather_done = sem("gather_done")
        info_done = sem("info_done")
        ueT_ready = sem("ueT_ready")
        selT_ready = sem("selT_ready")
        y_done = sem("y_done")
        y_sb_ready = sem("y_sb_ready")
        scatter_done = sem("scatter_done")
        scatter_added = sem("scatter_added")
        y_zeroed = sem("y_zeroed")
        eps_ready = sem("eps_ready")
        final_steps = sem("final_steps")
        stat_ready = sem("stat_ready")

        W1 = Region(work, 9444)
        q_tok = W1.take(NT, C_HEADS, HD)
        ctxT = q_tok.rearrange("p t h d -> p (t h d)").rearrange("p (k s) -> p k s", k=KD)
        kcat = W1.take(NT, C_HEADS, HD)
        ckr = W1.take(NT, LAT + ROPE)
        q_i = W1.take(NT, IH, HD)
        k_iw = W1.take(NT, 2 * HD + IH)
        ckvT = W1.take(2, S)
        qiT = W1.take(4, S)
        kiT = W1.take(S)
        score = W1.take(KW)
        selneg = W1.take(KW)
        kr_t = W1.take(ROPE)
        top8 = W1.take(NT, 8)
        WA1 = Region(ada, 6 * D)
        qT1 = WA1.take(8, S)
        kT1 = WA1.take(8, S)
        v1 = WA1.take(NT, D)
        W2 = Region(work, 9700, NT * D)
        y_acc = W2.take(NT, D)
        ueT = W2.take(KD, P)
        y_sb = W2.take(D)
        mid = W2.take(512)
        silu = W2.take(512)
        midT = W2.take(4, P)
        sel = W2.take(NT, P)
        selT = W2.take(S)
        info = W2.take(NT, 2)
        slot_info = W2.take(2)
        cur = W2.take(NT, 2)
        final_y = hn
        w_r = sb("w_r", [P, KD, E])
        b_r = sb("b_r", [P, E])
        g_kv = sb("g_kv", [P, 2])
        lg = W2.take(NT, E)
        top = W2.take(NT, E)
        top_i = sb("top_i", [P, NT, E], U32)
        rt = W2.take(NT, 48)
        possel = W2.take(NT, E + 1)
        comb = W2.take(NT, E + 1)
        jobs = W2.take(3 * E)
        job_tab = sb("job_tab", [P, 3 * E], I32)

        w_ada, b_ada = A["w_ada"], A["b_ada"]
        kp = lambda ap: ap.rearrange("(k p) n -> p k n", p=P)
        stream = []
        fills = [0] * NS1
        users = {"weights": 0, "ada": 0}
        last = [None] * NS1

        def slot_ap(s):
            return ring[:, s, :] if s < NS0 else wide[:, s - NS0, :]

        def push(slot, pieces, user):
            before = last[slot]
            fills[slot] += 16 * len(pieces)
            users[user] += 1
            last[slot] = (user, users[user])
            stream.append((slot, pieces, before))
            return slot, fills[slot]

        def block_ap(slot, k, n):
            return slot_ap(slot)[:, 0:k * n].rearrange("p (k n) -> p k n", k=k)

        n_item = [0]

        def item(srcs, k, n, user):
            s = n_item[0] % NS0
            n_item[0] += 1
            got = push(s, [(block_ap(s, k, n), kp(srcs))], user)
            return (block_ap(s, k, n), got)

        ada0 = [item(w_ada[0, :, i * ADA0:(i + 1) * ADA0], KD, ADA0, "ada") for i in range(NA0)]
        e_in = [item(A["e_w_in"][0, :, i * 512:(i + 1) * 512], KD, 512, "weights") for i in range(4)]
        glu_w = item(A["s5_w_glu"][0], 4, 512, "weights")
        e_out = [item(A["e_w_out"][0, :, i * 512:(i + 1) * 512], KD, 512, "weights") for i in range(2)]
        static_before = list(stream)
        ff_slot = [(n_item[0] + j) % NS0 for j in range(5)]
        ff_fill0 = [fills[s] for s in ff_slot]
        ff_inc = [16, 16, 32, 16, 16]
        ff_last0 = [last[s] for s in ff_slot]
        ff_w0, ff_a0 = users["weights"], users["ada"]
        for j, s in enumerate(ff_slot):
            fills[s] += ff_inc[j] * FB
        users["weights"] += 3 * FB
        users["ada"] += 2 * FB
        for j, s in enumerate(ff_slot):
            last[s] = ("weights", users["weights"] - 2 + j) if j < 3 else ("ada", users["ada"] - 4 + j)
        n_item[0] += 5 * FB
        stream.clear()
        o_cols = [(0, 256), (256, 384), (640, 384), (1024, 272), (1296, 512), (1808, 72)]
        o_in = [item(A["o_w_in"][0, :, a:a + n], KD, n, "weights") for a, n in o_cols]
        s = n_item[0] % NS0
        n_item[0] += 1
        uk_ap = slot_ap(s)[:, 0:2 * 768].rearrange("p (k n) -> p k n", k=2)
        uv_ap = slot_ap(s)[:, 2 * 768:2 * 1792].rearrange("p (k n) -> p k n", k=2)
        ukv = push(s, [(uk_ap, A["mla_w_uk"][0].rearrange("(k p) a b -> p k (a b)", p=P)),
                       (uv_ap, A["mla_w_uv"][0].rearrange("(k p) a b -> p k (a b)", p=P))], "weights")
        o_out = [item(A["o_w_out"][0, :, i * 512:(i + 1) * 512], KD, 512, "weights") for i in range(2)]
        static_after = list(stream)
        moe_last0 = list(last)
        moe_w0 = users["weights"]
        moe_fill0 = list(fills)
        moe_items = [("gate", 0), ("up", 0)]
        for b in range(1, MB):
            moe_items += [("gate", b), ("up", b), ("down", b - 1)]
        moe_items += [("down", MB - 1)]
        NI = len(moe_items)
        assert NI % NS1 == 0
        PER = NI // NS1
        moe_at = {it: i for i, it in enumerate(moe_items)}

        used = {"weights": weights_used, "ada": ada_used}

        block = ctx.enter_context(nc.Block())
        x_tok = A["x"].rearrange("o (t p) d -> p (o t) d", p=P)
        out_tok = out.rearrange("o (t p) d -> p (o t) d", p=P)

        s5_dt = sem("s5_dt")
        s5_x = sem("s5_x")
        s5_mag = sem("s5_mag")
        s5_r = sem("s5_r")
        s5_sin = sem("s5_sin")
        s5_den = sem("s5_den")
        s5_rden = sem("s5_rden")
        s5_pads = sem("s5_pads")
        s5_padT = sem("s5_padT")
        s5_wT_ready = sem("s5_wT_ready")
        phase_ready = sem("phase_ready")
        bu_done = sem("bu_done")
        bu_used = sem("bu_used")
        z_ready = sem("z_ready")
        post_ready = sem("post_ready")
        y_part_done = sem("y_part_done")
        y_pre = sem("y_pre")
        y_ready = sem("y_ready")
        glu_done = sem("glu_done")
        glu_tanh = sem("glu_tanh")
        proj_done = sem("proj_done")
        rope_done = sem("rope_done")
        nope_done = sem("nope_done")
        vs_ready = sem("vs_ready")
        qkT_done = sem("qkT_done")
        qkT_ready = sem("qkT_ready")
        score_done = sem("score_done")
        max_ready = sem("max_ready")
        exp_ready = sem("exp_ready")
        p_ready = sem("p_ready")
        pT_done = sem("pT_done")
        pT_ready = sem("pT_ready")
        o_done = sem("o_done")
        cat_ready = sem("cat_ready")
        gate_done = sem("gate_done")
        silu_done = sem("silu_done")
        up_done = sem("up_done")
        mid_ready = sem("mid_ready")
        midT_done = sem("midT_done")
        midT_ready = sem("midT_ready")
        down_done = sem("down_done")

        @block.sync
        def _(sp):
            def load(entry):
                slot, pieces, before = entry
                if before is not None:
                    sp.wait_ge(used[before[0]], before[1])
                for dst, src in pieces:
                    sp.dma_start(dst, src).then_inc(fill[slot], 16)

            with nc.allow_non_contiguous_dma(reason="one small vector"):
                sp.dma_start(c_col[:, :], A["c"][0].rearrange("(k p) -> p k", p=P)).then_inc(vec_in, 16)
            for e in static_before[:2]:
                load(e)
            sp.dma_start(cst[:, :], A["consts"]).then_inc(consts_in, 16)
            for e in static_before[2:4]:
                load(e)
            sp.dma_start(h[:, :, :], x_tok).then_inc(x_in, 16)
            for e in static_before[4:]:
                load(e)

            def ff_load(j, b):
                s = ff_slot[j]
                if j == 0:
                    sp.dma_start(block_ap(s, KD, FW), kp(A["ff_w_gate"][0])[:, :, bass.ds(b * FW, FW)]).then_inc(fill[s], 16)
                elif j == 1:
                    sp.dma_start(block_ap(s, KD, FW), kp(A["ff_w_up"][0])[:, :, bass.ds(b * FW, FW)]).then_inc(fill[s], 16)
                elif j == 2:
                    dst = block_ap(s, 3, D)
                    rows = A["ff_w_down"][0, bass.ds(b * FW, FW), :]
                    sp.dma_start(dst[:, 0:2, :], rows[0:2 * P, :].rearrange("(k p) n -> p k n", p=P)).then_inc(fill[s], 16)
                    sp.dma_start(dst[0:FW - 2 * P, 2, :], rows[2 * P:FW, :]).then_inc(fill[s], 16)
                else:
                    sp.dma_start(block_ap(s, KD, ADA1),
                                 kp(w_ada[1])[:, :, bass.ds((b * 2 + j - 3) * ADA1, ADA1)]).then_inc(fill[s], 16)

            for j in range(5):
                sp.wait_ge(used[ff_last0[j][0]], ff_last0[j][1])
                ff_load(j, 0)
            with sp.Fori(1, FB) as b:
                for j in range(3):
                    sp.wait_ge(weights_used, b * 3 + (ff_w0 - 2 + j))
                    ff_load(j, b)
                for j in (3, 4):
                    sp.wait_ge(ada_used, b * 2 + (ff_a0 - 1 + j - 3))
                    ff_load(j, b)
            for e in static_after:
                load(e)

            def moe_load(m, e):
                kind, b = moe_items[m]
                s = m % NS1
                if kind == "down":
                    src = A["moe_w_down"][0, bass.ds(e, 1), b * 512:(b + 1) * 512, :]
                    sp.dma_start(block_ap(s, 4, D), src.rearrange("e (k p) n -> p (e k) n", p=P)).then_inc(fill[s], 16)
                else:
                    src = A["moe_w_" + kind][0, bass.ds(e, 1), :, b * 512:(b + 1) * 512]
                    sp.dma_start(block_ap(s, KD, 512), src.rearrange("e (k p) n -> p (e k) n", p=P)).then_inc(fill[s], 16)

            for m in range(NS0):
                sp.wait_ge(used[moe_last0[m][0]], moe_last0[m][1])
                moe_load(m, 0)
            for m in range(NS0, NS1):
                moe_load(m, 0)
            with sp.Fori(0, E - 1) as e:
                for m in range(NS1, NI):
                    sp.wait_ge(weights_used, e * NI + (moe_w0 + m - NS1 + 1))
                    moe_load(m, e)
                for m in range(NS1):
                    sp.wait_ge(weights_used, e * NI + (moe_w0 + NI + m - NS1 + 1))
                    moe_load(m, e + 1)
            for m in range(NS1, NI):
                sp.wait_ge(weights_used, (E - 1) * NI + moe_w0 + m - NS1 + 1)
                moe_load(m, E - 1)
            sp.wait_ge(tables_ready, 1)
            with sp.If(sp.value_load(job_tab[0:1, 2 * E:2 * E + 1], min_val=0, max_val=E) > 0):
                with sp.Fori(0, E) as e:
                    n_e = sp.value_load(job_tab[0:1, bass.ds(e, 1)], min_val=0, max_val=S)
                    with sp.If(n_e > OVER):
                        job = sp.value_load(job_tab[0:1, bass.ds(e + E, 1)], min_val=E, max_val=2 * E)
                        for m in range(NI):
                            sp.wait_ge(weights_used, job * NI + (moe_w0 + m - NS1 + 1))
                            moe_load(m, e)
            sp.wait_ge(y_final, 2)
            sp.dma_start(out_tok, final_y).then_inc(out_stored, 16)
            sp.wait_ge(out_stored, 16)

        @block.gpsimd
        def _(pool):
            step = Steps(pool, pool_steps)
            par = lambda i: s5_p[:, i, :]

            def mul(o, a, b):
                step.wait()
                return step(nc.gpsimd.tensor_tensor(o, a, b, ALU.mult))

            def add(o, a, b):
                step.wait()
                return step(nc.gpsimd.tensor_tensor(o, a, b, ALU.add))

            def sub(o, a, b):
                step.wait()
                return step(nc.gpsimd.tensor_tensor(o, a, b, ALU.subtract))

            def affine(o, a, m, b):
                step.wait()
                return step(nc.gpsimd.tensor_scalar(o, a, m, b, ALU.mult, ALU.add))

            st = lambda a: a.rearrange("o (j g) p -> (g p) (o j)", g=2)
            with nc.allow_non_contiguous_dma(reason="small parameters"):
                pool.dma_start(par(LR), st(A["s5_a_re"])).then_inc(s5_in, 16)
                pool.dma_start(par(LI), st(A["s5_a_im"])).then_inc(s5_in, 16)
                for g in range(2):
                    pool.dma_start(s5_p[g * P_S5:(g + 1) * P_S5, LDT, :],
                                   A["s5_log_dt"].rearrange("o (j g) -> g (o j)", g=2)[g:g + 1, :]
                                   .broadcast_to([P_S5, NCH])).then_inc(s5_in, 16)
                pool.dma_start(s5_d[:, :], A["s5_d"].rearrange("o (t g) c -> (g c) (o t)", t=4)).then_inc(s5_in, 16)
                pool.dma_start(s5_bg[:, :], A["s5_b_glu"].rearrange("o (t p) -> p (o t)", p=P)).then_inc(s5_in, 16)
                for i, n in enumerate(("re", "im")):
                    pool.dma_start(b_in[:, i, :, :], A["s5_b_" + n].rearrange("o (j g) p c -> (g p) (o j) c", g=2)).then_inc(s5_in, 16)
                    pool.dma_start(c_in[:, i, :, :], A["s5_c_" + n].rearrange("o (t g) c p -> (g c) (o t) p", t=4)).then_inc(s5_in, 16)
                step(pool.memset(ada[:, :], 0.0))
                step.wait()
                pool.dma_start(ada[0:1, :], A["b_ada"][0:1, :]).then_inc(bias_in, 16)
                for i, (n, l) in enumerate((("g_mix", 0), ("g_mix", 1), ("g_ffn", 0), ("g_ffn", 1))):
                    pool.dma_start(g_col[:, i, :], A[n][l:l + 1, :].rearrange("o (k p) -> p (o k)", p=P)).then_inc(late_in, 16)
                pool.dma_start(g_kv[:, :], A["mla_g_kv"].rearrange("o (k p) -> p (o k)", p=P)).then_inc(late_in, 16)
                pool.dma_start(w_r[:, :, :], A["moe_w_router"][0].rearrange("(k p) e -> p k e", p=P)).then_inc(late_in, 16)
                pool.dma_start(b_r[:, :], A["moe_b_router"].broadcast_to([P, E])).then_inc(late_in, 16)
            pool.wait_ge(s5_in, 16 * 10)
            pool.wait_ge(s5_dt, 1)
            step(nc.gpsimd.tensor_tensor(par(X1), par(LR), par(DT), ALU.mult))
            step.wait()
            nc.gpsimd.tensor_tensor(par(ANG), par(LI), par(DT), ALU.mult).then_inc(s5_x, 1)
            pool.wait_ge(s5_x, 1)
            affine(par(KK), par(ANG), 1 / (2 * np.pi), ROUND)
            affine(par(KK), par(KK), 1.0, -ROUND)
            sub(par(RR), par(ANG), par(ANG))
            add(par(RR), par(RR), par(ANG))
            for c in TWO_PI:
                affine(par(TT), par(KK), c, 0.0)
                sub(par(RR), par(RR), par(TT))
            step.wait()
            step(nc.gpsimd.tensor_scalar(par(RR), par(RR), PI, -PI, ALU.min, ALU.max))
            step.wait()
            nc.gpsimd.tensor_scalar(par(RH), par(RR), 0.5, 0.0, ALU.mult, ALU.add).then_inc(s5_r, 1)
            mul(par(DEN), par(LR), par(LR))
            mul(par(T2), par(LI), par(LI))
            step.wait()
            nc.gpsimd.tensor_tensor(par(DEN), par(DEN), par(T2), ALU.add).then_inc(s5_den, 1)
            pool.wait_ge(s5_sin, 1)
            pool.wait_ge(s5_r, 1)
            pool.wait_ge(s5_den, 1)
            mul(par(TT), par(SH), par(SH))
            affine(par(CS), par(TT), -2.0, 1.0)
            pool.wait_ge(s5_mag, 1)
            mul(par(AR), par(MAG), par(CS))
            mul(par(AI), par(MAG), par(SN))
            affine(par(NR), par(AR), 1.0, -1.0)
            pool.wait_ge(s5_rden, 1)
            for o, a, b, c, d, last_op in ((FR, NR, LR, AI, LI, add), (FI, AI, LR, NR, LI, sub)):
                mul(par(TT), par(a), par(b))
                mul(par(T2), par(c), par(d))
                last_op(par(o), par(TT), par(T2))
                mul(par(o), par(o), par(RDEN))
            step.wait()
            step(pool.memset(b_pad, 0.0))
            for g in range(2):
                rows = slice(g * P_S5, (g + 1) * P_S5)
                f = lambda i: s5_p[rows, i, :].unsqueeze(2).broadcast_to([P_S5, NCH, C_S5])
                b = lambda i: b_in[rows, i, :, :]
                o = lambda i: b_pad[rows, i, :, :].rearrange("p t (j x) -> p (t j) x", x=2 * C_S5)[:, :, g * C_S5:(g + 1) * C_S5]
                t = phase[rows, 0, :, 0:C_S5]
                for i, (x, y, op) in enumerate(((0, 1, sub), (1, 0, add))):
                    mul(t, f(FI), b(y))
                    mul(o(i), f(FR), b(x))
                    op(o(i), o(i), t)
            for i in range(2):
                for t in range(4):
                    for g in range(2):
                        step.wait()
                        step(nc.gpsimd.tensor_scalar(c_pad[:, i, t, g * P_S5:(g + 1) * P_S5], c_in[:, i, t, :],
                                                     cst[:, C_HM + g:C_HM + g + 1], 0.0, ALU.mult, ALU.add))
            step.wait()
            nc.gpsimd.tensor_scalar(s5_bg[:, :], s5_bg[:, :], 0.5, 0.0, ALU.mult, ALU.add).then_inc(s5_pads, 1)
            pool.wait_ge(s5_pads, 1)
            step(pool.memset(phase[:, 0, :, 0:1], 1.0))
            step(pool.memset(phase[:, 1, :, 0:1], 0.0))
            affine(par(ER), par(CS), 1.0, 0.0)
            affine(par(EI), par(SN), 1.0, 0.0)
            m = 1
            while m < S:
                er = par(ER).unsqueeze(2).broadcast_to([P, NCH, m])
                ei = par(EI).unsqueeze(2).broadcast_to([P, NCH, m])
                c0, s0 = phase[:, 0, :, 0:m], phase[:, 1, :, 0:m]
                c1, s1 = phase[:, 0, :, m:2 * m], phase[:, 1, :, m:2 * m]
                t = s5_tmp[:, :, 0:m]
                mul(t, s0, ei)
                mul(c1, c0, er)
                sub(c1, c1, t)
                mul(t, c0, ei)
                mul(s1, s0, er)
                add(s1, s1, t)
                mul(par(TT), par(EI), par(EI))
                mul(par(T2), par(ER), par(EI))
                mul(par(ER), par(ER), par(ER))
                sub(par(ER), par(ER), par(TT))
                affine(par(EI), par(T2), 2.0, 0.0)
                m *= 2
            step.wait()
            pool.memset(s5_small[:, 0:1], 0.0).then_inc(phase_ready, 1)
            for j in range(NCH):
                pool.wait_ge(z_ready, j + 1)
                if j >= 2:
                    pool.wait_ge(y_part_done, j - 1)
                z = zbuf[:, j % 2]
                o = post[:, j % 2]
                if j == 0:
                    pool.wait_ge(phase_ready, 1)
                    pool.wait_ge(qkT_done, 4)
                for i in range(2):
                    w = nc.gpsimd.tensor_tensor(o[:, i], z, phase[:, i, j, :].unsqueeze(1).broadcast_to([P, 2, S]), ALU.mult)
                w.then_inc(post_ready, 1)
            pool.wait_ge(h_ready, 4)
            pool.memset(ada[:, :], 0.0).then_inc(ada_zeroed, 1)
            pool.wait_ge(ada_zeroed, 1)
            pool.dma_start(ada[0:1, :], A["b_ada"][1:2, :]).then_inc(bias_in, 16)
            pool.wait_ge(h_ready, 12)
            pool.memset(y_acc, 0.0).then_inc(y_zeroed, 1)
            pool.dma_start(gate_row[:, 0, :], A["g_final"].unsqueeze(0).broadcast_to([P, D])).then_inc(late_in, 16)

        @block.tensor
        def _(pe):
            mm = nc.tensor.matmul

            def tr(o, i):
                n = i.shape[0]
                return nc.tensor.transpose(o, i, ident[0:n, 0:n])

            pe.wait_ge(consts_in, 16)
            pe.wait_ge(s5_pads, 1)
            for i in range(2):
                for t in range(4):
                    w = tr(ps[i][:, t * P:(t + 1) * P], b_pad[:, i, t, :])
                w.then_inc(s5_padT, 1)
            for i in range(2):
                for t in range(4):
                    w = tr(ps[2 + i][:, t * P:(t + 1) * P], c_pad[:, i, t, :])
                w.then_inc(s5_padT, 1)

            def mod(layer):
                pe.wait_ge(ada_used, (NA0, NA0 + NA1)[layer])
                if layer:
                    pe.wait_ge(h_ready, 8)
                for i, sec in enumerate((0, 1, 3, 4)):
                    for k in range(KD):
                        w = mm(ps[4][:, i * KD + k:i * KD + k + 1], ada[:, sec * D + k * P:sec * D + (k + 1) * P],
                               ones[:, 0:1], start=True, stop=True)
                w.then_inc(mod_summed, 1)
                for i, (sec, half, bank) in enumerate(((2, 0, 5), (2, 1, 6), (5, 0, 7), (5, 1, 5))):
                    if i == 3:
                        pe.wait_ge(gate_ready, 4 * layer + 1)
                    a = sec * D + half * 512
                    mm(ps[bank][:, :], ones, ada[:, a:a + 512], start=True, stop=True).then_inc(mod_summed, 1)

            def norm(n):
                if n == 0:
                    pe.wait_ge(s5_wT_ready, 5)
                for t in range(NT):
                    pe.wait_ge(hn_ready, NT * n + t + 1)
                    for k in range(KD):
                        c = (k % 2) * S + t * P
                        w = tr(ps[k // 2][:, c:c + P], hn[:, t, k * P:(k + 1) * P])
                        if t == NT - 1 and k % 2:
                            w.then_inc(hnT_done, 1)

            def arrived(got):
                pe.wait_ge(fill[got[0]], got[1])

            def project(w_item, n, banks, xT, waits=(), last_sem=None):
                ap, got = w_item
                arrived(got)
                for t in range(NT):
                    if waits:
                        pe.wait_ge(*waits[t])
                    for k in range(KD):
                        w = mm(ps[banks[t]][:, 0:n], xT[:, k, t * P:(t + 1) * P], ap[:, k, 0:n],
                               start=k == 0, stop=k == KD - 1)
                        if t == 0 and k == 0 and pending[0]:
                            w.then_inc(weights_used, 1)
                            pending[0] = False
                    w.then_inc(last_sem, 1)
                pending[0] = True

            pending = [False]

            def release(w):
                if pending[0]:
                    w.then_inc(weights_used, 1)
                    pending[0] = False

            def scores(n, qT_, kT_, hh):
                r = slice(HD * (hh % 2), HD * (hh % 2) + HD)
                if n >= 2:
                    pe.wait_ge(max_ready, n - 1)
                for t in range(NT):
                    w = mm(ps[n % 2][:, KOFF[t]:KOFF[t] + KEYS[t]], qT_[r, hh // 2, t * P:(t + 1) * P],
                           kT_[r, hh // 2, 0:KEYS[t]], start=True, stop=True)
                    if t == 0:
                        release(w)
                w.then_inc(score_done, 1)

            def probsT(n):
                pe.wait_ge(p_ready, n + 1)
                if n >= 2:
                    pe.wait_ge(pT_ready, n - 1)
                for i in range(3):
                    w = tr(ps[2 + n % 2][:, i * P:(i + 1) * P], sm[:, n % 2, i * P:(i + 1) * P])
                w.then_inc(pT_done, 1)

            def weigh(n, v, hh, cat0):
                pe.wait_ge(pT_ready, n + 1)
                pair = hh // 2
                if pair >= 2 and hh % 2 == 0:
                    pe.wait_ge(cat_ready, cat0 + pair - 1)
                r = slice(HD * (hh % 2), HD * (hh % 2) + HD)
                o = ps[4 + pair % 2]
                p_ = pT[:, n % 2, :]
                hc = slice(hh * HD, (hh + 1) * HD)
                mm(o[r, 0:P], v[:, 0, hc], p_[:, 0:P], start=True, stop=True)
                mm(o[r, P:2 * P], v[:, 0, hc], p_[:, P:2 * P], start=True, stop=False)
                mm(o[r, P:2 * P], v[:, 1, hc], p_[:, 2 * P:3 * P], start=False, stop=True).then_inc(o_done, 1)

            mod(0)
            norm(0)
            pe.wait_ge(uT_ready, 8)
            pe.wait_ge(mod_ready, 1)
            pe.wait_ge(gate_ready, 4)
            project(e_in[0], 512, (4, 5), uT, (), proj_done)
            project(e_in[1], 512, (6, 7), uT, (), proj_done)
            project(e_in[2], 512, (0, 1), uT, (), proj_done)
            ap, got = e_in[3]
            arrived(got)
            for c in range(4):
                for k in range(KD):
                    w = mm(ps[2 + c // 2][:, (c % 2) * S:(c % 2 + 1) * S], ap[:, k, c * P:(c + 1) * P], uT[:, k, :],
                           start=k == 0, stop=k == KD - 1)
                    release(w)
                if c % 2:
                    w.then_inc(proj_done, 1)
            pending[0] = True
            pe.wait_ge(rope_done, 4)
            pe.wait_ge(nope_done, 4)
            for i in range(2):
                for pr in range(4):
                    for t in range(NT):
                        w = tr(ps[4 + 2 * i + pr // 2][:, (pr % 2) * S + t * P:(pr % 2) * S + (t + 1) * P],
                               qk_tok[:, t, i * 512 + pr * P:i * 512 + (pr + 1) * P])
                        release(w)
                    if pr % 2:
                        w.then_inc(qkT_done, 1)
            pe.wait_ge(vs_ready, 4)
            pe.wait_ge(qkT_ready, 4)

            def drive(j):
                if j == 0:
                    pe.wait_ge(s5_wT_ready, 5)
                else:
                    pe.wait_ge(bu_used, j)
                r = slice(32 * (j % 4), 32 * (j % 4) + 32)
                for i in range(2):
                    w = mm(ps[6][:, i * S:(i + 1) * S], s5_bT[r, i, j // 4, :], s_inT[r, j // 4, :], start=True, stop=True,
                           tile_position=(32 * (j % 4), 0))
                w.then_inc(bu_done, 1)

            def read_out(j):
                pe.wait_ge(post_ready, j + 1)
                t = j // 4
                if j % 4 == 0 and t >= 1:
                    pe.wait_ge(y_pre, t)
                r = slice(32 * (j % 4), 32 * (j % 4) + 32)
                o = ps[7][r, (t % 2) * S:(t % 2 + 1) * S]
                x = post[:, j % 2]
                for i, (c, a, b) in enumerate(((0, 0, 0), (1, 1, 1), (2, 1, 0), (2, 0, 1))):
                    w = mm(o, s5_cT[:, c, t, r], x[:, a, b, :], start=i == 0, stop=i == 3,
                           tile_position=(0, 32 * (j % 4)))
                w.then_inc(y_part_done, 1)

            scores(0, qT, kT, 0)
            for hh in range(A_HEADS):
                if hh + 1 < A_HEADS:
                    scores(hh + 1, qT, kT, hh + 1)
                drive(2 * hh)
                if hh:
                    read_out(2 * hh - 1)
                probsT(hh)
                drive(2 * hh + 1)
                weigh(hh, v_tok, hh, 0)
                read_out(2 * hh)
            read_out(NCH - 1)
            pe.wait_ge(y_ready, 4)
            pe.wait_ge(max_ready, A_HEADS)
            ap, got = glu_w
            arrived(got)
            for c in range(4):
                for k in range(4):
                    w = mm(ps[c // 2][:, (c % 2) * S:(c % 2 + 1) * S], ap[:, k, c * P:(c + 1) * P], s5_y[:, k, :],
                           start=k == 0, stop=k == 3)
                w.then_inc(glu_done, 1)
            pending[0] = True
            pe.wait_ge(cat_ready, 8)
            for n in range(2):
                project(e_out[n], 512, (4 + 2 * n, 5 + 2 * n), catT, (), mix_out_done)

            norm(1)
            pe.wait_ge(uT_ready, 16)

            def gate_up(ap, bank, n, t, u, sem_, xT):
                for k in range(KD):
                    w = mm(ps[bank][:, 0:n], xT(k, t), ap[:, k, 0:n], start=k == 0, stop=k == KD - 1)
                    if k == 0:
                        first = w
                w.then_inc(sem_, 1)
                return first

            def mid_transposes(u, tiles):
                pe.wait_ge(mid_ready, u + 1)
                for i, (a, n) in enumerate(tiles):
                    w = tr(ps[2][0:n, i * P:(i + 1) * P], mid[:, a:a + n])
                w.then_inc(midT_done, 1)

            xu = lambda k, t: uT[:, k, t * P:(t + 1) * P]

            def ff_block(b, first, final):
                def filled(j):
                    v = ff_fill0[j] + ff_inc[j]
                    pe.wait_ge(fill[ff_slot[j]], b * ff_inc[j] + v)

                def down(t, u):
                    pe.wait_ge(midT_ready, u + 1)
                    if t == 0:
                        filled(2)
                    ap = block_ap(ff_slot[2], 3, D)
                    for i, (a, n) in enumerate(FT):
                        for half in range(2):
                            w = mm(ps[4 + 2 * t + half][:, :], midT[0:n, i, :], ap[0:n, i, half * 512:(half + 1) * 512],
                                   start=first and i == 0, stop=final and i == 2)
                            if i == 0 and half == 0:
                                begun = w
                    return begun, w

                gate, up = block_ap(ff_slot[0], KD, FW), block_ap(ff_slot[1], KD, FW)
                u0 = b * NT
                filled(0)
                if not first:
                    pe.wait_ge(silu_done, u0)
                w = gate_up(gate, 0, FW, 0, u0, gate_done, xu)
                if first:
                    release(w)
                filled(1)
                if not first:
                    pe.wait_ge(mid_ready, u0)
                gate_up(up, 1, FW, 0, u0, up_done, xu)
                pe.wait_ge(silu_done, u0 + 1)
                gate_up(gate, 0, FW, 1, u0 + 1, gate_done, xu)
                mid_transposes(u0, FT)
                gate_up(up, 1, FW, 1, u0 + 1, up_done, xu).then_inc(weights_used, 1)
                down(0, u0)[0].then_inc(weights_used, 1)
                mid_transposes(u0 + 1, FT)
                down(1, u0 + 1)[1].then_inc(weights_used, 1)


            ff_block(0, True, False)
            with pe.Fori(1, FB - 1) as b:
                ff_block(b, False, False)
            ff_block(FB - 1, False, True)

            mod(1)
            norm(2)
            pe.wait_ge(uT_ready, 24)
            pe.wait_ge(mod_ready, 2)
            pe.wait_ge(gate_ready, 8)
            project(o_in[0], 256, (0, 1), uT, (), proj_done)
            project(o_in[1], 384, (2, 3), uT, (), proj_done)
            project(o_in[2], 384, (4, 5), uT, (), proj_done)
            project(o_in[3], 272, (6, 7), uT, (), proj_done)
            project(o_in[4], 512, (0, 1), uT, ((rope_done, 5), (rope_done, 6)), proj_done)
            project(o_in[5], 2 * HD - HD + IH, (2, 3), uT, ((nope_done, 5), (nope_done, 6)), proj_done)
            pe.wait_ge(nope_done, 8)
            for t in range(NT):
                pe.wait_ge(ckv_ready, t + 1)
                for k in range(2):
                    w = tr(ps[4][:, k * S + t * P:k * S + (t + 1) * P], ckr[:, t, k * P:(k + 1) * P])
            w.then_inc(ckvT_done, 1)
            pe.wait_ge(ckvT_ready, 2)
            pe.wait_ge(nope_done, 10)
            arrived(ukv)
            for i in range(4):
                t, half = i // 2, i % 2
                for k in range(2):
                    w = mm(ps[4 + i][:, 0:384], ckvT[:, k, t * P:(t + 1) * P], uk_ap[:, k, half * 384:(half + 1) * 384],
                           start=k == 0, stop=k == 1)
                    release(w)
                w.then_inc(kv_done, 1)
            pe.wait_ge(rope_done, 10)
            pe.wait_ge(nope_done, 12)
            for i in range(4):
                t, half = i // 2, i % 2
                for k in range(2):
                    w = mm(ps[i][:, :], ckvT[:, k, t * P:(t + 1) * P], uv_ap[:, k, half * 512:(half + 1) * 512],
                           start=k == 0, stop=k == 1)
                w.then_inc(kv_done, 1)
            pending[0] = True
            pe.wait_ge(kn_ready, 4)
            for pr in range(4):
                for t in range(NT):
                    w = tr(ps[4 + pr // 2][:, (pr % 2) * S + t * P:(pr % 2) * S + (t + 1) * P],
                           q_i[:, t, 2 * pr:2 * pr + 2, :].rearrange("p h d -> p (h d)"))
                    release(w)
                if pr % 2:
                    w.then_inc(idxT_done, 1)
            for t in range(NT):
                w = tr(ps[6][:, t * P:(t + 1) * P], k_iw[:, t, 0:2 * HD])
            w.then_inc(idxT_done, 1)
            pe.wait_ge(idxT_ready, 3)
            pe.wait_ge(v_ready, 4)
            for i in range(IH):
                r = slice(HD * (i % 2), HD * (i % 2) + HD)
                if i >= 2:
                    pe.wait_ge(relu_ready, i - 1)
                for t in range(NT):
                    w = mm(ps[i % 2][:, KOFF[t]:KOFF[t] + KEYS[t]], qiT[r, i // 2, t * P:(t + 1) * P], kiT[r, 0:KEYS[t]],
                           start=True, stop=True)
                w.then_inc(logit_done, 1)
            pe.wait_ge(rope_done, 12)
            for i, src in enumerate((q_tok, kcat)):
                for pr in range(8):
                    if i and pr % 2 == 0:
                        pe.wait_ge(qkT_ready, 4 + pr // 2 + 1)
                    for t in range(NT):
                        w = tr(ps[4 + pr // 2][:, (pr % 2) * S + t * P:(pr % 2) * S + (t + 1) * P],
                               src[:, t, 2 * pr:2 * pr + 2, :].rearrange("p h d -> p (h d)"))
                    if pr % 2:
                        w.then_inc(qkT_done, 1)
            pe.wait_ge(qkT_ready, 12)
            pe.wait_ge(relu_ready, IH)
            scores(A_HEADS, qT1, kT1, 0)
            for hh in range(C_HEADS):
                n = A_HEADS + hh
                if hh + 1 < C_HEADS:
                    scores(n + 1, qT1, kT1, hh + 1)
                probsT(n)
                weigh(n, v1, hh, 8)
            pe.wait_ge(cat_ready, 16)
            for n in range(2):
                project(o_out[n], 512, (4 + 2 * n, 5 + 2 * n), ctxT, (), mix_out_done)

            norm(3)
            pe.wait_ge(uT_ready, 32)
            pe.wait_ge(late_in, 16 * 7)
            for t in range(NT):
                for k in range(KD):
                    w = mm(ps[4][:, t * E:(t + 1) * E], uT[:, k, t * P:(t + 1) * P], w_r[:, k, :],
                           start=k == 0, stop=k == KD - 1)
                    release(w)
            w.then_inc(router_done, 1)
            pe.wait_ge(member_ready, 1)
            member = lambda t: rt[:, t, 16:24]
            mm(ps[5][:, 0:E], tri, member(0), start=True, stop=True)
            mm(ps[5][:, E:2 * E], tri, member(1), start=True, stop=False)
            mm(ps[5][:, E:2 * E], ones, member(0), start=False, stop=True)
            mm(ps[5][:, 2 * E:3 * E], ones, member(0), start=True, stop=False)
            mm(ps[5][:, 2 * E:3 * E], ones, member(1), start=False, stop=True).then_inc(pos_done, 1)

            def gather(g):
                pe.wait_ge(sel_ready, g + 1)
                for bank in range(2):
                    for k in range(4):
                        kk = 4 * bank + k
                        for t in range(NT):
                            w = mm(ps[6 + bank][:, k * P:(k + 1) * P], hn[:, t, kk * P:(kk + 1) * P], sel[:, t, :],
                                   start=t == 0, stop=t == NT - 1)
                    w.then_inc(gather_done, 1)
                for t in range(NT):
                    w = mm(ps[3][:, 0:2], sel[:, t, :], info[:, t, :], start=t == 0, stop=t == NT - 1)
                w.then_inc(info_done, 1)

            xe = lambda k, t: ueT[:, k, :]
            UF = FB * NT

            def expert(job, g, gather_next):
                def filled(m):
                    pe.wait_ge(fill[m % NS1], job * (16 * PER) + (moe_fill0[m % NS1] + 16 * (m // NS1 + 1)))

                def unit(b):
                    return job * MB + (UF + b)

                def down(b):
                    m = moe_at["down", b]
                    pe.wait_ge(midT_ready, unit(b) + 1)
                    filled(m)
                    ap = block_ap(slot_of(m), 4, D)
                    for i in range(4):
                        for half in range(2):
                            w = mm(ps[4 + half][:, :], midT[:, i, :], ap[:, i, half * 512:(half + 1) * 512],
                                   start=b == 0 and i == 0, stop=b == MB - 1 and i == 3)
                            if i == 0 and half == 0:
                                begun = w
                    return begun, w

                tiles = [(i * P, P) for i in range(4)]
                pe.wait_ge(ueT_ready, g * 8 + 8)
                for b in range(MB):
                    filled(moe_at["gate", b])
                    pe.wait_ge(silu_done, unit(b))
                    gate_up(block_ap(slot_of(moe_at["gate", b]), KD, 512), 0, 512, 0, None, gate_done, xe)
                    if b:
                        mid_transposes(unit(b - 1), tiles)
                    else:
                        pe.wait_ge(mid_ready, unit(0))
                    filled(moe_at["up", b])
                    gate_up(block_ap(slot_of(moe_at["up", b]), KD, 512), 1, 512, 0, None, up_done, xe)\
                        .then_inc(weights_used, 1)
                    if b:
                        begun, w = down(b - 1)
                        begun.then_inc(weights_used, 1)
                        w.then_inc(weights_used, 1)
                if gather_next:
                    gather(g + 1)
                mid_transposes(unit(MB - 1), tiles)
                begun, w = down(MB - 1)
                begun.then_inc(weights_used, 1)
                w.then_inc(weights_used, 1)
                pe.wait_ge(y_sb_ready, job * 2 + 2)
                pe.wait_ge(selT_ready, job + 1)
                if gather_next:
                    pe.wait_ge(ueT_ready, g * 8 + 16)
                for i in range(4):
                    t, half = i // 2, i % 2
                    if i >= 2:
                        pe.wait_ge(scatter_added, job * 4 + (i - 1))
                    mm(ps[6 + i % 2][:, :], selT[:, t * P:(t + 1) * P], y_sb[:, half * 512:(half + 1) * 512],
                       start=True, stop=True).then_inc(scatter_done, 1)
                pe.wait_ge(scatter_added, job * 4 + 4)

            slot_of = lambda m: m % NS1
            gather(0)
            with pe.Fori(0, E) as e:
                expert(e, e, True)
            pe.wait_ge(tables_ready, 1)
            with pe.If(pe.value_load(job_tab[0:1, 2 * E:2 * E + 1], min_val=0, max_val=E) > 0):
                with pe.Fori(0, E) as e:
                    n_e = pe.value_load(job_tab[0:1, bass.ds(e, 1)], min_val=0, max_val=S)
                    with pe.If(n_e > OVER):
                        job = pe.value_load(job_tab[0:1, bass.ds(e + E, 1)], min_val=E, max_val=2 * E)
                        gather(job + 1)
                        expert(job, job + 1, False)

        @block.scalar
        def _(act):
            fn = nc.scalar.activation
            par = lambda i: s5_p[:, i, :]
            step = Steps(act, act_steps)

            act.wait_ge(vec_in, 16)
            fn(c_col[:, :], c_col[:, :], ACT.Silu).then_inc(c_ready, 1)
            act.wait_ge(s5_in, 16 * 10)
            fn(par(DT), par(LDT), ACT.Exp).then_inc(s5_dt, 1)
            act.wait_ge(s5_x, 1)
            fn(par(MAG), par(X1), ACT.Exp).then_inc(s5_mag, 1)
            act.wait_ge(s5_r, 1)
            fn(par(SN), par(RR), ACT.Sin)
            fn(par(SH), par(RH), ACT.Sin).then_inc(s5_sin, 1)
            for i, (dst, scale) in enumerate(((s5_bT[:, 0], 1.0), (s5_bT[:, 1], 1.0), (s5_cT[:, 0], 1.0),
                                              (s5_cT[:, 1], -1.0), (s5_cT[:, 2], -1.0))):
                bank = ps[(0, 1, 2, 2, 3)[i]]
                act.wait_ge(s5_padT, (1, 2, 3, 3, 4)[i])
                fn(dst, bank[:, :].rearrange("p (t q) -> p t q", t=4), ACT.Copy, scale=scale).then_inc(s5_wT_ready, 1)

            def gates(layer):
                for i, (row, half, bank) in enumerate(((0, 0, 5), (0, 1, 6), (1, 0, 7), (1, 1, 5))):
                    act.wait_ge(mod_summed, 5 * layer + 2 + i)
                    fn(gate_row[:, row, half * 512:(half + 1) * 512], ps[bank][:, :], ACT.Copy).then_inc(gate_ready, 1)

            def rms(src, junk, width, n):
                for t in range(NT):
                    w = fn(junk(t), src(t), ACT.Square, accum_out=stat[:, t:t + 1])
                    step(w)
                step.wait()
                fn(stat[:, 2:4], stat[:, 0:2], ACT.Sqrt, bias=eps[:, 0:1], scale=1.0 / width).then_inc(rms_ready, 1)

            def norm_stats(n):
                if n == 0:
                    act.wait_ge(x_in, 16)
                    act.wait_ge(s5_wT_ready, 5)
                else:
                    act.wait_ge(h_ready, 4 * n)
                act.wait_ge(eps_ready, 1)
                rms(lambda t: h[:, t, :], lambda t: hn[:, t, :], D, n)

            def norm_out(n):
                m = n % 2
                act.wait_ge(mod_ready, n // 2 + 1)
                for k in (0, 1, 4, 5):
                    act.wait_ge(hnT_done, 4 * n + k // 2 + 1)
                    fn(uT[:, k, :], ps[k // 2][:, (k % 2) * S:(k % 2 + 1) * S], ACT.Identity, scale=mod_a[:, m, k:k + 1],
                       bias=mod_b[:, m, k:k + 1]).then_inc(uT_ready, 1)

            def heads(ap, n, width=HD):
                return ap.rearrange("p (h d) -> p h d", h=n)

            def exps(n, l1):
                act.wait_ge(max_ready, n + 1)
                q = n % 2
                for t in range(NT):
                    x = sm[:, q, KOFF[t]:KOFF[t] + KEYS[t]]
                    w = fn(x, x, ACT.Exp, scale=SC, bias=stat[:, 10 + 2 * q + t:11 + 2 * q + t],
                           **({"accum_out": stat[:, 14 + 2 * q + t:15 + 2 * q + t]} if l1 else {}))
                w.then_inc(exp_ready, 1)

            def probsT_out(n):
                act.wait_ge(pT_done, n + 1)
                if n >= 2:
                    act.wait_ge(o_done, n - 1)
                fn(pT[:, n % 2, :], ps[2 + n % 2][:, 0:KW], ACT.Copy).then_inc(pT_ready, 1)

            norm_stats(0)
            gates(0)
            norm_out(0)
            for i in range(4):
                act.wait_ge(proj_done, i + 1)
                t, a = i % 2, (i // 2) * 512
                fn(heads(qk_tok[:, t, a:a + 512], 8)[:, :, ROPE:], heads(ps[4 + i][:, :], 8)[:, :, ROPE:],
                   ACT.Copy).then_inc(nope_done, 1)
            for t in range(NT):
                act.wait_ge(proj_done, 5 + t)
                fn(v_tok[:, t, :], ps[t][:, :], ACT.Copy).then_inc(vs_ready, 1)
            for i in range(2):
                act.wait_ge(proj_done, 7 + i)
                fn(s_inT[:, 2 * i:2 * i + 2, :], ps[2 + i][:, :].rearrange("p (c s) -> p c s", c=2), ACT.Copy).then_inc(vs_ready, 1)
            for i, dst in ((1, qT), (3, kT)):
                act.wait_ge(qkT_done, i + 1)
                fn(dst[:, 2:4, :], ps[4 + i][:, :].rearrange("p (c s) -> p c s", c=2), ACT.Copy).then_inc(qkT_ready, 1)
            exps(0, False)
            for hh in range(A_HEADS):
                if hh + 1 < A_HEADS:
                    exps(hh + 1, False)
                probsT_out(hh)
            act.wait_ge(y_pre, 4)
            for t in range(4):
                fn(s5_y[:, t, :], s5_y[:, t, :], ACT.Gelu_apprx_tanh).then_inc(y_ready, 1)
            th = lambda c: hn.rearrange("p t d -> p (t d)")[:, c * S:(c + 1) * S]
            act.wait_ge(s5_pads, 1)
            act.wait_ge(y_part_done, NCH)
            for c in range(4):
                act.wait_ge(glu_done, 2 * (c // 2) + 2)
                fn(th(c), ps[c // 2][:, (c % 2) * S:(c % 2 + 1) * S], ACT.Tanh, scale=0.5,
                   bias=s5_bg[:, c:c + 1]).then_inc(glu_tanh, 1)

            norm_stats(1)
            norm_out(1)

            def silus(u, n, first=False):
                act.wait_ge(gate_done, u + 1)
                if not first:
                    act.wait_ge(mid_ready, u)
                fn(silu[:, 0:n], ps[0][:, 0:n], ACT.Silu).then_inc(silu_done, 1)

            def mid_out(u, tiles):
                act.wait_ge(midT_done, u + 1)
                full = [i for i, (_, n) in enumerate(tiles) if n == P]
                w = fn(midT[:, 0:len(full), :], ps[2][:, 0:len(full) * P].rearrange("p (i t) -> p i t", i=len(full)), ACT.Copy)
                if len(full) < len(tiles):
                    n = tiles[-1][1]
                    w = fn(midT[0:n, len(full), :], ps[2][0:n, len(full) * P:(len(full) + 1) * P], ACT.Copy)
                w.then_inc(midT_ready, 1)

            def ff_block(b, first=False):
                u0 = b * NT
                silus(u0, FW, first)
                silus(u0 + 1, FW)
                mid_out(u0, FT)
                mid_out(u0 + 1, FT)

            ff_block(0, True)
            with act.Fori(1, FB) as b:
                ff_block(b)

            norm_stats(2)
            gates(1)
            norm_out(2)
            for j in range(2):
                for t in range(NT):
                    act.wait_ge(proj_done, 11 + 2 * j + t)
                    fn(q_tok[:, t, 8 * j:8 * j + 8, ROPE:], heads(ps[2 + 2 * j + t][:, 0:384], 8), ACT.Copy).then_inc(nope_done, 1)
            for t in range(NT):
                act.wait_ge(proj_done, 15 + t)
                fn(ckr[:, t, :], ps[6 + t][:, 0:LAT + ROPE], ACT.Copy).then_inc(nope_done, 1)
            act.wait_ge(nope_done, 10)
            rms(lambda t: ckr[:, t, 0:LAT], lambda t: kcat[:, t, 0:4, :].rearrange("p h d -> p (h d)"), LAT, 0)
            for t in range(NT):
                act.wait_ge(proj_done, 17 + t)
                fn(q_i[:, t, :, ROPE:], heads(ps[t][:, :], 8)[:, :, ROPE:], ACT.Copy).then_inc(nope_done, 1)
            step.wait()
            for i in range(4):
                t, half = i // 2, i % 2
                act.wait_ge(kv_done, i + 1)
                fn(kcat[:, t, 8 * half:8 * half + 8, ROPE:], heads(ps[4 + i][:, 0:384], 8), ACT.Copy).then_inc(kn_ready, 1)
            for i in range(2):
                act.wait_ge(idxT_done, i + 1)
                fn(qiT[:, 2 * i:2 * i + 2, :], ps[4 + i][:, :].rearrange("p (c s) -> p c s", c=2), ACT.Copy).then_inc(idxT_ready, 1)
            for i in range(IH):
                act.wait_ge(logit_done, i + 1)
                if i >= 2:
                    act.wait_ge(score_added, i - 1)
                fn(sm[:, i % 2, :], ps[i % 2][:, 0:KW], ACT.Relu, scale=SC).then_inc(relu_ready, 1)
            for i in range(8):
                act.wait_ge(qkT_done, 5 + i)
                dst = (qT1, kT1)[i // 4]
                fn(dst[:, 2 * (i % 4):2 * (i % 4) + 2, :], ps[4 + i % 4][:, :].rearrange("p (c s) -> p c s", c=2),
                   ACT.Copy).then_inc(qkT_ready, 1)
            exps(A_HEADS, True)
            for hh in range(C_HEADS):
                n = A_HEADS + hh
                if hh + 1 < C_HEADS:
                    exps(n + 1, True)
                probsT_out(n)

            norm_stats(3)
            norm_out(3)
            act.wait_ge(gap_ready, 1)
            fn(rt[:, :, 40:41], rt[:, :, 41:42], ACT.Exp).then_inc(gap_exp, 1)

            UF = FB * NT

            def slots_in(g):
                for k in range(4):
                    act.wait_ge(gather_done, g * 2 + (k // 4 + 1))
                    fn(ueT[:, k, :], ps[6 + k // 4][:, (k % 4) * P:(k % 4 + 1) * P], ACT.Identity,
                       scale=mod_a[:, 1, k:k + 1], bias=mod_b[:, 1, k:k + 1]).then_inc(ueT_ready, 1)

            def expert(job, g, gather_next):
                tiles = [(i * P, P) for i in range(4)]
                for b in range(MB):
                    u = job * MB + (UF + b)
                    silus(u, 512)
                    if b:
                        mid_out(u - 1, tiles)
                if gather_next:
                    slots_in(g + 1)
                mid_out(job * MB + (UF + MB - 1), tiles)
                for half in range(2):
                    act.wait_ge(weights_used, job * NI + (moe_w0 + NI))
                    fn(y_sb[:, half * 512:(half + 1) * 512], ps[4 + half][:, :], ACT.Copy).then_inc(y_sb_ready, 1)

            slots_in(0)
            with act.Fori(0, E) as e:
                expert(e, e, True)
            act.wait_ge(tables_ready, 1)
            with act.If(act.value_load(job_tab[0:1, 2 * E:2 * E + 1], min_val=0, max_val=E) > 0):
                with act.Fori(0, E) as e:
                    n_e = act.value_load(job_tab[0:1, bass.ds(e, 1)], min_val=0, max_val=S)
                    with act.If(n_e > OVER):
                        job = act.value_load(job_tab[0:1, bass.ds(e + E, 1)], min_val=E, max_val=2 * E)
                        slots_in(job + 1)
                        expert(job, job + 1, False)
            norm_stats(4)

        @block.vector
        def _(dve):
            V = nc.vector
            par = lambda i: s5_p[:, i, :]
            step = Steps(dve, dve_steps)

            def chained(ins):
                step(ins)
                step.wait()

            V.memset(eps[:, :], EPS).then_inc(eps_ready, 1)

            def ada_item(ap, col, width, looped=None):
                for k in range(KD):
                    o = ada[:, col:col + width] if looped is None else ada[:, bass.ds(col, width)]
                    w = V.scalar_tensor_tensor(o, ap[:, k, :], c_col[:, k:k + 1], o, ALU.mult, ALU.add)
                    if k < KD - 1:
                        chained(w)
                w.then_inc(ada_used, 1)

            dve.wait_ge(c_ready, 1)
            dve.wait_ge(bias_in, 16)
            for i in range(NA0):
                ap, got = ada0[i]
                dve.wait_ge(fill[got[0]], got[1])
                ada_item(ap, i * ADA0, ADA0)
                if i == 3:
                    dve.wait_ge(s5_den, 1)
                    V.reciprocal(par(RDEN), par(DEN)).then_inc(s5_rden, 1)

            def mod(layer):
                dve.wait_ge(mod_summed, 5 * layer + 1)
                dve.wait_ge(late_in, 16 * 7)
                m = lambda i: ps[4][:, i * KD:(i + 1) * KD]
                for j in range(2):
                    V.tensor_copy(mod_b[:, j, :], m(2 * j))
                    w = V.scalar_tensor_tensor(mod_a[:, j, :], m(2 * j + 1), 1.0, g_col[:, 2 * j + layer, :], ALU.add, ALU.mult)
                w.then_inc(mod_ready, 1)

            def norm_scale(n, count):
                dve.wait_ge(rms_ready, count)
                chained(V.reciprocal(stat[:, 4:6], stat[:, 2:4]))
                for t in range(NT):
                    V.tensor_scalar(hn[:, t, :], h[:, t, :], stat[:, 4 + t:5 + t], None, ALU.mult).then_inc(hn_ready, 1)

            def norm_out(n):
                m = n % 2
                dve.wait_ge(mod_ready, n // 2 + 1)
                for k in (2, 3, 6, 7):
                    dve.wait_ge(hnT_done, 4 * n + k // 2 + 1)
                    V.tensor_scalar(uT[:, k, :], ps[k // 2][:, (k % 2) * S:(k % 2 + 1) * S], mod_a[:, m, k:k + 1], mod_b[:, m, k:k + 1],
                                    ALU.mult, ALU.add).then_inc(uT_ready, 1)

            def rope(dst, src, t, n, sem_):
                x1, x2 = src[:, :, 0:HALF], src[:, :, HALF:ROPE]
                a, b = rope_buf[:, 0, 0:n, :], rope_buf[:, 1, 0:n, :]
                step(V.tensor_tensor(a, x1, cos(t, n), ALU.mult))
                chained(V.tensor_tensor(b, x2, sin(t, n), ALU.mult))
                chained(V.tensor_tensor(dst[:, :, 0:HALF], a, b, ALU.subtract))
                step(V.tensor_tensor(a, x2, cos(t, n), ALU.mult))
                chained(V.tensor_tensor(b, x1, sin(t, n), ALU.mult))
                V.tensor_tensor(dst[:, :, HALF:ROPE], a, b, ALU.add).then_inc(sem_, 1)

            def heads(ap, n):
                return ap.rearrange("p (h d) -> p h d", h=n)

            def mask_max(n, neg):
                dve.wait_ge(score_done, n + 1)
                if n >= 2:
                    dve.wait_ge(pT_done, n - 1)
                q = n % 2
                chained(V.tensor_tensor(sm[:, q, :], ps[q][:, 0:KW], neg, ALU.add))
                for t in range(NT):
                    w = V.reduce_max(stat[:, 6 + 2 * q + t:7 + 2 * q + t], sm[:, q, KOFF[t]:KOFF[t] + KEYS[t]], axis=AX.X)
                    step(w)
                step.wait()
                V.tensor_scalar(stat[:, 10 + 2 * q:12 + 2 * q], stat[:, 6 + 2 * q:8 + 2 * q], -SC, None,
                                ALU.mult).then_inc(max_ready, 1)

            def probs(n, l1):
                dve.wait_ge(exp_ready, n + 1)
                q = n % 2
                den, rden = stat[:, 14 + 2 * q:16 + 2 * q], stat[:, 18 + 2 * q:20 + 2 * q]
                if not l1:
                    for t in range(NT):
                        x = sm[:, q, KOFF[t]:KOFF[t] + KEYS[t]]
                        c = cst[:, C_CNT + KOFF[t]:C_CNT + KOFF[t] + KEYS[t]]
                        step(V.tensor_tensor_reduce(out=x, in0=x, in1=c, scale=1.0, scalar=0.0, op0=ALU.mult, op1=ALU.add,
                                                    accum_out=den[:, t:t + 1]))
                    step.wait()
                chained(V.reciprocal(rden, den))
                for t in range(NT):
                    x = sm[:, q, KOFF[t]:KOFF[t] + KEYS[t]]
                    w = V.tensor_scalar(x, x, rden[:, t:t + 1], None, ALU.mult)
                w.then_inc(p_ready, 1)

            def head_out(n, dst, pair):
                dve.wait_ge(o_done, n + 1)
                V.tensor_copy(dst[:, pair, :], ps[4 + pair % 2][:, 0:S]).then_inc(cat_ready, 1)

            def residual(count, m, base, in0=None, h0=0):
                for i in range(4):
                    n, t = i // 2, i % 2
                    if in0 is None:
                        dve.wait_ge(mix_out_done, base + i + 1)
                        y = ps[4 + 2 * n + t][:, :]
                    else:
                        y = in0(n, t)
                    tmp = flat_uT[:, i * 512:(i + 1) * 512]
                    chained(V.tensor_tensor(tmp, y, gate_row[:, m, n * 512:(n + 1) * 512], ALU.mult))
                    x = h[:, t, n * 512:(n + 1) * 512]
                    V.tensor_tensor(x, x, tmp, ALU.add).then_inc(h_ready, 1)

            mod(0)
            norm_scale(0, 1)
            norm_out(0)
            for i in range(4):
                dve.wait_ge(nope_done, i + 1)
                t, a = i % 2, (i // 2) * 512
                rope(heads(qk_tok[:, t, a:a + 512], 8), heads(ps[4 + i][:, :], 8), t, 8, rope_done)
                dve.wait_ge(rope_done, i + 1)
            for i, dst in ((0, qT), (2, kT)):
                dve.wait_ge(qkT_done, i + 1)
                V.tensor_copy(dst[:, 0:2, :], ps[4 + i][:, :].rearrange("p (c s) -> p c s", c=2)).then_inc(qkT_ready, 1)

            def turn(j):
                dve.wait_ge(bu_done, j + 1)
                if j == 0:
                    dve.wait_ge(phase_ready, 1)
                bu = ps[6][:, :].rearrange("p (a s) -> p a s", a=2)
                c = lambda i: phase[:, i, j, :].unsqueeze(1).broadcast_to([P, 2, S])
                step.wait()
                step(V.tensor_tensor(rotA, bu, c(0), ALU.mult))
                V.tensor_tensor(rotB, bu, c(1), ALU.mult).then_inc(bu_used, 1)
                dve.wait_ge(bu_used, j + 1)
                step(V.tensor_tensor(s5_v[:, 0, :], rotA[:, 0, :], rotB[:, 1, :], ALU.add))
                chained(V.tensor_tensor(s5_v[:, 1, :], rotA[:, 1, :], rotB[:, 0, :], ALU.subtract))
                if j >= 2:
                    dve.wait_ge(post_ready, j - 1)
                z = zbuf[:, j % 2]
                for i in range(2):
                    w = V.tensor_tensor_scan(z[:, i, :], s5_p[:, MAG, j:j + 1].broadcast_to([P, S]), s5_v[:, i, :],
                                             0.0, ALU.mult, ALU.add)
                    if i == 0:
                        step(w)
                w.then_inc(z_ready, 1)
                dve.wait_ge(z_ready, j + 1)

            def y_before_gelu(t):
                dve.wait_ge(y_part_done, 4 * t + 4)
                V.scalar_tensor_tensor(s5_y[:, t, :], s_inT[:, t, :], s5_d[:, t:t + 1], ps[7][:, (t % 2) * S:(t % 2 + 1) * S],
                                       ALU.mult, ALU.add).then_inc(y_pre, 1)

            dve.wait_ge(vs_ready, 4)
            neg0 = cst[:, C_NEG:C_NEG + KW]
            mask_max(0, neg0)
            for hh in range(A_HEADS):
                if hh + 1 < A_HEADS:
                    mask_max(hh + 1, neg0)
                turn(2 * hh)
                probs(hh, False)
                turn(2 * hh + 1)
                if hh % 2:
                    head_out(hh, catT, hh // 2)
                elif hh:
                    y_before_gelu(hh // 2 - 1)
            y_before_gelu(3)
            for c in range(4):
                dve.wait_ge(glu_tanh, c + 1)
                t = hn.rearrange("p t d -> p (t d)")[:, c * S:(c + 1) * S]
                chained(V.tensor_scalar(t, t, 0.5, 0.5, ALU.mult, ALU.add))
                V.tensor_tensor(catT[:, 4 + c, :], t, s5_y[:, c, :], ALU.mult).then_inc(cat_ready, 1)
            residual(0, 0, 0)

            norm_scale(1, 2)
            norm_out(1)
            dve.wait_ge(bias_in, 32)

            def mids(u, n, first=False):
                dve.wait_ge(up_done, u + 1)
                dve.wait_ge(silu_done, u + 1)
                if not first:
                    dve.wait_ge(midT_done, u)
                V.tensor_tensor(mid[:, 0:n], ps[1][:, 0:n], silu[:, 0:n], ALU.mult).then_inc(mid_ready, 1)

            def ff_block(b, first=False):
                mids(b * NT, FW, first)
                mids(b * NT + 1, FW)
                for i in range(2):
                    s = ff_slot[3 + i]
                    dve.wait_ge(fill[s], b * 16 + (ff_fill0[3 + i] + 16))
                    ada_item(block_ap(s, KD, ADA1), b * (2 * ADA1) + i * ADA1, ADA1, b)

            ff_block(0, True)
            with dve.Fori(1, FB) as b:
                step.enter(b, 1, 2 * (KD - 1))
                ff_block(b)
            step.leave(1, FB - 1)
            dve.wait_ge(weights_used, ff_w0 + 3 * FB)
            residual(0, 1, 0, lambda n, t: ps[4 + 2 * t + n][:, :])

            mod(1)
            norm_scale(2, 3)
            norm_out(2)
            for t in range(NT):
                dve.wait_ge(proj_done, 9 + t)
                rope(q_tok[:, t], heads(ps[t][:, 0:256], 16), t, 16, rope_done)
                dve.wait_ge(rope_done, 5 + t)
            dve.wait_ge(rms_ready, 4)
            chained(V.reciprocal(stat[:, 4:6], stat[:, 2:4]))
            for t in range(NT):
                V.tensor_scalar(ckr[:, t, 0:LAT], ckr[:, t, 0:LAT], stat[:, 4 + t:5 + t], None, ALU.mult).then_inc(ckv_ready, 1)
            for t in range(NT):
                dve.wait_ge(nope_done, 11 + t)
                rope(q_i[:, t], heads(ps[t][:, :], 8), t, 8, rope_done)
                dve.wait_ge(rope_done, 7 + t)
            for t in range(NT):
                dve.wait_ge(proj_done, 19 + t)
                kk = k_iw[:, t, :]
                step(V.tensor_copy(kk[:, ROPE:HD], ps[2 + t][:, ROPE:HD]))
                step(V.tensor_scalar(kk[:, 2 * HD:], ps[2 + t][:, HD:HD + IH], IH ** -0.5, None, ALU.mult))
                rope(kk[:, 0:HD].unsqueeze(1), ps[2 + t][:, 0:HD].unsqueeze(1), t, 1, rope_done)
                dve.wait_ge(rope_done, 9 + t)
                step.wait()
                step(V.tensor_copy(kk[:, HD:2 * HD], kk[:, 0:HD]))
            for k in range(2):
                dve.wait_ge(ckvT_done, 1)
                V.tensor_scalar(ckvT[:, k, :], ps[4][:, k * S:(k + 1) * S], g_kv[:, k:k + 1], None, ALU.mult).then_inc(ckvT_ready, 1)
            for t in range(NT):
                kr = kr_t[:, :].unsqueeze(1)
                rope(kr, ckr[:, t, LAT:].unsqueeze(1), t, 1, dve_steps)
                step.n += 1
                step.wait()
                V.tensor_copy(kcat[:, t, :, 0:ROPE], kr.broadcast_to([P, C_HEADS, ROPE])).then_inc(rope_done, 1)
                dve.wait_ge(rope_done, 11 + t)
            for i in range(4):
                t, half = i // 2, i % 2
                dve.wait_ge(kv_done, 5 + i)
                V.tensor_copy(v1[:, t, half * 512:(half + 1) * 512], ps[i][:, :]).then_inc(v_ready, 1)
            dve.wait_ge(idxT_done, 3)
            V.tensor_copy(kiT[:, :], ps[6][:, 0:S]).then_inc(idxT_ready, 1)
            for i in range(IH):
                dve.wait_ge(relu_ready, i + 1)
                for t in range(NT):
                    c = slice(KOFF[t], KOFF[t] + KEYS[t])
                    wi = k_iw[:, t, 2 * HD + i:2 * HD + i + 1]
                    if i == 0:
                        w = V.tensor_scalar(score[:, c], sm[:, 0, c], wi, None, ALU.mult)
                    else:
                        w = V.scalar_tensor_tensor(score[:, c], sm[:, i % 2, c], wi, score[:, c], ALU.mult, ALU.add)
                w.then_inc(score_added, 1)
                dve.wait_ge(score_added, i + 1)
            chained(V.tensor_tensor(score, score, cst[:, C_CB:C_CB + KW], ALU.add))
            for i in range(TOPK // 8):
                for t in range(NT):
                    step(V.max(top8[:, t, :], score[:, KOFF[t]:KOFF[t] + KEYS[t]]))
                step.wait()
                for t in range(NT):
                    x = score[:, KOFF[t]:KOFF[t] + KEYS[t]]
                    step(V.match_replace(x, top8[:, t, :], x, NEG))
                step.wait()
            chained(V.tensor_scalar(selneg, score, NEG / 3, BIG, ALU.is_le, ALU.mult))
            chained(V.tensor_tensor(selneg, selneg, cst[:, C_CAU:C_CAU + KW], ALU.mult))
            chained(V.tensor_scalar(selneg, selneg, BIG, None, ALU.subtract))
            mask_max(A_HEADS, selneg)
            for hh in range(C_HEADS):
                n = A_HEADS + hh
                if hh + 1 < C_HEADS:
                    mask_max(n + 1, selneg)
                probs(n, True)
                if hh % 2:
                    head_out(n, ctxT, hh // 2)
            residual(0, 0, 4)

            norm_scale(3, 5)
            norm_out(3)
            dve.wait_ge(router_done, 1)
            for t in range(NT):
                step(V.tensor_tensor(lg[:, t, :], ps[4][:, t * E:(t + 1) * E], b_r[:, :], ALU.add))
            step(V.memset(possel[:, :, E:E + 1], -1.0))
            step(V.memset(comb[:, :, E:E + 1], 0.0))
            step.wait()
            for t in range(NT):
                step(V.max(top[:, t, :], lg[:, t, :]))
            step.wait()
            for t in range(NT):
                step(V.max_index(top_i[:, t, :], top[:, t, :], lg[:, t, :]))
            step.wait()
            step(V.tensor_copy(rt[:, :, 24:26], top_i[:, :, 0:2]))
            V.tensor_tensor(rt[:, :, 41:42], top[:, :, 1:2], top[:, :, 0:1], ALU.subtract).then_inc(gap_ready, 1)
            step.wait()
            for t in range(NT):
                for i in range(2):
                    step(V.tensor_scalar(rt[:, t, 8 * i:8 * i + 8], iota(E), rt[:, t, 24 + i:25 + i], None, ALU.is_equal))
            step.wait()
            V.tensor_tensor(rt[:, :, 16:24], rt[:, :, 0:8], rt[:, :, 8:16], ALU.add).then_inc(member_ready, 1)
            dve.wait_ge(gap_exp, 1)
            chained(V.tensor_scalar(rt[:, :, 42:43], rt[:, :, 40:41], 1.0, None, ALU.add))
            chained(V.reciprocal(rt[:, :, 43:44], rt[:, :, 42:43]))
            chained(V.tensor_tensor(rt[:, :, 44:45], rt[:, :, 40:41], rt[:, :, 43:44], ALU.mult))
            for t in range(NT):
                chained(V.tensor_scalar(comb[:, t, 0:E], rt[:, t, 0:8], rt[:, t, 43:44], None, ALU.mult))
                chained(V.scalar_tensor_tensor(comb[:, t, 0:E], rt[:, t, 8:16], rt[:, t, 44:45], comb[:, t, 0:E], ALU.mult, ALU.add))
            dve.wait_ge(pos_done, 1)
            dve.wait_ge(member_ready, 1)
            for t in range(NT):
                chained(V.scalar_tensor_tensor(possel[:, t, 0:E], ps[5][:, t * E:(t + 1) * E], 1.0, rt[:, t, 16:24], ALU.add, ALU.mult))
            chained(V.tensor_scalar(possel[:, :, 0:E], possel[:, :, 0:E], -1.0, None, ALU.add))
            cnt, rnd, over = jobs[:, 0:E], jobs[:, E:2 * E], jobs[:, 2 * E:3 * E]
            chained(V.tensor_copy(cnt, ps[5][:, 2 * E:3 * E]))
            chained(V.tensor_scalar(over, cnt, OVER + 0.5, None, ALU.is_gt))
            chained(V.tensor_tensor_scan(rnd, ones[:, 0:E], over, 0.0, ALU.mult, ALU.add))
            step(V.tensor_copy(job_tab[:, 0:E], cnt))
            step(V.tensor_copy(job_tab[:, 2 * E:2 * E + 1], rnd[:, E - 1:E]))
            step.wait()
            chained(V.tensor_tensor(rnd, rnd, over, ALU.subtract))
            chained(V.tensor_scalar(rnd, rnd, float(E), None, ALU.add))
            V.tensor_copy(job_tab[:, E:2 * E], rnd).then_inc(tables_ready, 1)
            for t in range(NT):
                step(V.tensor_copy(info[:, t, 0:1], cst[:, C_TOK + t:C_TOK + t + 1]))

            UF = FB * NT

            def select(e, g, rnd_):
                step.wait()
                for t in range(NT):
                    step(V.tensor_scalar(cur[:, t, 0:1], possel[:, t, bass.ds(e, 1)], float(-P * rnd_), None, ALU.add))
                    step(V.tensor_copy(info[:, t, 1:2], comb[:, t, bass.ds(e, 1)]))
                step.wait()
                for t in range(NT):
                    w = V.tensor_scalar(sel[:, t, :], iota(P), cur[:, t, 0:1], None, ALU.is_equal)
                    if t == 0:
                        step(w)
                w.then_inc(sel_ready, 1)

            def slots_in(g):
                for k in range(4, KD):
                    dve.wait_ge(gather_done, g * 2 + (k // 4 + 1))
                    V.tensor_scalar(ueT[:, k, :], ps[6 + k // 4][:, (k % 4) * P:(k % 4 + 1) * P], mod_a[:, 1, k:k + 1],
                                    mod_b[:, 1, k:k + 1], ALU.mult, ALU.add).then_inc(ueT_ready, 1)

            def back(g, job):
                dve.wait_ge(info_done, g + 1)
                chained(V.tensor_copy(slot_info, ps[3][:, 0:2]))
                V.tensor_scalar(selT, iota(S), slot_info[:, 0:1], slot_info[:, 1:2], ALU.is_equal,
                                ALU.mult).then_inc(selT_ready, 1)

            def expert(job, e_next, g, gather_next):
                for b in range(MB):
                    mids(job * MB + (UF + b), 512)
                    if b == 0:
                        back(g, job)
                        if gather_next:
                            select(e_next, g + 1, 0)
                if gather_next:
                    slots_in(g + 1)
                for i in range(4):
                    t, half = i // 2, i % 2
                    dve.wait_ge(scatter_done, job * 4 + (i + 1))
                    y = y_acc[:, t, half * 512:(half + 1) * 512]
                    V.tensor_tensor(y, y, ps[6 + i % 2][:, :], ALU.add).then_inc(scatter_added, 1)

            select(0, 0, 0)
            slots_in(0)
            dve.wait_ge(y_zeroed, 1)
            with dve.Fori(0, E) as e:
                step.enter(e, 0, 6)
                expert(e, e + 1, e, True)
            step.leave(0, E)
            n_over = dve.value_load(job_tab[0:1, 2 * E:2 * E + 1], min_val=0, max_val=E)
            with dve.If(n_over > 0):
                with dve.Fori(0, E) as e:
                    n_e = dve.value_load(job_tab[0:1, bass.ds(e, 1)], min_val=0, max_val=S)
                    with dve.If(n_e > OVER):
                        job = dve.value_load(job_tab[0:1, bass.ds(e + E, 1)], min_val=E, max_val=2 * E)
                        step.enter(job, E, 6)
                        select(e, job + 1, 1)
                        slots_in(job + 1)
                        expert(job, None, job + 1, False)
            step.sem, step.n, step.reg = final_steps, 0, None
            dve.wait_ge(scatter_added, n_over * 4 + 4 * E)
            residual(0, 1, 0, lambda n, t: y_acc[:, t, n * 512:(n + 1) * 512])

            dve.wait_ge(rms_ready, 6)
            V.reciprocal(stat[:, 4:6], stat[:, 2:4]).then_inc(stat_ready, 1)
            dve.wait_ge(stat_ready, 1)
            dve.wait_ge(late_in, 16 * 8)
            for t in range(NT):
                V.scalar_tensor_tensor(final_y[:, t, :], h[:, t, :], stat[:, 4 + t:5 + t], gate_row[:, 0, :],
                                       ALU.mult, ALU.mult).then_inc(y_final, 1)


_INS = ["x", "c", "w_ada", "b_ada", "g_mix", "g_ffn", "g_final", "e_w_in", "e_w_out", "s5_a_re", "s5_a_im",
        "s5_log_dt", "s5_b_re", "s5_b_im", "s5_c_re", "s5_c_im", "s5_d", "s5_w_glu", "s5_b_glu",
        "ff_w_gate", "ff_w_up", "ff_w_down", "o_w_in", "o_w_out", "mla_g_kv", "mla_w_uk", "mla_w_uv",
        "moe_w_router", "moe_b_router", "moe_w_gate", "moe_w_up", "moe_w_down"]


def kernel(**inputs):
    import concourse.bacc as bacc
    from concourse.bass_utils import run_bass_kernel_spmd as run

    nc = bacc.Bacc("TRN2", target_bir_lowering=False, num_devices=1)
    arrays, aps = {}, {}
    for name in _INS:
        a = np.ascontiguousarray(inputs[name])
        arrays[f"in_{name}"] = a
        aps[name] = nc.dram_tensor(f"in_{name}", a.shape, mybir.dt.from_np(a.dtype), kind="ExternalInput").ap()
    consts = constants()
    arrays["in_consts"] = consts
    aps["consts"] = nc.dram_tensor("in_consts", consts.shape, F32, kind="ExternalInput").ap()
    out = nc.dram_tensor("out_0", (1, S, D), F32, kind="ExternalOutput").ap()
    trunk(nc, aps, out)
    r = run(nc, [arrays], core_ids=[0])
    return r.results[0]["out_0"]
```

```python
import numpy as np
from contextlib import ExitStack

import concourse.bass as bass
from concourse import mybir

F32 = mybir.dt.float32
F32R = mybir.dt.float32r
U32 = mybir.dt.uint32
I32 = mybir.dt.int32
ALU = mybir.AluOpType
ACT = mybir.ActivationFunctionType
AX = mybir.AxisListType

P = 128
D = 1024
S = 256
NT = S // P
KD = D // P
EPS = 1e-6
HD = 64
ROPE = HD // 4
HALF = ROPE // 2
SC = HD ** -0.5
A_HEADS = 8
A_W = A_HEADS * HD
G_S5, P_S5, C_S5 = 32, 64, 16
NCH = G_S5 * P_S5 // P
C_HEADS = 16
NOPE = HD - ROPE
LAT = D // 4
IH = 8
TOPK = min(256, S // 4)
FF = 2816
FB = 8
FW = FF // FB
FT = [(0, P), (P, P), (2 * P, FW - 2 * P)]
E = 8
FE = 3584
MB = FE // 512
SLOT = 4096
CHUNK, NB = 1024, 4
NCI = 4
NS0, NS1 = 5, 7
ADA0, ADA1 = 512, 384
NA0, NA1 = 6 * D // ADA0, 6 * D // ADA1
KEYS = [P, 2 * P]
KOFF = [0, P]
KW = sum(KEYS)
BIG = 1e30
NEG = -3e38
ROUND = 12582912.0
PI = 3.1415925
OVER = P
TWO_PI = (6.28125, 0.0019353071693331, 1.0253131677018246e-11)

C_ID, C_ONE, C_TRI = 0, P, 2 * P
C_IOTA = 3 * P
C_CNT = C_IOTA + S
C_NEG = C_CNT + KW
C_CAU = C_NEG + KW
C_CB = C_CAU + KW
C_COS = C_CB + KW
C_SIN = C_COS + NT * HALF
C_HM = C_SIN + NT * HALF
C_TOK = C_HM + 2
NC = C_TOK + 2


def constants():
    c = np.zeros((P, NC), np.float32)
    p = np.arange(P)
    c[:, C_ID:C_ID + P] = np.eye(P)
    c[:, C_ONE:C_ONE + P] = 1
    c[:, C_TRI:C_TRI + P] = p[:, None] < p[None, :]
    c[:, C_IOTA:C_IOTA + S] = np.arange(S)
    for t in range(NT):
        d = (t * P + p)[:, None] - np.arange(KEYS[t])[None, :]
        n = (d >= 0) * ((d <= 128) * 1 + (d % 4 == 0) * 1 + (d % 16 == 0) * 1)
        a, b = KOFF[t], KOFF[t] + KEYS[t]
        c[:, C_CNT + a:C_CNT + b] = n
        c[:, C_NEG + a:C_NEG + b] = np.where(n == 0, -BIG, 0)
        c[:, C_CAU + a:C_CAU + b] = d >= 0
        c[:, C_CB + a:C_CB + b] = np.where(d >= 0, 0, NEG)
        inv = np.float32(500000.0) ** (-np.arange(0, ROPE, 2, dtype=np.float32) / np.float32(ROPE))
        ang = (t * P + p).astype(np.float32)[:, None] * inv.astype(np.float32)[None, :]
        c[:, C_COS + t * HALF:C_COS + (t + 1) * HALF] = np.cos(ang.astype(np.float64))
        c[:, C_SIN + t * HALF:C_SIN + (t + 1) * HALF] = np.sin(ang.astype(np.float64))
        c[:, C_TOK + t] = t * P + p
        c[:, C_HM + t] = (p // C_S5) % 2 == t
    return c


class Places:

    def __init__(self, nc, base, size):
        self.nc, self.base, self.size = nc, base, size

    def at(self, name, offset, shape, dt=F32):
        assert offset + int(np.prod(shape[1:])) <= self.size, name
        return self.nc.alloc_sbuf_tensor_at(name, shape, dt, offset=self.base + 4 * offset)


class Steps:

    def __init__(self, eng, sem):
        self.eng, self.sem, self.n = eng, sem, 0

        self.reg, self.per, self.at = None, 0, 0

    def __call__(self, ins):
        ins.then_inc(self.sem, 1)
        self.n += 1
        return ins

    def wait(self):
        if self.reg is None:
            self.eng.wait_ge(self.sem, self.n)
        else:
            self.eng.wait_ge(self.sem, self.reg * self.per + self.n)

    def enter(self, reg, first, per):
        self.reg, self.per, self.at = reg, per, self.n
        self.n -= first * per

    def leave(self, first, turns):
        assert self.n + first * self.per == self.at + self.per, (self.n, self.at, self.per)
        self.n = self.at + turns * self.per
        self.reg = None


def trunk(nc, A, out):
    ctx = ExitStack()
    with ctx:
        def sb(name, shape, dt=F32):
            return ctx.enter_context(nc.sbuf_tensor(name, shape, dt))

        def sem(name):
            return ctx.enter_context(nc.semaphore(name))

        cst = sb("cst", [P, NC])
        h = sb("h", [P, NT, D])
        gate_row = sb("gate_row", [P, 2, D])
        ring = sb("ring", [P, NS0, SLOT])
        c_col = sb("c_col", [P, KD])
        g_col = sb("g_col", [P, 4, KD])
        b_col = sb("b_col", [P, 4, KD])
        mod_a = sb("mod_a", [P, 2, KD])
        mod_b = sb("mod_b", [P, 2, KD])
        stat = sb("stat", [P, 24])
        eps = sb("eps", [P, 1])
        s5_d = sb("s5_d", [P, 4])
        s5_bg = sb("s5_bg", [P, 4])
        w_r = sb("w_r", [P, KD, E])
        b_r = sb("b_r", [P, E])
        g_kv = sb("g_kv", [P, 2])
        top_i = sb("top_i", [P, NT, E], U32)
        job_tab = sb("job_tab", [P, 3 * E], I32)
        AT_UT, AT_ADA, AT_WIDE, AT_WORK = 0, KD * S, KD * S + 6 * D, KD * S + 6 * D + 2 * SLOT
        WORK = 9600
        base = (nc.sbuf_base + 31) // 32 * 32
        arena = sb("arena", [P, AT_WORK + WORK])
        at = Places(nc, base, AT_WORK + WORK).at
        uT = at("uT", AT_UT, [P, KD, S])
        ada = at("ada", AT_ADA, [P, 6 * D])
        phase_buf = at("phase_buf", AT_WIDE, [P, 2, SLOT])
        work = at("work", AT_WORK, [P, WORK])
        ring_more = at("ring_more", AT_UT, [P, NS1 - NS0, SLOT])
        w_hi = at("w_hi", AT_WIDE, [P, NB, CHUNK], F32R)
        w_lo = at("w_lo", AT_WIDE + NB * CHUNK, [P, NB, CHUNK], F32R)
        ps = [ctx.enter_context(nc.psum_tensor(f"ps{i}", [P, 512], F32)) for i in range(8)]

        ident = cst[:, C_ID:C_ID + P]
        ones = cst[:, C_ONE:C_ONE + P]
        tri = cst[:, C_TRI:C_TRI + P]

        def iota(n):
            return cst[:, C_IOTA:C_IOTA + n]

        def cos(t, heads):
            return cst[:, C_COS + t * HALF:C_COS + (t + 1) * HALF].unsqueeze(1).broadcast_to([P, heads, HALF])

        def sin(t, heads):
            return cst[:, C_SIN + t * HALF:C_SIN + (t + 1) * HALF].unsqueeze(1).broadcast_to([P, heads, HALF])

        class Region:

            def __init__(self, buf, size, at=0):
                self.buf, self.size, self.at = buf, size, at

            def take(self, *shape):
                n = int(np.prod(shape))
                a = self.buf[:, self.at:self.at + n]
                self.at += n
                assert self.at <= self.size, self.at
                if len(shape) == 1:
                    return a
                names = "abcd"[:len(shape)]
                return a.rearrange(f"p ({' '.join(names)}) -> p {' '.join(names)}",
                                   **{x: s for x, s in zip(names, shape)})

        flat_uT = uT[:, :, :].rearrange("p a b -> p (a b)")
        rope_buf = work[:, WORK - 256:WORK].rearrange("p (a h d) -> p a h d", a=2, h=C_HEADS)
        W0 = Region(work, WORK - 256)
        hn = W0.take(NT, D)
        qk_tok = hn
        s5_y = W0.take(4, S)
        s5_p = W0.take(24, NCH)
        s5_bT = W0.take(2, 4, P)
        s5_cT = W0.take(3, 4, P)
        s5_tmp = W0.take(NCH, P)
        s5_v = W0.take(2, S)
        s5_small = W0.take(10)
        s5_rb = W0.take(192)
        WA = Region(ada, 6 * D)
        qT = WA.take(4, S)
        kT = WA.take(4, S)
        v_tok = WA.take(NT, A_W)
        s_inT = WA.take(4, S)
        catT = WA.take(KD, S)
        tmp_flat = s5_tmp.rearrange("p a b -> p (a b)")
        rotA = tmp_flat[:, 0:512].rearrange("p (a b) -> p a b", a=2)
        rotB = tmp_flat[:, 512:1024].rearrange("p (a b) -> p a b", a=2)
        zbuf = tmp_flat[:, 1024:2048].rearrange("p (n a b) -> p n a b", n=2, a=2)
        post = hn.rearrange("p t (n a b) -> p t n a b", n=2, a=2)
        WU = Region(flat_uT, KD * S)
        sm = WU.take(2, KW)
        pT = WU.take(2, KW)
        phase = phase_buf[:, :, :].rearrange("p a (b c) -> p a b c", b=NCH)

        b_in = flat_uT[:, 0:512].rearrange("p (a b c) -> p a b c", a=2, b=NCH)
        c_in = flat_uT[:, 512:1024].rearrange("p (a b c) -> p a b c", a=2, b=4)
        b_pad = flat_uT[:, 1024:2048].rearrange("p (a b c) -> p a b c", a=2, b=4)
        c_pad = hn.rearrange("p t (b c) -> p t b c", b=8)

        (LR, LI, LDT, DT, X1, ANG, MAG, KK, TT, RR, RH, SN, SH, CS, AR, AI, NR, DEN, RDEN, FR, FI,
         ER, EI, T2) = range(24)

        consts_in = sem("consts_in")
        x_in = sem("x_in")
        vec_in = sem("vec_in")
        s5_in = sem("s5_in")
        bias_in = sem("bias_in")
        late_in = sem("late_in")
        fill = [sem(f"slot{i}_filled") for i in range(NS1)]
        weights_used = sem("weights_used")
        ada_used = sem("ada_used")
        hi_ready, lo_ready, chunk_done = sem("hi_ready"), sem("lo_ready"), sem("chunk_done")
        dve_steps, act_steps, pool_steps = sem("dve_steps"), sem("act_steps"), sem("pool_steps")
        c_ready = sem("c_ready")
        ada_zeroed = sem("ada_zeroed")
        mod_summed = sem("mod_summed")
        mod_ready = sem("mod_ready")
        gate_ready = sem("gate_ready")
        h_ready = sem("h_ready")
        rms_ready = sem("rms_ready")
        hn_ready = sem("hn_ready")
        hnT_done = sem("hnT_done")
        uT_ready = sem("uT_ready")
        mix_out_done = sem("mix_out_done")
        out_stored = sem("out_stored")

        tables_ready = sem("tables_ready")
        y_final = sem("y_final")
        ckv_ready = sem("ckv_ready")
        ckvT_done = sem("ckvT_done")
        ckvT_ready = sem("ckvT_ready")
        kv_done = sem("kv_done")
        kn_ready = sem("kn_ready")
        v_ready = sem("v_ready")
        idxT_done = sem("idxT_done")
        idxT_ready = sem("idxT_ready")
        logit_done = sem("logit_done")
        relu_ready = sem("relu_ready")
        score_added = sem("score_added")
        mask_ready = sem("mask_ready")
        router_done = sem("router_done")
        gap_ready = sem("gap_ready")
        gap_exp = sem("gap_exp")
        member_ready = sem("member_ready")
        pos_done = sem("pos_done")
        sel_ready = sem("sel_ready")
        gather_done = sem("gather_done")
        info_done = sem("info_done")
        x_e_ready = sem("x_e_ready")
        e_hi_ready = sem("e_hi_ready")
        e_ready = sem("e_ready")
        x_hi_ready = sem("x_hi_ready")
        x_ready = sem("x_ready")
        midT_hi_ready = sem("midT_hi_ready")
        small_in = sem("small_in")
        experts_done = sem("experts_done")
        selT_ready = sem("selT_ready")
        y_sb_ready = sem("y_sb_ready")
        scatter_done = sem("scatter_done")
        scatter_added = sem("scatter_added")
        eps_ready = sem("eps_ready")
        final_steps = sem("final_steps")
        stat_ready = sem("stat_ready")

        W1 = Region(work, WORK - 256)
        q_tok = W1.take(NT, C_HEADS, HD)
        ctxT = q_tok.rearrange("p t h d -> p (t h d)").rearrange("p (k s) -> p k s", k=KD)
        AT_X = AT_WORK + W1.at
        kcat = W1.take(NT, C_HEADS, HD)
        ckvT = W1.take(2, S)
        qiT = W1.take(4, S)
        kiT = W1.take(S)
        score = W1.take(KW)
        assert W1.at >= NT * D + 2 * KD * S
        x_hi = at("x_hi", AT_X, [P, KD, S], F32R)
        x_lo = at("x_lo", AT_X + KD * S, [P, KD, S], F32R)
        ckr = W1.take(NT, LAT + ROPE)
        q_i = W1.take(NT, IH, HD)
        k_iw = W1.take(NT, 2 * HD + IH)
        selneg = W1.take(KW)
        kr_t = W1.take(ROPE)
        top8 = W1.take(NT, 8)
        WA1 = Region(ada, 6 * D)
        qT1 = WA1.take(8, S)
        kT1 = WA1.take(8, S)
        v1 = WA1.take(NT, D)
        W2 = Region(work, WORK, NT * D + 2 * KD * S)
        mid = W2.take(NT, FW)
        AT_M = AT_WORK + W2.at
        mT_hi = at("mT_hi", AT_M, [P, NT, 3, P], F32R)
        mT_lo = at("mT_lo", AT_M + NT * 3 * P, [P, NT, 3, P], F32R)
        assert W2.at + 2 * NT * 3 * P <= WORK
        W3 = Region(work, WORK, NT * D)
        e_hi = at("e_hi", AT_WORK + W3.at, [P, KD, P], F32R)
        e_lo = at("e_lo", AT_WORK + W3.at + KD * P, [P, KD, P], F32R)
        W3.take(2 * KD * P)
        eT_hi = at("eT_hi", AT_WORK + W3.at, [P, 4, P], F32R)
        eT_lo = at("eT_lo", AT_WORK + W3.at + 4 * P, [P, 4, P], F32R)
        W3.take(2 * 4 * P)
        x_e = W3.take(KD, P)
        y_sb = W3.take(D)
        mid_e = W3.take(512)
        sel = W3.take(NT, P)
        selT = W3.take(S)
        info = W3.take(NT, 2)
        slot_info = W3.take(2)
        cur = W3.take(NT, 2)
        lg = W3.take(NT, E)
        top = W3.take(NT, E)
        rt = W3.take(NT, 48)
        possel = W3.take(NT, E + 1)
        comb = W3.take(NT, E + 1)
        jobs = W3.take(3 * E)
        final_y = hn

        w_ada, b_ada = A["w_ada"], A["b_ada"]
        kp = lambda ap: ap.rearrange("(k p) n -> p k n", p=P)
        stream = []
        fills = [0] * NS1
        users = {"weights": 0, "ada": 0, "split": 0}
        last = [None] * NS1

        def slot_ap(s):
            return ring[:, s, :] if s < NS0 else ring_more[:, s - NS0, :]

        def push(slot, pieces, user):
            before = last[slot]
            fills[slot] += 16 * len(pieces)
            chunks = users["split"]
            users[user] += NCI if user == "split" else 1
            last[slot] = (user, users[user])
            stream.append((slot, pieces, before))
            return slot, fills[slot], chunks

        def block_ap(slot, k, n):
            return slot_ap(slot)[:, 0:k * n].rearrange("p (k n) -> p k n", k=k)

        n_item = [0]

        def item(srcs, k, n, user):
            s = n_item[0] % NS0
            n_item[0] += 1
            got = push(s, [(block_ap(s, k, n), kp(srcs))], user)
            return (block_ap(s, k, n), got)

        def ada_items(sections):
            return [(sec, half, item(w_ada[0, :, sec * D + half * 512:sec * D + (half + 1) * 512], KD, 512, "weights"))
                    for sec in sections for half in range(2)]

        ada_first = ada_items((0, 1))
        e_in = [item(A["e_w_in"][0, :, i * 512:(i + 1) * 512], KD, 512, "weights") for i in range(4)]
        ada_rest = ada_items((3, 4, 2, 5))
        glu_w = item(A["s5_w_glu"][0], 4, 512, "weights")
        e_out = [item(A["e_w_out"][0, :, i * 512:(i + 1) * 512], KD, 512, "weights") for i in range(2)]

        def ff_pieces(kind, b, slot):
            if kind in ("gate", "up"):
                return [(block_ap(slot, KD, FW), kp(A["ff_w_" + kind][0])[:, :, bass.ds(b * FW, FW)])]
            if kind == "down":
                dst = block_ap(slot, 3, D)
                rows = A["ff_w_down"][0, bass.ds(b * FW, FW), :]
                return [(dst[:, 0:2, :], rows[0:2 * P, :].rearrange("(k p) n -> p k n", p=P)),
                        (dst[0:FW - 2 * P, 2, :], rows[2 * P:FW, :])]
            i = b * 2 + int(kind[-1])
            return [(block_ap(slot, KD, ADA1), kp(w_ada[1])[:, :, bass.ds(i * ADA1, ADA1)])]

        def ff_user(kind):
            return "ada" if kind.startswith("ada") else "split"

        def ff_static(kinds, b):
            got = {}
            for kind in kinds:
                s = n_item[0] % NS0
                n_item[0] += 1
                got[kind] = push(s, ff_pieces(kind, b, s), ff_user(kind))
            return got

        ff_first = ff_static(("gate", "up", "ada0", "ada1"), 0)
        static_before = list(stream)
        FFK = ("gate", "down", "up", "ada0", "ada1")
        ff_slot = {k: (n_item[0] + j) % NS0 for j, k in enumerate(FFK)}
        ff_inc = {k: 32 if k == "down" else 16 for k in FFK}
        ff_fill1 = {k: fills[ff_slot[k]] for k in FFK}
        ff_last1 = {k: last[ff_slot[k]] for k in FFK}
        ff_chunks1, ff_ada1 = users["split"], users["ada"]
        ff_chunk = {k: NCI * j for j, k in enumerate(("gate", "down", "up"))}
        CB = 3 * NCI
        for k in FFK:
            fills[ff_slot[k]] += ff_inc[k] * (FB - 1)
        users["split"] += CB * (FB - 1)
        users["ada"] += 2 * (FB - 1)
        n_item[0] += 5 * (FB - 1)
        for k in FFK:
            last[ff_slot[k]] = (("ada", users["ada"] - 1 + int(k[-1])) if k.startswith("ada")
                                else ("split", users["split"] - CB + ff_chunk[k] + NCI))
        stream.clear()
        ff_last = ff_static(("down",), FB - 1)
        o_cols = [(0, 256), (256, 384), (640, 384), (1024, 272), (1296, 512), (1808, 72)]
        o_in = [item(A["o_w_in"][0, :, a:a + n], KD, n, "split") for a, n in o_cols]
        s = n_item[0] % NS0
        n_item[0] += 1
        uk_ap = slot_ap(s)[:, 0:2 * 768].rearrange("p (k n) -> p k n", k=2)
        uv_ap = slot_ap(s)[:, 2 * 768:2 * 1792].rearrange("p (k n) -> p k n", k=2)
        ukv = push(s, [(uk_ap, A["mla_w_uk"][0].rearrange("(k p) a b -> p k (a b)", p=P)),
                       (uv_ap, A["mla_w_uv"][0].rearrange("(k p) a b -> p k (a b)", p=P))], "weights")
        o_out = [item(A["o_w_out"][0, :, i * 512:(i + 1) * 512], KD, 512, "weights") for i in range(2)]
        static_after = list(stream)
        moe_last0 = list(last)
        moe_c0 = users["split"]
        moe_fill0 = list(fills)
        moe_items = [("gate", 0), ("up", 0)]
        for b in range(1, MB):
            moe_items += [("gate", b), ("up", b), ("down", b - 1)]
        moe_items += [("down", MB - 1)]
        NI = len(moe_items)
        assert NI % NS1 == 0
        PER = NI // NS1
        CE = NCI * NI
        moe_at = {it: i for i, it in enumerate(moe_items)}

        def ff_chunk_of(n):
            return lambda slot, c: (slot_ap(slot)[:, 2 * c * n:(2 * c + 2) * n], P)

        def ff_down_chunk(slot, c):
            if c < 2:
                return slot_ap(slot)[:, c * D:(c + 1) * D], P
            n = FT[2][1]
            return slot_ap(slot)[0:n, 2 * D + (c - 2) * 512:2 * D + (c - 1) * 512], n

        def moe_chunk(slot, c):
            return slot_ap(slot)[:, c * CHUNK:(c + 1) * CHUNK], P

        used = {"weights": weights_used, "ada": ada_used, "split": lo_ready}

        block = ctx.enter_context(nc.Block())
        x_tok = A["x"].rearrange("o (t p) d -> p (o t) d", p=P)
        out_tok = out.rearrange("o (t p) d -> p (o t) d", p=P)

        s5_dt = sem("s5_dt")
        s5_x = sem("s5_x")
        s5_mag = sem("s5_mag")
        s5_r = sem("s5_r")
        s5_sin = sem("s5_sin")
        s5_den = sem("s5_den")
        s5_rden = sem("s5_rden")
        s5_pads = sem("s5_pads")
        s5_padT = sem("s5_padT")
        s5_wT_ready = sem("s5_wT_ready")
        phase_ready = sem("phase_ready")
        bu_done = sem("bu_done")
        bu_used = sem("bu_used")
        z_ready = sem("z_ready")
        post_ready = sem("post_ready")
        y_part_done = sem("y_part_done")
        y_pre = sem("y_pre")
        y_ready = sem("y_ready")
        glu_done = sem("glu_done")
        glu_tanh = sem("glu_tanh")
        proj_done = sem("proj_done")
        rope_done = sem("rope_done")
        nope_done = sem("nope_done")
        vs_ready = sem("vs_ready")
        qkT_done = sem("qkT_done")
        qkT_ready = sem("qkT_ready")
        score_done = sem("score_done")
        max_ready = sem("max_ready")
        exp_ready = sem("exp_ready")
        p_ready = sem("p_ready")
        pT_done = sem("pT_done")
        pT_ready = sem("pT_ready")
        o_done = sem("o_done")
        cat_ready = sem("cat_ready")
        gate_done = sem("gate_done")
        silu_done = sem("silu_done")
        up_done = sem("up_done")
        mid_ready = sem("mid_ready")
        midT_done = sem("midT_done")
        midT_ready = sem("midT_ready")
        down_done = sem("down_done")

        @block.sync
        def _(sp):
            def load(entry):
                slot, pieces, before = entry
                if before is not None:
                    sp.wait_ge(used[before[0]], before[1])
                for dst, src in pieces:
                    sp.dma_start(dst, src).then_inc(fill[slot], 16)

            for e in static_before:
                load(e)

            def ff_load(k, b):
                for dst, src in ff_pieces(k, b - 1 if k == "down" else b, ff_slot[k]):
                    sp.dma_start(dst, src).then_inc(fill[ff_slot[k]], 16)

            for k in FFK:
                sp.wait_ge(used[ff_last1[k][0]], ff_last1[k][1])
                ff_load(k, 1)
            with sp.Fori(0, FB - 2) as i:
                for k in FFK:
                    if k.startswith("ada"):
                        sp.wait_ge(ada_used, i * 2 + (ff_ada1 + 1 + int(k[-1])))
                    else:
                        sp.wait_ge(lo_ready, i * CB + (ff_chunks1 + ff_chunk[k] + NCI))
                    ff_load(k, i + 2)
            for e in static_after:
                load(e)

            def moe_load(m, e):
                kind, b = moe_items[m]
                s = m % NS1
                if kind == "down":
                    src = A["moe_w_down"][0, bass.ds(e, 1), b * 512:(b + 1) * 512, :]
                    sp.dma_start(block_ap(s, 4, D), src.rearrange("e (k p) n -> p (e k) n", p=P)).then_inc(fill[s], 16)
                else:
                    src = A["moe_w_" + kind][0, bass.ds(e, 1), :, b * 512:(b + 1) * 512]
                    sp.dma_start(block_ap(s, KD, 512), src.rearrange("e (k p) n -> p (e k) n", p=P)).then_inc(fill[s], 16)

            for m in range(NS0):
                sp.wait_ge(used[moe_last0[m][0]], moe_last0[m][1])
                moe_load(m, 0)
            sp.wait_ge(router_done, 1)
            for m in range(NS0, NS1):
                moe_load(m, 0)

            def moe_wait(m, e):
                sp.wait_ge(lo_ready, e * CE + (moe_c0 + NCI * (m - NS1 + 1)))

            with sp.Fori(0, E - 1) as e:
                for m in range(NS1, NI):
                    moe_wait(m, e)
                    moe_load(m, e)
                for m in range(NS1):
                    moe_wait(NI + m, e)
                    moe_load(m, e + 1)
            for m in range(NS1, NI):
                moe_wait(m, E - 1)
                moe_load(m, E - 1)
            sp.wait_ge(tables_ready, 1)
            with sp.If(sp.value_load(job_tab[0:1, 2 * E:2 * E + 1], min_val=0, max_val=E) > 0):
                with sp.Fori(0, E) as e:
                    n_e = sp.value_load(job_tab[0:1, bass.ds(e, 1)], min_val=0, max_val=S)
                    with sp.If(n_e > OVER):
                        job = sp.value_load(job_tab[0:1, bass.ds(e + E, 1)], min_val=E, max_val=2 * E)
                        for m in range(NI):
                            moe_wait(m, job)
                            moe_load(m, e)
            sp.wait_ge(y_final, 2)
            sp.dma_start(out_tok, final_y).then_inc(out_stored, 16)
            sp.wait_ge(out_stored, 16)

        @block.gpsimd
        def _(pool):
            step = Steps(pool, pool_steps)
            par = lambda i: s5_p[:, i, :]

            def mul(o, a, b):
                step.wait()
                return step(nc.gpsimd.tensor_tensor(o, a, b, ALU.mult))

            def add(o, a, b):
                step.wait()
                return step(nc.gpsimd.tensor_tensor(o, a, b, ALU.add))

            def sub(o, a, b):
                step.wait()
                return step(nc.gpsimd.tensor_tensor(o, a, b, ALU.subtract))

            def affine(o, a, m, b):
                step.wait()
                return step(nc.gpsimd.tensor_scalar(o, a, m, b, ALU.mult, ALU.add))

            st = lambda a: a.rearrange("o (j g) p -> (g p) (o j)", g=2)
            with nc.allow_non_contiguous_dma(reason="small parameters"):
                pool.dma_start(par(LR), st(A["s5_a_re"])).then_inc(s5_in, 16)
                pool.dma_start(par(LI), st(A["s5_a_im"])).then_inc(s5_in, 16)
                for g in range(2):
                    pool.dma_start(s5_p[g * P_S5:(g + 1) * P_S5, LDT, :],
                                   A["s5_log_dt"].rearrange("o (j g) -> g (o j)", g=2)[g:g + 1, :]
                                   .broadcast_to([P_S5, NCH])).then_inc(s5_in, 16)
                pool.dma_start(s5_d[:, :], A["s5_d"].rearrange("o (t g) c -> (g c) (o t)", t=4)).then_inc(s5_in, 16)
                pool.dma_start(s5_bg[:, :], A["s5_b_glu"].rearrange("o (t p) -> p (o t)", p=P)).then_inc(s5_in, 16)
                for i, n in enumerate(("re", "im")):
                    pool.dma_start(b_in[:, i, :, :], A["s5_b_" + n].rearrange("o (j g) p c -> (g p) (o j) c", g=2)).then_inc(s5_in, 16)
                    pool.dma_start(c_in[:, i, :, :], A["s5_c_" + n].rearrange("o (t g) c p -> (g c) (o t) p", t=4)).then_inc(s5_in, 16)
                pool.dma_start(w_r[:, :, :], A["moe_w_router"][0].rearrange("(k p) e -> p k e", p=P)).then_inc(late_in, 16)
                pool.dma_start(b_r[:, :], A["moe_b_router"].broadcast_to([P, E])).then_inc(late_in, 16)
            pool.wait_ge(s5_in, 16 * 10)
            pool.wait_ge(s5_dt, 1)
            step(nc.gpsimd.tensor_tensor(par(X1), par(LR), par(DT), ALU.mult))
            step.wait()
            nc.gpsimd.tensor_tensor(par(ANG), par(LI), par(DT), ALU.mult).then_inc(s5_x, 1)
            pool.wait_ge(s5_x, 1)
            affine(par(KK), par(ANG), 1 / (2 * np.pi), ROUND)
            affine(par(KK), par(KK), 1.0, -ROUND)
            sub(par(RR), par(ANG), par(ANG))
            add(par(RR), par(RR), par(ANG))
            for c in TWO_PI:
                affine(par(TT), par(KK), c, 0.0)
                sub(par(RR), par(RR), par(TT))
            step.wait()
            step(nc.gpsimd.tensor_scalar(par(RR), par(RR), PI, -PI, ALU.min, ALU.max))
            step.wait()
            nc.gpsimd.tensor_scalar(par(RH), par(RR), 0.5, 0.0, ALU.mult, ALU.add).then_inc(s5_r, 1)
            mul(par(DEN), par(LR), par(LR))
            mul(par(T2), par(LI), par(LI))
            step.wait()
            nc.gpsimd.tensor_tensor(par(DEN), par(DEN), par(T2), ALU.add).then_inc(s5_den, 1)
            pool.wait_ge(s5_sin, 1)
            pool.wait_ge(s5_r, 1)
            pool.wait_ge(s5_den, 1)
            mul(par(TT), par(SH), par(SH))
            affine(par(CS), par(TT), -2.0, 1.0)
            pool.wait_ge(s5_mag, 1)
            mul(par(AR), par(MAG), par(CS))
            mul(par(AI), par(MAG), par(SN))
            affine(par(NR), par(AR), 1.0, -1.0)
            pool.wait_ge(s5_rden, 1)
            for o, a, b, c, d, last_op in ((FR, NR, LR, AI, LI, add), (FI, AI, LR, NR, LI, sub)):
                mul(par(TT), par(a), par(b))
                mul(par(T2), par(c), par(d))
                last_op(par(o), par(TT), par(T2))
                mul(par(o), par(o), par(RDEN))
            step.wait()
            step(pool.memset(b_pad, 0.0))
            for g in range(2):
                rows = slice(g * P_S5, (g + 1) * P_S5)
                f = lambda i: s5_p[rows, i, :].unsqueeze(2).broadcast_to([P_S5, NCH, C_S5])
                b = lambda i: b_in[rows, i, :, :]
                o = lambda i: b_pad[rows, i, :, :].rearrange("p t (j x) -> p (t j) x", x=2 * C_S5)[:, :, g * C_S5:(g + 1) * C_S5]
                t = phase[rows, 0, :, 0:C_S5]
                for i, (x, y, op) in enumerate(((0, 1, sub), (1, 0, add))):
                    mul(t, f(FI), b(y))
                    mul(o(i), f(FR), b(x))
                    op(o(i), o(i), t)
            for i in range(2):
                for t in range(4):
                    for g in range(2):
                        step.wait()
                        step(nc.gpsimd.tensor_scalar(c_pad[:, i, t, g * P_S5:(g + 1) * P_S5], c_in[:, i, t, :],
                                                     cst[:, C_HM + g:C_HM + g + 1], 0.0, ALU.mult, ALU.add))
            step.wait()
            nc.gpsimd.tensor_scalar(s5_bg[:, :], s5_bg[:, :], 0.5, 0.0, ALU.mult, ALU.add).then_inc(s5_pads, 1)
            pool.wait_ge(s5_pads, 1)
            step(pool.memset(phase[:, 0, :, 0:1], 1.0))
            step(pool.memset(phase[:, 1, :, 0:1], 0.0))
            affine(par(ER), par(CS), 1.0, 0.0)
            affine(par(EI), par(SN), 1.0, 0.0)
            m = 1
            while m < S:
                er = par(ER).unsqueeze(2).broadcast_to([P, NCH, m])
                ei = par(EI).unsqueeze(2).broadcast_to([P, NCH, m])
                c0, s0 = phase[:, 0, :, 0:m], phase[:, 1, :, 0:m]
                c1, s1 = phase[:, 0, :, m:2 * m], phase[:, 1, :, m:2 * m]
                t = s5_tmp[:, :, 0:m]
                mul(t, s0, ei)
                mul(c1, c0, er)
                sub(c1, c1, t)
                mul(t, c0, ei)
                mul(s1, s0, er)
                add(s1, s1, t)
                mul(par(TT), par(EI), par(EI))
                mul(par(T2), par(ER), par(EI))
                mul(par(ER), par(ER), par(ER))
                sub(par(ER), par(ER), par(TT))
                affine(par(EI), par(T2), 2.0, 0.0)
                m *= 2
            step.wait()
            pool.memset(s5_small[:, 0:1], 0.0).then_inc(phase_ready, 1)
            for j in range(NCH):
                pool.wait_ge(z_ready, j + 1)
                if j >= 2:
                    pool.wait_ge(y_part_done, j - 1)
                z = zbuf[:, j % 2]
                o = post[:, j % 2]
                if j == 0:
                    pool.wait_ge(phase_ready, 1)
                    pool.wait_ge(qkT_done, 4)
                for i in range(2):
                    w = nc.gpsimd.tensor_tensor(o[:, i], z, phase[:, i, j, :].unsqueeze(1).broadcast_to([P, 2, S]), ALU.mult)
                w.then_inc(post_ready, 1)
            pool.wait_ge(h_ready, 4)
            pool.memset(ada[:, :], 0.0).then_inc(ada_zeroed, 1)
            pool.wait_ge(ada_zeroed, 1)
            pool.dma_start(ada[0:1, :], A["b_ada"][1:2, :]).then_inc(bias_in, 16)
            pool.wait_ge(h_ready, 12)
            pool.dma_start(gate_row[:, 0, :], A["g_final"].unsqueeze(0).broadcast_to([P, D])).then_inc(late_in, 16)

        @block.tensor
        def _(pe):
            mm = nc.tensor.matmul
            pending = [False]

            def release(w):
                if pending[0]:
                    w.then_inc(weights_used, 1)
                    pending[0] = False

            def mm3(o, xh, xl, wh, wl, start, stop):
                mm(o, xh, wh, start=start, stop=False)
                mm(o, xh, wl, start=False, stop=False)
                return mm(o, xl, wh, start=False, stop=stop)

            def tr(o, i):
                n = i.shape[0]
                return nc.tensor.transpose(o, i, ident[0:n, 0:n])

            def s5_transposes():
                pe.wait_ge(s5_pads, 1)
                for i in range(2):
                    for t in range(4):
                        w = tr(ps[i][:, t * P:(t + 1) * P], b_pad[:, i, t, :])
                    w.then_inc(s5_padT, 1)
                for i in range(2):
                    for t in range(4):
                        w = tr(ps[2 + i][:, t * P:(t + 1) * P], c_pad[:, i, t, :])
                    w.then_inc(s5_padT, 1)

            def ada_columns(items, bank, at):
                for n, (sec, half, (ap, got)) in enumerate(items):
                    arrived(got)
                    for c in range(4):
                        for k in range(KD):
                            col = at + n * 4 + c
                            w = mm(ps[bank][:, col:col + 1], ap[:, k, c * P:(c + 1) * P], c_col[:, k:k + 1],
                                   start=k == 0, stop=k == KD - 1)
                            if c == 0 and k == 0:
                                release(w)
                    pending[0] = True
                w.then_inc(mod_summed, 1)

            def ada_gate(it, bank):
                sec, half, (ap, got) = it
                arrived(got)
                for k in range(KD):
                    w = mm(ps[bank][:, :], c_col[:, k:k + 1].broadcast_to([P, P]), ap[:, k, :], start=k == 0, stop=k == KD - 1)
                    if k == 0:
                        release(w)
                w.then_inc(mod_summed, 1)
                pending[0] = True

            def mod1():
                pe.wait_ge(ada_used, NA1)
                pe.wait_ge(h_ready, 8)
                for i, sec in enumerate((0, 1, 3, 4)):
                    for k in range(KD):
                        w = mm(ps[4][:, i * KD + k:i * KD + k + 1], ada[:, sec * D + k * P:sec * D + (k + 1) * P],
                               ones[:, 0:1], start=True, stop=True)
                w.then_inc(mod_summed, 1)
                for i, (sec, half, bank) in enumerate(((2, 0, 5), (2, 1, 6), (5, 0, 7), (5, 1, 5))):
                    if i == 3:
                        pe.wait_ge(gate_ready, 5)
                    a = sec * D + half * 512
                    mm(ps[bank][:, :], ones, ada[:, a:a + 512], start=True, stop=True).then_inc(mod_summed, 1)

            def norm(n):
                if n == 0:
                    pe.wait_ge(s5_wT_ready, 5)
                for t in range(NT):
                    pe.wait_ge(hn_ready, NT * n + t + 1)
                    for k in range(KD):
                        c = (k % 2) * S + t * P
                        w = tr(ps[k // 2][:, c:c + P], hn[:, t, k * P:(k + 1) * P])
                        if t == 0 and k == 0:
                            release(w)
                        if t == NT - 1 and k % 2:
                            w.then_inc(hnT_done, 1)

            def arrived(got):
                pe.wait_ge(fill[got[0]], got[1])

            def project(w_item, n, banks, xT, waits=(), last_sem=None):
                ap, got = w_item
                arrived(got)
                for t in range(NT):
                    if waits:
                        pe.wait_ge(*waits[t])
                    for k in range(KD):
                        w = mm(ps[banks[t]][:, 0:n], xT[:, k, t * P:(t + 1) * P], ap[:, k, 0:n],
                               start=k == 0, stop=k == KD - 1)
                        if t == 0 and k == 0 and pending[0]:
                            w.then_inc(weights_used, 1)
                            pending[0] = False
                    w.then_inc(last_sem, 1)
                pending[0] = True

            def scores(n, qT_, kT_, hh):
                r = slice(HD * (hh % 2), HD * (hh % 2) + HD)
                if n >= 2:
                    pe.wait_ge(max_ready, n - 1)
                for t in range(NT):
                    w = mm(ps[n % 2][:, KOFF[t]:KOFF[t] + KEYS[t]], qT_[r, hh // 2, t * P:(t + 1) * P],
                           kT_[r, hh // 2, 0:KEYS[t]], start=True, stop=True)
                    if t == 0:
                        release(w)
                w.then_inc(score_done, 1)

            def probsT(n):
                pe.wait_ge(p_ready, n + 1)
                if n >= 2:
                    pe.wait_ge(pT_ready, n - 1)
                for i in range(3):
                    w = tr(ps[2 + n % 2][:, i * P:(i + 1) * P], sm[:, n % 2, i * P:(i + 1) * P])
                w.then_inc(pT_done, 1)

            def weigh(n, v, hh, cat0):
                pe.wait_ge(pT_ready, n + 1)
                pair = hh // 2
                if pair >= 2 and hh % 2 == 0:
                    pe.wait_ge(cat_ready, cat0 + pair - 1)
                r = slice(HD * (hh % 2), HD * (hh % 2) + HD)
                o = ps[4 + pair % 2]
                p_ = pT[:, n % 2, :]
                hc = slice(hh * HD, (hh + 1) * HD)
                mm(o[r, 0:P], v[:, 0, hc], p_[:, 0:P], start=True, stop=True)
                mm(o[r, P:2 * P], v[:, 0, hc], p_[:, P:2 * P], start=True, stop=False)
                mm(o[r, P:2 * P], v[:, 1, hc], p_[:, 2 * P:3 * P], start=False, stop=True).then_inc(o_done, 1)

            pe.wait_ge(c_ready, 1)
            ada_columns(ada_first, 4, 0)
            pe.wait_ge(consts_in, 16)
            s5_transposes()
            norm(0)
            pe.wait_ge(uT_ready, 8)
            pe.wait_ge(mod_ready, 1)
            project(e_in[0], 512, (4, 5), uT, (), proj_done)
            project(e_in[1], 512, (6, 7), uT, (), proj_done)
            project(e_in[2], 512, (0, 1), uT, (), proj_done)
            ap, got = e_in[3]
            arrived(got)
            for c in range(4):
                for k in range(KD):
                    w = mm(ps[2 + c // 2][:, (c % 2) * S:(c % 2 + 1) * S], ap[:, k, c * P:(c + 1) * P], uT[:, k, :],
                           start=k == 0, stop=k == KD - 1)
                    release(w)
                if c % 2:
                    w.then_inc(proj_done, 1)
            pending[0] = True
            pe.wait_ge(rope_done, 4)
            pe.wait_ge(nope_done, 4)
            for i in range(2):
                for pr in range(4):
                    for t in range(NT):
                        w = tr(ps[4 + 2 * i + pr // 2][:, (pr % 2) * S + t * P:(pr % 2) * S + (t + 1) * P],
                               qk_tok[:, t, i * 512 + pr * P:i * 512 + (pr + 1) * P])
                        release(w)
                    if pr % 2:
                        w.then_inc(qkT_done, 1)
            pe.wait_ge(vs_ready, 4)
            ada_columns(ada_rest[:4], 0, 0)
            for i, bank in enumerate((1, 2, 3, 1)):
                if i == 3:
                    pe.wait_ge(gate_ready, 1)
                ada_gate(ada_rest[4 + i], bank)
            pe.wait_ge(qkT_ready, 4)
            pe.wait_ge(gate_ready, 4)
            pe.wait_ge(mod_ready, 2)

            def drive(j):
                if j == 0:
                    pe.wait_ge(s5_wT_ready, 5)
                else:
                    pe.wait_ge(bu_used, j)
                r = slice(32 * (j % 4), 32 * (j % 4) + 32)
                for i in range(2):
                    w = mm(ps[6][:, i * S:(i + 1) * S], s5_bT[r, i, j // 4, :], s_inT[r, j // 4, :], start=True, stop=True,
                           tile_position=(32 * (j % 4), 0))
                w.then_inc(bu_done, 1)

            def read_out(j):
                pe.wait_ge(post_ready, j + 1)
                t = j // 4
                if j % 4 == 0 and t >= 1:
                    pe.wait_ge(y_pre, t)
                r = slice(32 * (j % 4), 32 * (j % 4) + 32)
                o = ps[7][r, (t % 2) * S:(t % 2 + 1) * S]
                x = post[:, j % 2]
                for i, (c, a, b) in enumerate(((0, 0, 0), (1, 1, 1), (2, 1, 0), (2, 0, 1))):
                    w = mm(o, s5_cT[:, c, t, r], x[:, a, b, :], start=i == 0, stop=i == 3,
                           tile_position=(0, 32 * (j % 4)))
                w.then_inc(y_part_done, 1)

            scores(0, qT, kT, 0)
            for hh in range(A_HEADS):
                if hh + 1 < A_HEADS:
                    scores(hh + 1, qT, kT, hh + 1)
                drive(2 * hh)
                if hh:
                    read_out(2 * hh - 1)
                probsT(hh)
                drive(2 * hh + 1)
                weigh(hh, v_tok, hh, 0)
                read_out(2 * hh)
            read_out(NCH - 1)
            pe.wait_ge(y_ready, 4)
            pe.wait_ge(max_ready, A_HEADS)
            ap, got = glu_w
            arrived(got)
            for c in range(4):
                for k in range(4):
                    w = mm(ps[c // 2][:, (c % 2) * S:(c % 2 + 1) * S], ap[:, k, c * P:(c + 1) * P], s5_y[:, k, :],
                           start=k == 0, stop=k == 3)
                w.then_inc(glu_done, 1)
            pending[0] = True
            pe.wait_ge(cat_ready, 8)
            for n in range(2):
                project(e_out[n], 512, (4 + 2 * n, 5 + 2 * n), catT, (), mix_out_done)

            norm(1)

            def chunk_mm(q, c, outs, xh, xl, ks, rhs, n, first, final, signal=True):
                pe.wait_ge(lo_ready, q + 1)
                for t, o in enumerate(outs):
                    for j, k in enumerate(ks):
                        w = mm3(o, xh(k, t), xl(k, t), rhs(w_hi, c, j), rhs(w_lo, c, j),
                                first and j == 0, final and j == len(ks) - 1)
                w.then_inc(chunk_done, 1)

            def halves(n):
                return lambda buf, c, j: buf[:, c, j * n:(j + 1) * n]

            xh = lambda k, t: x_hi[:, k, t * P:(t + 1) * P]
            xl = lambda k, t: x_lo[:, k, t * P:(t + 1) * P]

            def rows(q, banks, n, chunks, norm_n=None):
                for c in chunks:
                    if norm_n is not None:
                        pe.wait_ge(x_ready, KD * norm_n + 2 * c + 2)
                    chunk_mm(q + c, c, [ps[i][:, 0:n] for i in banks], xh, xl, (2 * c, 2 * c + 1), halves(n), n,
                             c == 0, c == NCI - 1)

            def ff_T(u0):
                for t in range(NT):
                    pe.wait_ge(mid_ready, u0 + t + 1)
                    for i, (a, n) in enumerate(FT):
                        w = tr(ps[2 + t][0:n, i * P:(i + 1) * P], mid[:, t, a:a + n])
                    w.then_inc(midT_done, 1)

            def ff_down(q, u0, first, final):
                pe.wait_ge(midT_ready, u0 + 2)
                for c in range(NCI):
                    i = min(c, 2)
                    n = FT[i][1]
                    pe.wait_ge(lo_ready, q + c + 1)
                    for half in ((0, 1), (0, 1), (0,), (1,))[c]:
                        a = half * 512 if c < 2 else 0
                        for t in range(NT):
                            w = mm3(ps[4 + 2 * t + half][:, :], mT_hi[0:n, t, i, :], mT_lo[0:n, t, i, :],
                                    w_hi[0:n, c, a:a + 512], w_lo[0:n, c, a:a + 512], first and c == 0, final and c >= 2)
                    w.then_inc(chunk_done, 1)

            def ff_block(i, first):
                q = i * CB + ff_chunks1
                u0 = i * NT
                pe.wait_ge(silu_done, u0 + 2)
                rows(q, (0, 1), FW, (0, 1))
                ff_T(u0)
                rows(q, (0, 1), FW, (2, 3))
                ff_down(q + NCI, u0, first, False)
                rows(q + 2 * NCI, (2, 3), FW, range(NCI))

            rows(ff_first["gate"][2], (0, 1), FW, range(NCI), 0)
            rows(ff_first["up"][2], (2, 3), FW, range(NCI))
            ff_block(0, True)
            with pe.Fori(1, FB - 1) as i:
                ff_block(i, False)
            ff_T((FB - 1) * NT)
            ff_down(ff_last["down"][2], (FB - 1) * NT, False, True)

            mod1()
            norm(2)
            pe.wait_ge(mod_ready, 3)
            pe.wait_ge(gate_ready, 8)
            for j, banks in enumerate(((0, 1), (2, 3), (4, 5), (6, 7), (0, 1), (2, 3))):
                if j == 4:
                    pe.wait_ge(rope_done, 6)
                if j == 5:
                    pe.wait_ge(nope_done, 6)
                rows(o_in[j][1][2], banks, o_cols[j][1], range(NCI), 1 if j == 0 else None)
            pe.wait_ge(nope_done, 8)
            for t in range(NT):
                pe.wait_ge(ckv_ready, t + 1)
                for k in range(2):
                    w = tr(ps[4][:, k * S + t * P:k * S + (t + 1) * P], ckr[:, t, k * P:(k + 1) * P])
            w.then_inc(ckvT_done, 1)
            pe.wait_ge(ckvT_ready, 2)
            pe.wait_ge(nope_done, 10)
            arrived(ukv[:2])
            for i in range(4):
                t, half = i // 2, i % 2
                for k in range(2):
                    w = mm(ps[4 + i][:, 0:384], ckvT[:, k, t * P:(t + 1) * P], uk_ap[:, k, half * 384:(half + 1) * 384],
                           start=k == 0, stop=k == 1)
                    release(w)
                w.then_inc(kv_done, 1)
            pe.wait_ge(rope_done, 10)
            pe.wait_ge(nope_done, 12)
            for i in range(4):
                t, half = i // 2, i % 2
                for k in range(2):
                    w = mm(ps[i][:, :], ckvT[:, k, t * P:(t + 1) * P], uv_ap[:, k, half * 512:(half + 1) * 512],
                           start=k == 0, stop=k == 1)
                w.then_inc(kv_done, 1)
            pending[0] = True
            pe.wait_ge(kn_ready, 4)
            for pr in range(4):
                for t in range(NT):
                    w = tr(ps[4 + pr // 2][:, (pr % 2) * S + t * P:(pr % 2) * S + (t + 1) * P],
                           q_i[:, t, 2 * pr:2 * pr + 2, :].rearrange("p h d -> p (h d)"))
                    release(w)
                if pr % 2:
                    w.then_inc(idxT_done, 1)
            for t in range(NT):
                w = tr(ps[6][:, t * P:(t + 1) * P], k_iw[:, t, 0:2 * HD])
            w.then_inc(idxT_done, 1)
            pe.wait_ge(idxT_ready, 3)
            pe.wait_ge(v_ready, 4)
            for i in range(IH):
                r = slice(HD * (i % 2), HD * (i % 2) + HD)
                if i >= 2:
                    pe.wait_ge(relu_ready, i - 1)
                for t in range(NT):
                    w = mm(ps[i % 2][:, KOFF[t]:KOFF[t] + KEYS[t]], qiT[r, i // 2, t * P:(t + 1) * P], kiT[r, 0:KEYS[t]],
                           start=True, stop=True)
                w.then_inc(logit_done, 1)
            pe.wait_ge(rope_done, 12)
            for i, src in enumerate((q_tok, kcat)):
                for pr in range(8):
                    if i and pr % 2 == 0:
                        pe.wait_ge(qkT_ready, 4 + pr // 2 + 1)
                    for t in range(NT):
                        w = tr(ps[4 + pr // 2][:, (pr % 2) * S + t * P:(pr % 2) * S + (t + 1) * P],
                               src[:, t, 2 * pr:2 * pr + 2, :].rearrange("p h d -> p (h d)"))
                    if pr % 2:
                        w.then_inc(qkT_done, 1)
            pe.wait_ge(qkT_ready, 12)
            pe.wait_ge(relu_ready, IH)
            scores(A_HEADS, qT1, kT1, 0)
            for hh in range(C_HEADS):
                n = A_HEADS + hh
                if hh + 1 < C_HEADS:
                    scores(n + 1, qT1, kT1, hh + 1)
                probsT(n)
                weigh(n, v1, hh, 8)
            pe.wait_ge(cat_ready, 16)
            for n in range(2):
                project(o_out[n], 512, (4 + 2 * n, 5 + 2 * n), ctxT, (), mix_out_done)

            norm(3)
            pe.wait_ge(uT_ready, 32)
            pe.wait_ge(late_in, 16 * 2)
            for t in range(NT):
                for k in range(KD):
                    w = mm(ps[4][:, t * E:(t + 1) * E], uT[:, k, t * P:(t + 1) * P], w_r[:, k, :],
                           start=k == 0, stop=k == KD - 1)
                    release(w)
            w.then_inc(router_done, 1)
            pe.wait_ge(member_ready, 1)
            member = lambda t: rt[:, t, 16:24]
            mm(ps[5][:, 0:E], tri, member(0), start=True, stop=True)
            mm(ps[5][:, E:2 * E], tri, member(1), start=True, stop=False)
            mm(ps[5][:, E:2 * E], ones, member(0), start=False, stop=True)
            mm(ps[5][:, 2 * E:3 * E], ones, member(0), start=True, stop=False)
            mm(ps[5][:, 2 * E:3 * E], ones, member(1), start=False, stop=True).then_inc(pos_done, 1)

            def gather(g):
                pe.wait_ge(sel_ready, g + 1)
                for bank in range(2):
                    for k in range(4):
                        kk = 4 * bank + k
                        for t in range(NT):
                            w = mm(ps[6 + bank][:, k * P:(k + 1) * P], hn[:, t, kk * P:(kk + 1) * P], sel[:, t, :],
                                   start=t == 0, stop=t == NT - 1)
                    w.then_inc(gather_done, 1)
                for t in range(NT):
                    w = mm(ps[3][:, 0:2], sel[:, t, :], info[:, t, :], start=t == 0, stop=t == NT - 1)
                w.then_inc(info_done, 1)

            eh = lambda k, t: e_hi[:, k, :]
            el = lambda k, t: e_lo[:, k, :]
            UF = FB * NT

            def expert(job, g, gather_next):
                def unit(b):
                    return job * MB + (UF + b)

                def chunks(kind, b):
                    return job * CE + (moe_c0 + NCI * moe_at[kind, b])

                def project(kind, b, bank):
                    for c in range(NCI):
                        chunk_mm(chunks(kind, b) + c, c, [ps[bank][:, :]], eh, el, (2 * c, 2 * c + 1), halves(512), 512,
                                 c == 0, c == NCI - 1)

                def transposes(b):
                    pe.wait_ge(mid_ready, unit(b) + 1)
                    for i in range(4):
                        w = tr(ps[2][:, i * P:(i + 1) * P], mid_e[:, i * P:(i + 1) * P])
                    w.then_inc(midT_done, 1)

                def down(b):
                    pe.wait_ge(midT_ready, unit(b) + 1)
                    for c in range(NCI):
                        pe.wait_ge(lo_ready, chunks("down", b) + (c + 1))
                        for half in range(2):
                            n = slice(half * 512, (half + 1) * 512)
                            w = mm3(ps[4 + half][:, :], eT_hi[:, c, :], eT_lo[:, c, :], w_hi[:, c, n], w_lo[:, c, n],
                                    b == 0 and c == 0, b == MB - 1 and c == NCI - 1)
                        w.then_inc(chunk_done, 1)

                pe.wait_ge(e_ready, g * 2 + 2)
                for b in range(MB):
                    pe.wait_ge(silu_done, unit(b))
                    project("gate", b, 0)
                    if b:
                        transposes(b - 1)
                    else:
                        pe.wait_ge(mid_ready, unit(0))
                    project("up", b, 1)
                    if b:
                        down(b - 1)
                if gather_next:
                    gather(g + 1)
                transposes(MB - 1)
                down(MB - 1)
                pe.wait_ge(y_sb_ready, job * 2 + 2)
                pe.wait_ge(selT_ready, job + 1)
                if gather_next:
                    pe.wait_ge(e_ready, g * 2 + 4)
                for i in range(4):
                    t, half = i // 2, i % 2
                    mm(ps[4 + i][:, :], selT[:, t * P:(t + 1) * P], y_sb[:, half * 512:(half + 1) * 512],
                       start=True, stop=True).then_inc(scatter_done, 1)
                pe.wait_ge(scatter_added, job * 4 + 4)

            gather(0)
            with pe.Fori(0, E) as e:
                expert(e, e, True)
            pe.wait_ge(tables_ready, 1)
            with pe.If(pe.value_load(job_tab[0:1, 2 * E:2 * E + 1], min_val=0, max_val=E) > 0):
                with pe.Fori(0, E) as e:
                    n_e = pe.value_load(job_tab[0:1, bass.ds(e, 1)], min_val=0, max_val=S)
                    with pe.If(n_e > OVER):
                        job = pe.value_load(job_tab[0:1, bass.ds(e + E, 1)], min_val=E, max_val=2 * E)
                        gather(job + 1)
                        expert(job, job + 1, False)

        @block.scalar
        def _(act):
            fn = nc.scalar.activation
            par = lambda i: s5_p[:, i, :]
            step = Steps(act, act_steps)

            with nc.allow_non_contiguous_dma(reason="small parameters"):
                col = lambda ap: ap.rearrange("o (k p) -> p (o k)", p=P)
                act.dma_start(c_col[:, :], col(A["c"])).then_inc(vec_in, 16)
                act.dma_start(h[:, :, :], x_tok).then_inc(x_in, 16)
                act.dma_start(cst[:, :], A["consts"]).then_inc(consts_in, 16)
                for i, sec in enumerate((0, 1, 3, 4)):
                    act.dma_start(b_col[:, i, :], col(A["b_ada"][0:1, sec * D:(sec + 1) * D])).then_inc(small_in, 16)
                for i, (n, l) in enumerate((("g_mix", 0), ("g_mix", 1), ("g_ffn", 0), ("g_ffn", 1))):
                    act.dma_start(g_col[:, i, :], col(A[n][l:l + 1, :])).then_inc(small_in, 16)
                act.dma_start(g_kv[:, :], col(A["mla_g_kv"])).then_inc(small_in, 16)
                for i, sec in enumerate((2, 5)):
                    act.dma_start(gate_row[:, i, :], A["b_ada"][0:1, sec * D:(sec + 1) * D].broadcast_to([P, D])).then_inc(small_in, 16)
            act.wait_ge(vec_in, 16)
            fn(c_col[:, :], c_col[:, :], ACT.Silu).then_inc(c_ready, 1)
            act.wait_ge(s5_in, 16 * 10)
            fn(par(DT), par(LDT), ACT.Exp).then_inc(s5_dt, 1)
            act.wait_ge(s5_x, 1)
            fn(par(MAG), par(X1), ACT.Exp).then_inc(s5_mag, 1)
            act.wait_ge(s5_r, 1)
            fn(par(SN), par(RR), ACT.Sin)
            fn(par(SH), par(RH), ACT.Sin).then_inc(s5_sin, 1)
            for i, (dst, scale) in enumerate(((s5_bT[:, 0], 1.0), (s5_bT[:, 1], 1.0), (s5_cT[:, 0], 1.0),
                                              (s5_cT[:, 1], -1.0), (s5_cT[:, 2], -1.0))):
                bank = ps[(0, 1, 2, 2, 3)[i]]
                act.wait_ge(s5_padT, (1, 2, 3, 3, 4)[i])
                fn(dst, bank[:, :].rearrange("p (t q) -> p t q", t=4), ACT.Copy, scale=scale).then_inc(s5_wT_ready, 1)

            def gates1():
                for i, (row, half, bank) in enumerate(((0, 0, 5), (0, 1, 6), (1, 0, 7), (1, 1, 5))):
                    act.wait_ge(mod_summed, 8 + i)
                    fn(gate_row[:, row, half * 512:(half + 1) * 512], ps[bank][:, :], ACT.Copy).then_inc(gate_ready, 1)

            def rms(src, junk, width, n):
                for t in range(NT):
                    w = fn(junk(t), src(t), ACT.Square, accum_out=stat[:, t:t + 1])
                    step(w)
                step.wait()
                fn(stat[:, 2:4], stat[:, 0:2], ACT.Sqrt, bias=eps[:, 0:1], scale=1.0 / width).then_inc(rms_ready, 1)

            def norm_stats(n):
                if n == 0:
                    act.wait_ge(x_in, 16)
                    act.wait_ge(s5_wT_ready, 5)
                elif n < 4:
                    act.wait_ge(h_ready, 4 * n)
                else:
                    act.wait_ge(experts_done, 1)
                act.wait_ge(eps_ready, 1)
                rms(lambda t: h[:, t, :], lambda t: hn[:, t, :], D, n)

            def norm_out(n):
                m = n % 2
                act.wait_ge(mod_ready, (1, 2, 3, 3)[n])
                for k in (0, 1, 4, 5):
                    act.wait_ge(hnT_done, 4 * n + k // 2 + 1)
                    fn(uT[:, k, :], ps[k // 2][:, (k % 2) * S:(k % 2 + 1) * S], ACT.Identity, scale=mod_a[:, m, k:k + 1],
                       bias=mod_b[:, m, k:k + 1]).then_inc(uT_ready, 1)

            def norm_hi(n):
                for k in range(KD):
                    act.wait_ge(uT_ready, KD * n + k + 1)
                    fn(x_hi[:, k, :], uT[:, k, :], ACT.Copy).then_inc(x_hi_ready, 1)

            def high(q, c, src, n=P):
                if not isinstance(q, int) or q >= NB:
                    act.wait_ge(chunk_done, q + 1 - NB)
                w = w_hi[0:n, c, 0:src.free_size()]
                fn(w, src, ACT.Copy).then_inc(hi_ready, 1)

            def arrived(slot, value):
                act.wait_ge(fill[slot], value)

            def heads(ap, n, width=HD):
                return ap.rearrange("p (h d) -> p h d", h=n)

            def exps(n, l1):
                act.wait_ge(max_ready, n + 1)
                q = n % 2
                for t in range(NT):
                    x = sm[:, q, KOFF[t]:KOFF[t] + KEYS[t]]
                    w = fn(x, x, ACT.Exp, scale=SC, bias=stat[:, 10 + 2 * q + t:11 + 2 * q + t],
                           **({"accum_out": stat[:, 14 + 2 * q + t:15 + 2 * q + t]} if l1 else {}))
                w.then_inc(exp_ready, 1)

            def probsT_out(n):
                act.wait_ge(pT_done, n + 1)
                if n >= 2:
                    act.wait_ge(o_done, n - 1)
                fn(pT[:, n % 2, :], ps[2 + n % 2][:, 0:KW], ACT.Copy).then_inc(pT_ready, 1)

            norm_stats(0)
            norm_out(0)
            for i in range(4):
                act.wait_ge(proj_done, i + 1)
                t, a = i % 2, (i // 2) * 512
                fn(heads(qk_tok[:, t, a:a + 512], 8)[:, :, ROPE:], heads(ps[4 + i][:, :], 8)[:, :, ROPE:],
                   ACT.Copy).then_inc(nope_done, 1)
            for t in range(NT):
                act.wait_ge(proj_done, 5 + t)
                fn(v_tok[:, t, :], ps[t][:, :], ACT.Copy).then_inc(vs_ready, 1)
            for i in range(2):
                act.wait_ge(proj_done, 7 + i)
                fn(s_inT[:, 2 * i:2 * i + 2, :], ps[2 + i][:, :].rearrange("p (c s) -> p c s", c=2), ACT.Copy).then_inc(vs_ready, 1)
            for i, dst in ((1, qT), (3, kT)):
                act.wait_ge(qkT_done, i + 1)
                fn(dst[:, 2:4, :], ps[4 + i][:, :].rearrange("p (c s) -> p c s", c=2), ACT.Copy).then_inc(qkT_ready, 1)
            exps(0, False)
            for hh in range(A_HEADS):
                if hh + 1 < A_HEADS:
                    exps(hh + 1, False)
                probsT_out(hh)
            act.wait_ge(y_pre, 4)
            for t in range(4):
                fn(s5_y[:, t, :], s5_y[:, t, :], ACT.Gelu_apprx_tanh).then_inc(y_ready, 1)
            th = lambda c: hn.rearrange("p t d -> p (t d)")[:, c * S:(c + 1) * S]
            act.wait_ge(s5_pads, 1)
            act.wait_ge(y_part_done, NCH)
            for c in range(4):
                act.wait_ge(glu_done, 2 * (c // 2) + 2)
                fn(th(c), ps[c // 2][:, (c % 2) * S:(c % 2 + 1) * S], ACT.Tanh, scale=0.5,
                   bias=s5_bg[:, c:c + 1]).then_inc(glu_tanh, 1)

            def item_high(q, slot, value, chunk, chunks=range(NCI)):
                arrived(slot, value)
                for c in chunks:
                    high(q + c, c, *chunk(slot, c))

            def silus(u0):
                for t in range(NT):
                    fn(mid[:, t, :], ps[t][:, 0:FW], ACT.Silu).then_inc(silu_done, 1)

            def midT_high(u0):
                for t in range(NT):
                    act.wait_ge(midT_done, u0 + t + 1)
                    fn(mT_hi[:, t, 0:2, :], ps[2 + t][:, 0:2 * P].rearrange("p (i t) -> p i t", i=2), ACT.Copy)
                    n = FT[2][1]
                    fn(mT_hi[0:n, t, 2, :], ps[2 + t][0:n, 2 * P:3 * P], ACT.Copy).then_inc(midT_hi_ready, 1)

            norm_stats(1)
            act.wait_ge(h_ready, 4)
            item_high(ff_first["gate"][2], *ff_first["gate"][:2], ff_chunk_of(FW))
            norm_hi(1)
            item_high(ff_first["up"][2], *ff_first["up"][:2], ff_chunk_of(FW))
            act.wait_ge(chunk_done, NCI)
            silus(0)
            with act.Fori(0, FB - 1) as i:
                q = i * CB + ff_chunks1
                v = lambda k: (ff_slot[k], i * ff_inc[k] + (ff_fill1[k] + ff_inc[k]))
                item_high(q, *v("gate"), ff_chunk_of(FW))
                midT_high(i * NT)
                item_high(q + NCI, *v("down"), ff_down_chunk)
                act.wait_ge(chunk_done, q + NCI)
                silus(i * NT + NT)
                item_high(q + 2 * NCI, *v("up"), ff_chunk_of(FW))
            midT_high((FB - 1) * NT)
            item_high(ff_last["down"][2], *ff_last["down"][:2], ff_down_chunk)

            norm_stats(2)
            gates1()
            proj_end = lambda j: o_in[j][1][2] + NCI

            def evac(j):
                if j in (1, 2):
                    act.wait_ge(chunk_done, proj_end(j))
                    for t in range(NT):
                        fn(q_tok[:, t, 8 * j - 8:8 * j, ROPE:], heads(ps[2 * j + t][:, 0:384], 8), ACT.Copy).then_inc(nope_done, 1)
                if j == 3:
                    act.wait_ge(chunk_done, proj_end(j))
                    for t in range(NT):
                        fn(ckr[:, t, :], ps[6 + t][:, 0:LAT + ROPE], ACT.Copy).then_inc(nope_done, 1)
                if j == 4:
                    act.wait_ge(chunk_done, proj_end(j))
                    for t in range(NT):
                        fn(q_i[:, t, :, ROPE:], heads(ps[t][:, :], 8)[:, :, ROPE:], ACT.Copy).then_inc(nope_done, 1)

            for j in range(6):
                q, (slot, value, _) = o_in[j][1][2], o_in[j][1]
                chunk = ff_chunk_of(o_cols[j][1])
                item_high(q, slot, value, chunk, (0, 1))
                if j == 0:
                    item_high(q, slot, value, chunk, (2, 3))
                    norm_hi(2)
                else:
                    evac(j - 1)
                    item_high(q, slot, value, chunk, (2, 3))
            act.wait_ge(nope_done, 10)
            act.wait_ge(x_ready, 2 * KD)
            rms(lambda t: ckr[:, t, 0:LAT], lambda t: flat_uT[:, t * LAT:(t + 1) * LAT], LAT, 0)
            step.wait()
            act.wait_ge(chunk_done, proj_end(5))
            for i in range(4):
                t, half = i // 2, i % 2
                act.wait_ge(kv_done, i + 1)
                fn(kcat[:, t, 8 * half:8 * half + 8, ROPE:], heads(ps[4 + i][:, 0:384], 8), ACT.Copy).then_inc(kn_ready, 1)
            for i in range(2):
                act.wait_ge(idxT_done, i + 1)
                fn(qiT[:, 2 * i:2 * i + 2, :], ps[4 + i][:, :].rearrange("p (c s) -> p c s", c=2), ACT.Copy).then_inc(idxT_ready, 1)
            for i in range(IH):
                act.wait_ge(logit_done, i + 1)
                if i >= 2:
                    act.wait_ge(score_added, i - 1)
                fn(sm[:, i % 2, :], ps[i % 2][:, 0:KW], ACT.Relu, scale=SC).then_inc(relu_ready, 1)
            for i in range(8):
                act.wait_ge(qkT_done, 5 + i)
                dst = (qT1, kT1)[i // 4]
                fn(dst[:, 2 * (i % 4):2 * (i % 4) + 2, :], ps[4 + i % 4][:, :].rearrange("p (c s) -> p c s", c=2),
                   ACT.Copy).then_inc(qkT_ready, 1)
            exps(A_HEADS, True)
            for hh in range(C_HEADS):
                n = A_HEADS + hh
                if hh + 1 < C_HEADS:
                    exps(n + 1, True)
                probsT_out(n)

            norm_stats(3)
            norm_out(3)
            act.wait_ge(gap_ready, 1)
            fn(rt[:, :, 40:41], rt[:, :, 41:42], ACT.Exp).then_inc(gap_exp, 1)

            UF = FB * NT

            def slots_high(g):
                for i in range(2):
                    act.wait_ge(x_e_ready, g * 2 + (i + 1))
                    fn(e_hi[:, 4 * i:4 * i + 4, :], x_e[:, 4 * i:4 * i + 4, :], ACT.Copy).then_inc(e_hi_ready, 1)

            def expert(job, g, gather_next):
                def convert(kind, b, cs=range(NCI)):
                    m = moe_at[kind, b]
                    item_high(job * CE + (moe_c0 + NCI * m), m % NS1,
                              job * (16 * PER) + (moe_fill0[m % NS1] + 16 * (m // NS1 + 1)), moe_chunk, cs)

                def silu_of(b):
                    act.wait_ge(chunk_done, job * CE + (moe_c0 + NCI * (moe_at["gate", b] + 1)))
                    act.wait_ge(midT_done, job * MB + (UF + b))
                    fn(mid_e[:, :], ps[0][:, :], ACT.Silu).then_inc(silu_done, 1)

                def midT_high_of(b):
                    act.wait_ge(midT_done, job * MB + (UF + b + 1))
                    fn(eT_hi[:, :, :], ps[2][:, :].rearrange("p (i t) -> p i t", i=4), ACT.Copy).then_inc(midT_hi_ready, 1)

                for b in range(MB):
                    convert("gate", b, (0,))
                    if b == 1:
                        silu_of(0)
                    convert("gate", b, (1, 2, 3))
                    convert("up", b)
                    if b:
                        midT_high_of(b - 1)
                        convert("down", b - 1, (0, 1))
                        silu_of(b)
                        convert("down", b - 1, (2, 3))
                convert("down", MB - 1, (0, 1))
                if gather_next:
                    slots_high(g + 1)
                midT_high_of(MB - 1)
                convert("down", MB - 1, (2, 3))

            slots_high(0)
            with act.Fori(0, E) as e:
                expert(e, e, True)
            act.wait_ge(tables_ready, 1)
            with act.If(act.value_load(job_tab[0:1, 2 * E:2 * E + 1], min_val=0, max_val=E) > 0):
                with act.Fori(0, E) as e:
                    n_e = act.value_load(job_tab[0:1, bass.ds(e, 1)], min_val=0, max_val=S)
                    with act.If(n_e > OVER):
                        job = act.value_load(job_tab[0:1, bass.ds(e + E, 1)], min_val=E, max_val=2 * E)
                        slots_high(job + 1)
                        expert(job, job + 1, False)
            norm_stats(4)

        @block.vector
        def _(dve):
            V = nc.vector
            par = lambda i: s5_p[:, i, :]
            step = Steps(dve, dve_steps)

            def chained(ins):
                step(ins)
                step.wait()

            V.memset(eps[:, :], EPS).then_inc(eps_ready, 1)

            def ada_item(ap, col, width, looped=None):
                for k in range(KD):
                    o = ada[:, col:col + width] if looped is None else ada[:, bass.ds(col, width)]
                    w = V.scalar_tensor_tensor(o, ap[:, k, :], c_col[:, k:k + 1], o, ALU.mult, ALU.add)
                    if k < KD - 1:
                        chained(w)
                w.then_inc(ada_used, 1)

            def columns(i, psum, j, mods):
                a = psum
                chained(V.tensor_tensor(b_col[:, 2 * i:2 * i + 2, :], a, b_col[:, 2 * i:2 * i + 2, :], ALU.add))
                step(V.tensor_copy(mod_b[:, i, :], b_col[:, 2 * i, :]))
                V.scalar_tensor_tensor(mod_a[:, i, :], b_col[:, 2 * i + 1, :], 1.0, g_col[:, j, :], ALU.add,
                                       ALU.mult).then_inc(mod_ready, 1)

            def mod0_first():
                dve.wait_ge(mod_summed, 1)
                dve.wait_ge(small_in, 16 * 11)
                columns(0, ps[4][:, 0:2 * KD].rearrange("p (a k) -> p a k", a=2), 0, 1)

            def mod0_rest():
                dve.wait_ge(mod_summed, 2)
                columns(1, ps[0][:, 0:2 * KD].rearrange("p (a k) -> p a k", a=2), 2, 2)
                for i, bank in enumerate((1, 2, 3, 1)):
                    dve.wait_ge(mod_summed, 3 + i)
                    g = gate_row[:, i // 2, (i % 2) * 512:(i % 2 + 1) * 512]
                    V.tensor_tensor(g, g, ps[bank][:, :], ALU.add).then_inc(gate_ready, 1)

            def mod1():
                dve.wait_ge(mod_summed, 7)
                m = lambda i: ps[4][:, i * KD:(i + 1) * KD]
                for j in range(2):
                    V.tensor_copy(mod_b[:, j, :], m(2 * j))
                    w = V.scalar_tensor_tensor(mod_a[:, j, :], m(2 * j + 1), 1.0, g_col[:, 2 * j + 1, :], ALU.add, ALU.mult)
                w.then_inc(mod_ready, 1)

            def low(q, c, src, n=P):
                dve.wait_ge(hi_ready, q + 1)
                f = src.free_size()
                V.tensor_tensor(w_lo[0:n, c, 0:f], src, w_hi[0:n, c, 0:f].bitcast(F32), ALU.subtract).then_inc(lo_ready, 1)

            def item_low(q, slot, chunk, chunks=range(NCI)):
                for c in chunks:
                    low(q + c, c, *chunk(slot, c))

            def norm_scale(n, count):
                dve.wait_ge(rms_ready, count)
                chained(V.reciprocal(stat[:, 4:6], stat[:, 2:4]))
                for t in range(NT):
                    V.tensor_scalar(hn[:, t, :], h[:, t, :], stat[:, 4 + t:5 + t], None, ALU.mult).then_inc(hn_ready, 1)

            def norm_out(n):
                m = n % 2
                for k in (2, 3, 6, 7):
                    dve.wait_ge(hnT_done, 4 * n + k // 2 + 1)
                    V.tensor_scalar(uT[:, k, :], ps[k // 2][:, (k % 2) * S:(k % 2 + 1) * S], mod_a[:, m, k:k + 1], mod_b[:, m, k:k + 1],
                                    ALU.mult, ALU.add).then_inc(uT_ready, 1)

            def norm_split(n):
                m = n % 2
                for k in range(KD):
                    dve.wait_ge(hnT_done, 4 * n + k // 2 + 1)
                    V.tensor_scalar(uT[:, k, :], ps[k // 2][:, (k % 2) * S:(k % 2 + 1) * S], mod_a[:, m, k:k + 1],
                                    mod_b[:, m, k:k + 1], ALU.mult, ALU.add).then_inc(uT_ready, 1)
                for k in range(KD):
                    dve.wait_ge(x_hi_ready, KD * (n - 1) + k + 1)
                    V.tensor_tensor(x_lo[:, k, :], uT[:, k, :], x_hi[:, k, :].bitcast(F32), ALU.subtract).then_inc(x_ready, 1)

            def rope(dst, src, t, n, sem_):
                x1, x2 = src[:, :, 0:HALF], src[:, :, HALF:ROPE]
                a, b = rope_buf[:, 0, 0:n, :], rope_buf[:, 1, 0:n, :]
                step(V.tensor_tensor(a, x1, cos(t, n), ALU.mult))
                chained(V.tensor_tensor(b, x2, sin(t, n), ALU.mult))
                chained(V.tensor_tensor(dst[:, :, 0:HALF], a, b, ALU.subtract))
                step(V.tensor_tensor(a, x2, cos(t, n), ALU.mult))
                chained(V.tensor_tensor(b, x1, sin(t, n), ALU.mult))
                V.tensor_tensor(dst[:, :, HALF:ROPE], a, b, ALU.add).then_inc(sem_, 1)

            def heads(ap, n):
                return ap.rearrange("p (h d) -> p h d", h=n)

            def mask_max(n, neg):
                dve.wait_ge(score_done, n + 1)
                if n >= 2:
                    dve.wait_ge(pT_done, n - 1)
                q = n % 2
                chained(V.tensor_tensor(sm[:, q, :], ps[q][:, 0:KW], neg, ALU.add))
                for t in range(NT):
                    w = V.reduce_max(stat[:, 6 + 2 * q + t:7 + 2 * q + t], sm[:, q, KOFF[t]:KOFF[t] + KEYS[t]], axis=AX.X)
                    step(w)
                step.wait()
                V.tensor_scalar(stat[:, 10 + 2 * q:12 + 2 * q], stat[:, 6 + 2 * q:8 + 2 * q], -SC, None,
                                ALU.mult).then_inc(max_ready, 1)

            def probs(n, l1):
                dve.wait_ge(exp_ready, n + 1)
                q = n % 2
                den, rden = stat[:, 14 + 2 * q:16 + 2 * q], stat[:, 18 + 2 * q:20 + 2 * q]
                if not l1:
                    for t in range(NT):
                        x = sm[:, q, KOFF[t]:KOFF[t] + KEYS[t]]
                        c = cst[:, C_CNT + KOFF[t]:C_CNT + KOFF[t] + KEYS[t]]
                        step(V.tensor_tensor_reduce(out=x, in0=x, in1=c, scale=1.0, scalar=0.0, op0=ALU.mult, op1=ALU.add,
                                                    accum_out=den[:, t:t + 1]))
                    step.wait()
                chained(V.reciprocal(rden, den))
                for t in range(NT):
                    x = sm[:, q, KOFF[t]:KOFF[t] + KEYS[t]]
                    w = V.tensor_scalar(x, x, rden[:, t:t + 1], None, ALU.mult)
                w.then_inc(p_ready, 1)

            def head_out(n, dst, pair):
                dve.wait_ge(o_done, n + 1)
                V.tensor_copy(dst[:, pair, :], ps[4 + pair % 2][:, 0:S]).then_inc(cat_ready, 1)

            def residual(count, m, base, in0=None, h0=0):
                for i in range(4):
                    n, t = i // 2, i % 2
                    if in0 is None:
                        dve.wait_ge(mix_out_done, base + i + 1)
                        y = ps[4 + 2 * n + t][:, :]
                    else:
                        y = in0(n, t)
                    tmp = flat_uT[:, i * 512:(i + 1) * 512]
                    chained(V.tensor_tensor(tmp, y, gate_row[:, m, n * 512:(n + 1) * 512], ALU.mult))
                    x = h[:, t, n * 512:(n + 1) * 512]
                    V.tensor_tensor(x, x, tmp, ALU.add).then_inc(h_ready, 1)

            mod0_first()
            dve.wait_ge(s5_den, 1)
            V.reciprocal(par(RDEN), par(DEN)).then_inc(s5_rden, 1)
            norm_scale(0, 1)
            dve.wait_ge(mod_ready, 1)
            norm_out(0)
            for i in range(4):
                dve.wait_ge(nope_done, i + 1)
                t, a = i % 2, (i // 2) * 512
                rope(heads(qk_tok[:, t, a:a + 512], 8), heads(ps[4 + i][:, :], 8), t, 8, rope_done)
                dve.wait_ge(rope_done, i + 1)
            for i, dst in ((0, qT), (2, kT)):
                dve.wait_ge(qkT_done, i + 1)
                V.tensor_copy(dst[:, 0:2, :], ps[4 + i][:, :].rearrange("p (c s) -> p c s", c=2)).then_inc(qkT_ready, 1)

            mod0_rest()

            def turn(j):
                dve.wait_ge(bu_done, j + 1)
                if j == 0:
                    dve.wait_ge(phase_ready, 1)
                bu = ps[6][:, :].rearrange("p (a s) -> p a s", a=2)
                c = lambda i: phase[:, i, j, :].unsqueeze(1).broadcast_to([P, 2, S])
                step.wait()
                step(V.tensor_tensor(rotA, bu, c(0), ALU.mult))
                V.tensor_tensor(rotB, bu, c(1), ALU.mult).then_inc(bu_used, 1)
                dve.wait_ge(bu_used, j + 1)
                step(V.tensor_tensor(s5_v[:, 0, :], rotA[:, 0, :], rotB[:, 1, :], ALU.add))
                chained(V.tensor_tensor(s5_v[:, 1, :], rotA[:, 1, :], rotB[:, 0, :], ALU.subtract))
                if j >= 2:
                    dve.wait_ge(post_ready, j - 1)
                z = zbuf[:, j % 2]
                for i in range(2):
                    w = V.tensor_tensor_scan(z[:, i, :], s5_p[:, MAG, j:j + 1].broadcast_to([P, S]), s5_v[:, i, :],
                                             0.0, ALU.mult, ALU.add)
                    if i == 0:
                        step(w)
                w.then_inc(z_ready, 1)
                dve.wait_ge(z_ready, j + 1)

            def y_before_gelu(t):
                dve.wait_ge(y_part_done, 4 * t + 4)
                V.scalar_tensor_tensor(s5_y[:, t, :], s_inT[:, t, :], s5_d[:, t:t + 1], ps[7][:, (t % 2) * S:(t % 2 + 1) * S],
                                       ALU.mult, ALU.add).then_inc(y_pre, 1)

            dve.wait_ge(vs_ready, 4)
            neg0 = cst[:, C_NEG:C_NEG + KW]
            mask_max(0, neg0)
            for hh in range(A_HEADS):
                if hh + 1 < A_HEADS:
                    mask_max(hh + 1, neg0)
                turn(2 * hh)
                probs(hh, False)
                turn(2 * hh + 1)
                if hh % 2:
                    head_out(hh, catT, hh // 2)
                elif hh:
                    y_before_gelu(hh // 2 - 1)
            y_before_gelu(3)
            for c in range(4):
                dve.wait_ge(glu_tanh, c + 1)
                t = hn.rearrange("p t d -> p (t d)")[:, c * S:(c + 1) * S]
                chained(V.tensor_scalar(t, t, 0.5, 0.5, ALU.mult, ALU.add))
                V.tensor_tensor(catT[:, 4 + c, :], t, s5_y[:, c, :], ALU.mult).then_inc(cat_ready, 1)
            residual(0, 0, 0)

            norm_scale(1, 2)
            dve.wait_ge(mod_ready, 2)
            item_low(ff_first["gate"][2], ff_first["gate"][0], ff_chunk_of(FW))
            norm_split(1)
            item_low(ff_first["up"][2], ff_first["up"][0], ff_chunk_of(FW))
            dve.wait_ge(bias_in, 16)
            for i in range(2):
                slot, value, _ = ff_first[f"ada{i}"]
                dve.wait_ge(fill[slot], value)
                ada_item(block_ap(slot, KD, ADA1), i * ADA1, ADA1)

            def mids(u0, q):
                dve.wait_ge(chunk_done, q)
                for t in range(NT):
                    dve.wait_ge(silu_done, u0 + t + 1)
                    V.tensor_tensor(mid[:, t, :], mid[:, t, :], ps[2 + t][:, 0:FW], ALU.mult).then_inc(mid_ready, 1)

            def midT_low(u0):
                for t in range(NT):
                    dve.wait_ge(midT_hi_ready, u0 + t + 1)
                    V.tensor_tensor(mT_lo[:, t, 0:2, :], ps[2 + t][:, 0:2 * P].rearrange("p (i t) -> p i t", i=2),
                                    mT_hi[:, t, 0:2, :].bitcast(F32), ALU.subtract)
                    n = FT[2][1]
                    V.tensor_tensor(mT_lo[0:n, t, 2, :], ps[2 + t][0:n, 2 * P:3 * P], mT_hi[0:n, t, 2, :].bitcast(F32),
                                    ALU.subtract).then_inc(midT_ready, 1)

            with dve.Fori(0, FB - 1) as i:
                step.enter(i, 0, 2 * (KD - 1))
                q = i * CB + ff_chunks1
                item_low(q, ff_slot["gate"], ff_chunk_of(FW), (0, 1))
                mids(i * NT, q)
                item_low(q, ff_slot["gate"], ff_chunk_of(FW), (2, 3))
                midT_low(i * NT)
                item_low(q + NCI, ff_slot["down"], ff_down_chunk)
                for j in range(2):
                    item_low(q + 2 * NCI, ff_slot["up"], ff_chunk_of(FW), (2 * j, 2 * j + 1))
                    k = f"ada{j}"
                    dve.wait_ge(fill[ff_slot[k]], i * 16 + (ff_fill1[k] + 16))
                    ada_item(block_ap(ff_slot[k], KD, ADA1), i * (2 * ADA1) + (2 + j) * ADA1, ADA1, i)
            step.leave(0, FB - 1)
            mids((FB - 1) * NT, ff_last["down"][2])
            midT_low((FB - 1) * NT)
            item_low(ff_last["down"][2], ff_last["down"][0], ff_down_chunk)
            dve.wait_ge(chunk_done, ff_last["down"][2] + NCI)
            residual(0, 1, 0, lambda n, t: ps[4 + 2 * t + n][:, :])

            mod1()
            norm_scale(2, 3)
            dve.wait_ge(mod_ready, 3)
            proj_end = lambda j: o_in[j][1][2] + NCI

            def rope_out(j):
                if j == 0:
                    for t in range(NT):
                        dve.wait_ge(chunk_done, proj_end(0))
                        rope(q_tok[:, t], heads(ps[t][:, 0:256], 16), t, 16, rope_done)
                        dve.wait_ge(rope_done, 5 + t)
                if j == 4:
                    for t in range(NT):
                        dve.wait_ge(nope_done, 11 + t)
                        rope(q_i[:, t], heads(ps[t][:, :], 8), t, 8, rope_done)
                        dve.wait_ge(rope_done, 7 + t)

            for j in range(6):
                q, slot = o_in[j][1][2], o_in[j][1][0]
                chunk = ff_chunk_of(o_cols[j][1])
                item_low(q, slot, chunk, (0, 1))
                if j == 0:
                    item_low(q, slot, chunk, (2, 3))
                    norm_split(2)
                else:
                    rope_out(j - 1)
                    item_low(q, slot, chunk, (2, 3))
            dve.wait_ge(rms_ready, 4)
            chained(V.reciprocal(stat[:, 4:6], stat[:, 2:4]))
            for t in range(NT):
                V.tensor_scalar(ckr[:, t, 0:LAT], ckr[:, t, 0:LAT], stat[:, 4 + t:5 + t], None, ALU.mult).then_inc(ckv_ready, 1)
            for t in range(NT):
                dve.wait_ge(chunk_done, proj_end(5))
                kk = k_iw[:, t, :]
                step(V.tensor_copy(kk[:, ROPE:HD], ps[2 + t][:, ROPE:HD]))
                step(V.tensor_scalar(kk[:, 2 * HD:], ps[2 + t][:, HD:HD + IH], IH ** -0.5, None, ALU.mult))
                rope(kk[:, 0:HD].unsqueeze(1), ps[2 + t][:, 0:HD].unsqueeze(1), t, 1, rope_done)
                dve.wait_ge(rope_done, 9 + t)
                step.wait()
                step(V.tensor_copy(kk[:, HD:2 * HD], kk[:, 0:HD]))
            for k in range(2):
                dve.wait_ge(ckvT_done, 1)
                V.tensor_scalar(ckvT[:, k, :], ps[4][:, k * S:(k + 1) * S], g_kv[:, k:k + 1], None, ALU.mult).then_inc(ckvT_ready, 1)
            for t in range(NT):
                kr = kr_t[:, :].unsqueeze(1)
                rope(kr, ckr[:, t, LAT:].unsqueeze(1), t, 1, dve_steps)
                step.n += 1
                step.wait()
                V.tensor_copy(kcat[:, t, :, 0:ROPE], kr.broadcast_to([P, C_HEADS, ROPE])).then_inc(rope_done, 1)
                dve.wait_ge(rope_done, 11 + t)
            for i in range(4):
                t, half = i // 2, i % 2
                dve.wait_ge(kv_done, 5 + i)
                V.tensor_copy(v1[:, t, half * 512:(half + 1) * 512], ps[i][:, :]).then_inc(v_ready, 1)
            dve.wait_ge(idxT_done, 3)
            V.tensor_copy(kiT[:, :], ps[6][:, 0:S]).then_inc(idxT_ready, 1)
            for i in range(IH):
                dve.wait_ge(relu_ready, i + 1)
                for t in range(NT):
                    c = slice(KOFF[t], KOFF[t] + KEYS[t])
                    wi = k_iw[:, t, 2 * HD + i:2 * HD + i + 1]
                    if i == 0:
                        w = V.tensor_scalar(score[:, c], sm[:, 0, c], wi, None, ALU.mult)
                    else:
                        w = V.scalar_tensor_tensor(score[:, c], sm[:, i % 2, c], wi, score[:, c], ALU.mult, ALU.add)
                w.then_inc(score_added, 1)
                dve.wait_ge(score_added, i + 1)
            chained(V.tensor_tensor(score, score, cst[:, C_CB:C_CB + KW], ALU.add))
            for i in range(TOPK // 8):
                for t in range(NT):
                    step(V.max(top8[:, t, :], score[:, KOFF[t]:KOFF[t] + KEYS[t]]))
                step.wait()
                for t in range(NT):
                    x = score[:, KOFF[t]:KOFF[t] + KEYS[t]]
                    step(V.match_replace(x, top8[:, t, :], x, NEG))
                step.wait()
            chained(V.tensor_scalar(selneg, score, NEG / 3, BIG, ALU.is_le, ALU.mult))
            chained(V.tensor_tensor(selneg, selneg, cst[:, C_CAU:C_CAU + KW], ALU.mult))
            chained(V.tensor_scalar(selneg, selneg, BIG, None, ALU.subtract))
            mask_max(A_HEADS, selneg)
            for hh in range(C_HEADS):
                n = A_HEADS + hh
                if hh + 1 < C_HEADS:
                    mask_max(n + 1, selneg)
                probs(n, True)
                if hh % 2:
                    head_out(n, ctxT, hh // 2)
            residual(0, 0, 4)

            norm_scale(3, 5)
            dve.wait_ge(late_in, 16 * 2)
            norm_out(3)
            dve.wait_ge(router_done, 1)
            for t in range(NT):
                step(V.tensor_tensor(lg[:, t, :], ps[4][:, t * E:(t + 1) * E], b_r[:, :], ALU.add))
            step(V.memset(possel[:, :, E:E + 1], -1.0))
            step(V.memset(comb[:, :, E:E + 1], 0.0))
            step.wait()
            for t in range(NT):
                step(V.max(top[:, t, :], lg[:, t, :]))
            step.wait()
            for t in range(NT):
                step(V.max_index(top_i[:, t, :], top[:, t, :], lg[:, t, :]))
            step.wait()
            step(V.tensor_copy(rt[:, :, 24:26], top_i[:, :, 0:2]))
            V.tensor_tensor(rt[:, :, 41:42], top[:, :, 1:2], top[:, :, 0:1], ALU.subtract).then_inc(gap_ready, 1)
            step.wait()
            for t in range(NT):
                for i in range(2):
                    step(V.tensor_scalar(rt[:, t, 8 * i:8 * i + 8], iota(E), rt[:, t, 24 + i:25 + i], None, ALU.is_equal))
            step.wait()
            V.tensor_tensor(rt[:, :, 16:24], rt[:, :, 0:8], rt[:, :, 8:16], ALU.add).then_inc(member_ready, 1)
            dve.wait_ge(gap_exp, 1)
            chained(V.tensor_scalar(rt[:, :, 42:43], rt[:, :, 40:41], 1.0, None, ALU.add))
            chained(V.reciprocal(rt[:, :, 43:44], rt[:, :, 42:43]))
            chained(V.tensor_tensor(rt[:, :, 44:45], rt[:, :, 40:41], rt[:, :, 43:44], ALU.mult))
            for t in range(NT):
                chained(V.tensor_scalar(comb[:, t, 0:E], rt[:, t, 0:8], rt[:, t, 43:44], None, ALU.mult))
                chained(V.scalar_tensor_tensor(comb[:, t, 0:E], rt[:, t, 8:16], rt[:, t, 44:45], comb[:, t, 0:E], ALU.mult, ALU.add))
            dve.wait_ge(pos_done, 1)
            dve.wait_ge(member_ready, 1)
            for t in range(NT):
                chained(V.scalar_tensor_tensor(possel[:, t, 0:E], ps[5][:, t * E:(t + 1) * E], 1.0, rt[:, t, 16:24], ALU.add, ALU.mult))
            chained(V.tensor_scalar(possel[:, :, 0:E], possel[:, :, 0:E], -1.0, None, ALU.add))
            cnt, rnd, over = jobs[:, 0:E], jobs[:, E:2 * E], jobs[:, 2 * E:3 * E]
            chained(V.tensor_copy(cnt, ps[5][:, 2 * E:3 * E]))
            chained(V.tensor_scalar(over, cnt, OVER + 0.5, None, ALU.is_gt))
            chained(V.tensor_tensor_scan(rnd, ones[:, 0:E], over, 0.0, ALU.mult, ALU.add))
            step(V.tensor_copy(job_tab[:, 0:E], cnt))
            step(V.tensor_copy(job_tab[:, 2 * E:2 * E + 1], rnd[:, E - 1:E]))
            step.wait()
            chained(V.tensor_tensor(rnd, rnd, over, ALU.subtract))
            chained(V.tensor_scalar(rnd, rnd, float(E), None, ALU.add))
            V.tensor_copy(job_tab[:, E:2 * E], rnd).then_inc(tables_ready, 1)
            for t in range(NT):
                step(V.tensor_copy(info[:, t, 0:1], cst[:, C_TOK + t:C_TOK + t + 1]))

            UF = FB * NT

            def select(e, g, rnd_):
                step.wait()
                for t in range(NT):
                    step(V.tensor_scalar(cur[:, t, 0:1], possel[:, t, bass.ds(e, 1)], float(-P * rnd_), None, ALU.add))
                    step(V.tensor_copy(info[:, t, 1:2], comb[:, t, bass.ds(e, 1)]))
                step.wait()
                for t in range(NT):
                    w = V.tensor_scalar(sel[:, t, :], iota(P), cur[:, t, 0:1], None, ALU.is_equal)
                    if t == 0:
                        step(w)
                w.then_inc(sel_ready, 1)

            def slots_in(g):
                for i in range(2):
                    dve.wait_ge(gather_done, g * 2 + (i + 1))
                    for k in range(4 * i, 4 * i + 4):
                        w = V.tensor_scalar(x_e[:, k, :], ps[6 + i][:, (k % 4) * P:(k % 4 + 1) * P], mod_a[:, 1, k:k + 1],
                                            mod_b[:, 1, k:k + 1], ALU.mult, ALU.add)
                    w.then_inc(x_e_ready, 1)
                for i in range(2):
                    dve.wait_ge(e_hi_ready, g * 2 + (i + 1))
                    k = slice(4 * i, 4 * i + 4)
                    V.tensor_tensor(e_lo[:, k, :], x_e[:, k, :], e_hi[:, k, :].bitcast(F32), ALU.subtract).then_inc(e_ready, 1)

            def back(g, job):
                dve.wait_ge(info_done, g + 1)
                chained(V.tensor_copy(slot_info, ps[3][:, 0:2]))
                V.tensor_scalar(selT, iota(S), slot_info[:, 0:1], slot_info[:, 1:2], ALU.is_equal,
                                ALU.mult).then_inc(selT_ready, 1)

            def expert(job, e_next, g, gather_next):
                def convert(kind, b, cs=range(NCI)):
                    m = moe_at[kind, b]
                    item_low(job * CE + (moe_c0 + NCI * m), m % NS1, moe_chunk, cs)

                def mids_of(b):
                    dve.wait_ge(chunk_done, job * CE + (moe_c0 + NCI * (moe_at["up", b] + 1)))
                    dve.wait_ge(silu_done, job * MB + (UF + b + 1))
                    V.tensor_tensor(mid_e[:, :], mid_e[:, :], ps[1][:, :], ALU.mult).then_inc(mid_ready, 1)

                def midT_low_of(b):
                    dve.wait_ge(midT_hi_ready, job * MB + (UF + b + 1))
                    V.tensor_tensor(eT_lo[:, :, :], ps[2][:, :].rearrange("p (i t) -> p i t", i=4),
                                    eT_hi[:, :, :].bitcast(F32), ALU.subtract).then_inc(midT_ready, 1)

                for b in range(MB):
                    convert("gate", b, (0,))
                    if b:
                        mids_of(b - 1)
                    convert("gate", b, (1, 2, 3))
                    convert("up", b)
                    if b == 0:
                        back(g, job)
                        if gather_next:
                            select(e_next, g + 1, 0)
                    else:
                        midT_low_of(b - 1)
                        convert("down", b - 1)
                convert("down", MB - 1, (0, 1))
                mids_of(MB - 1)
                if gather_next:
                    slots_in(g + 1)
                midT_low_of(MB - 1)
                convert("down", MB - 1, (2, 3))
                dve.wait_ge(chunk_done, job * CE + (moe_c0 + CE))
                for half in range(2):
                    n = slice(half * 512, (half + 1) * 512)
                    V.tensor_tensor(y_sb[:, n], ps[4 + half][:, :], gate_row[:, 1, n], ALU.mult).then_inc(y_sb_ready, 1)
                for i in range(4):
                    t, half = i // 2, i % 2
                    dve.wait_ge(scatter_done, job * 4 + (i + 1))
                    y = h[:, t, half * 512:(half + 1) * 512]
                    V.tensor_tensor(y, y, ps[4 + i][:, :], ALU.add).then_inc(scatter_added, 1)

            select(0, 0, 0)
            slots_in(0)
            with dve.Fori(0, E) as e:
                step.enter(e, 0, 6)
                expert(e, e + 1, e, True)
            step.leave(0, E)
            n_over = dve.value_load(job_tab[0:1, 2 * E:2 * E + 1], min_val=0, max_val=E)
            with dve.If(n_over > 0):
                with dve.Fori(0, E) as e:
                    n_e = dve.value_load(job_tab[0:1, bass.ds(e, 1)], min_val=0, max_val=S)
                    with dve.If(n_e > OVER):
                        job = dve.value_load(job_tab[0:1, bass.ds(e + E, 1)], min_val=E, max_val=2 * E)
                        step.enter(job, E, 6)
                        select(e, job + 1, 1)
                        slots_in(job + 1)
                        expert(job, None, job + 1, False)
            step.sem, step.n, step.reg = final_steps, 0, None
            dve.wait_ge(scatter_added, n_over * 4 + 4 * E)
            V.memset(eps[:, :], EPS).then_inc(experts_done, 1)

            dve.wait_ge(rms_ready, 6)
            V.reciprocal(stat[:, 4:6], stat[:, 2:4]).then_inc(stat_ready, 1)
            dve.wait_ge(stat_ready, 1)
            dve.wait_ge(late_in, 16 * 3)
            for t in range(NT):
                V.scalar_tensor_tensor(final_y[:, t, :], h[:, t, :], stat[:, 4 + t:5 + t], gate_row[:, 0, :],
                                       ALU.mult, ALU.mult).then_inc(y_final, 1)


_INS = ["x", "c", "w_ada", "b_ada", "g_mix", "g_ffn", "g_final", "e_w_in", "e_w_out", "s5_a_re", "s5_a_im",
        "s5_log_dt", "s5_b_re", "s5_b_im", "s5_c_re", "s5_c_im", "s5_d", "s5_w_glu", "s5_b_glu",
        "ff_w_gate", "ff_w_up", "ff_w_down", "o_w_in", "o_w_out", "mla_g_kv", "mla_w_uk", "mla_w_uv",
        "moe_w_router", "moe_b_router", "moe_w_gate", "moe_w_up", "moe_w_down"]


def kernel(**inputs):
    import concourse.bacc as bacc
    from concourse.bass_utils import run_bass_kernel_spmd as run

    nc = bacc.Bacc("TRN2", target_bir_lowering=False, num_devices=1)
    arrays, aps = {}, {}
    for name in _INS:
        a = np.ascontiguousarray(inputs[name])
        arrays[f"in_{name}"] = a
        aps[name] = nc.dram_tensor(f"in_{name}", a.shape, mybir.dt.from_np(a.dtype), kind="ExternalInput").ap()
    consts = constants()
    arrays["in_consts"] = consts
    aps["consts"] = nc.dram_tensor("in_consts", consts.shape, F32, kind="ExternalInput").ap()
    out = nc.dram_tensor("out_0", (1, S, D), F32, kind="ExternalOutput").ap()
    trunk(nc, aps, out)
    r = run(nc, [arrays], core_ids=[0])
    return r.results[0]["out_0"]
```

```python
import numpy as np
from contextlib import ExitStack

import concourse.bass as bass
from concourse import mybir

F32 = mybir.dt.float32
F32R = mybir.dt.float32r
U32 = mybir.dt.uint32
I32 = mybir.dt.int32
ALU = mybir.AluOpType
ACT = mybir.ActivationFunctionType
AX = mybir.AxisListType

P = 128
D = 1024
S = 256
NT = S // P
KD = D // P
EPS = 1e-6
HD = 64
ROPE = HD // 4
HALF = ROPE // 2
SC = HD ** -0.5
A_HEADS = 8
A_W = A_HEADS * HD
G_S5, P_S5, C_S5 = 32, 64, 16
NCH = G_S5 * P_S5 // P
C_HEADS = 16
NOPE = HD - ROPE
LAT = D // 4
IH = 8
TOPK = min(256, S // 4)
FF = 2816
FB = 8
FW = FF // FB
FT = [(0, P), (P, P), (2 * P, FW - 2 * P)]
E = 8
FE = 3584
MB = FE // 512
SLOT = 4096
CHUNK, NB = 1024, 4
NCI = 4
NS0, NS1 = 5, 7
ADA1 = 384
NA1 = 6 * D // ADA1
KEYS = [P, 2 * P]
KOFF = [0, P]
KW = sum(KEYS)
BIG = 1e30
NEG = -3e38
ROUND = 12582912.0
PI = 3.1415925
OVER = P
TWO_PI = (6.28125, 0.0019353071693331, 1.0253131677018246e-11)

C_ID, C_ONE, C_TRI = 0, P, 2 * P
C_IOTA = 3 * P
C_CNT = C_IOTA + S
C_NEG = C_CNT + KW
C_CAU = C_NEG + KW
C_CB = C_CAU + KW
C_COS = C_CB + KW
C_SIN = C_COS + NT * HALF
C_HM = C_SIN + NT * HALF
C_TOK = C_HM + 2
NC = C_TOK + 2


def constants():
    c = np.zeros((P, NC), np.float32)
    p = np.arange(P)
    c[:, C_ID:C_ID + P] = np.eye(P)
    c[:, C_ONE:C_ONE + P] = 1
    c[:, C_TRI:C_TRI + P] = p[:, None] < p[None, :]
    c[:, C_IOTA:C_IOTA + S] = np.arange(S)
    for t in range(NT):
        d = (t * P + p)[:, None] - np.arange(KEYS[t])[None, :]
        n = (d >= 0) * ((d <= 128) * 1 + (d % 4 == 0) * 1 + (d % 16 == 0) * 1)
        a, b = KOFF[t], KOFF[t] + KEYS[t]
        c[:, C_CNT + a:C_CNT + b] = n
        c[:, C_NEG + a:C_NEG + b] = np.where(n == 0, -BIG, 0)
        c[:, C_CAU + a:C_CAU + b] = d >= 0
        c[:, C_CB + a:C_CB + b] = np.where(d >= 0, 0, NEG)
        inv = np.float32(500000.0) ** (-np.arange(0, ROPE, 2, dtype=np.float32) / np.float32(ROPE))
        ang = (t * P + p).astype(np.float32)[:, None] * inv.astype(np.float32)[None, :]
        c[:, C_COS + t * HALF:C_COS + (t + 1) * HALF] = np.cos(ang.astype(np.float64))
        c[:, C_SIN + t * HALF:C_SIN + (t + 1) * HALF] = np.sin(ang.astype(np.float64))
        c[:, C_TOK + t] = t * P + p
        c[:, C_HM + t] = (p // C_S5) % 2 == t
    return c


class Places:

    def __init__(self, nc, base, size):
        self.nc, self.base, self.size = nc, base, size

    def at(self, name, offset, shape, dt=F32):
        assert offset + int(np.prod(shape[1:])) <= self.size, name
        return self.nc.alloc_sbuf_tensor_at(name, shape, dt, offset=self.base + 4 * offset)


class Steps:

    def __init__(self, eng, sem):
        self.eng, self.sem, self.n = eng, sem, 0

        self.reg, self.per, self.at = None, 0, 0

    def __call__(self, ins):
        ins.then_inc(self.sem, 1)
        self.n += 1
        return ins

    def wait(self):
        if self.reg is None:
            self.eng.wait_ge(self.sem, self.n)
        else:
            self.eng.wait_ge(self.sem, self.reg * self.per + self.n)

    def enter(self, reg, first, per):
        self.reg, self.per, self.at = reg, per, self.n
        self.n -= first * per

    def leave(self, first, turns):
        assert self.n + first * self.per == self.at + self.per, (self.n, self.at, self.per)
        self.n = self.at + turns * self.per
        self.reg = None


def trunk(nc, A, out):
    ctx = ExitStack()
    with ctx:
        def sb(name, shape, dt=F32):
            return ctx.enter_context(nc.sbuf_tensor(name, shape, dt))

        def sem(name):
            return ctx.enter_context(nc.semaphore(name))

        cst = sb("cst", [P, NC])
        h = sb("h", [P, NT, D])
        gate_row = sb("gate_row", [P, 2, D])
        ring = sb("ring", [P, NS0, SLOT])
        c_col = sb("c_col", [P, KD])
        bg_col = sb("bg_col", [P, 8, KD])
        g_col = bg_col[:, 4:8, :]
        b_col = bg_col[:, 0:4, :]
        mod_a = sb("mod_a", [P, 2, KD])
        mod_b = sb("mod_b", [P, 2, KD])
        stat = sb("stat", [P, 32])
        eps = sb("eps", [P, 1])
        s5_d = sb("s5_d", [P, 4])
        s5_bg = sb("s5_bg", [P, 4])
        w_r = sb("w_r", [P, KD, E])
        b_r = sb("b_r", [P, E])
        g_kv = sb("g_kv", [P, 2])
        top_i = sb("top_i", [P, NT, E], U32)
        job_tab = sb("job_tab", [P, 3 * E], I32)
        AT_UT, AT_ADA, AT_WIDE, AT_WORK = 0, KD * S, KD * S + 6 * D, KD * S + 6 * D + 2 * SLOT
        WORK = 9600
        base = (nc.sbuf_base + 31) // 32 * 32
        arena = sb("arena", [P, AT_WORK + WORK])
        at = Places(nc, base, AT_WORK + WORK).at
        uT = at("uT", AT_UT, [P, KD, S])
        ada = at("ada", AT_ADA, [P, 6 * D])
        phase_buf = at("phase_buf", AT_WIDE, [P, 2, SLOT])
        work = at("work", AT_WORK, [P, WORK])
        ring_more = at("ring_more", AT_UT, [P, NS1 - NS0, SLOT])
        w_hi = at("w_hi", AT_WIDE, [P, NB, CHUNK], F32R)
        w_lo = at("w_lo", AT_WIDE + NB * CHUNK, [P, NB, CHUNK], F32R)
        ps = [ctx.enter_context(nc.psum_tensor(f"ps{i}", [P, 512], F32)) for i in range(8)]

        ident = cst[:, C_ID:C_ID + P]
        ones = cst[:, C_ONE:C_ONE + P]
        tri = cst[:, C_TRI:C_TRI + P]

        def iota(n):
            return cst[:, C_IOTA:C_IOTA + n]

        def cos(t, heads):
            return cst[:, C_COS + t * HALF:C_COS + (t + 1) * HALF].unsqueeze(1).broadcast_to([P, heads, HALF])

        def sin(t, heads):
            return cst[:, C_SIN + t * HALF:C_SIN + (t + 1) * HALF].unsqueeze(1).broadcast_to([P, heads, HALF])

        class Region:

            def __init__(self, buf, size, at=0):
                self.buf, self.size, self.at = buf, size, at

            def take(self, *shape):
                n = int(np.prod(shape))
                a = self.buf[:, self.at:self.at + n]
                self.at += n
                assert self.at <= self.size, self.at
                if len(shape) == 1:
                    return a
                names = "abcd"[:len(shape)]
                return a.rearrange(f"p ({' '.join(names)}) -> p {' '.join(names)}",
                                   **{x: s for x, s in zip(names, shape)})

        flat_uT = uT[:, :, :].rearrange("p a b -> p (a b)")
        rope_buf = work[:, WORK - 256:WORK].rearrange("p (a h d) -> p a h d", a=2, h=C_HEADS)
        W0 = Region(work, WORK - 256)
        hn = W0.take(NT, D)
        qk_tok = hn
        s5_y = W0.take(4, S)
        s5_p = W0.take(24, NCH)
        s5_bT = W0.take(2, 4, P)
        s5_cT = W0.take(3, 4, P)
        s5_tmp = W0.take(NCH, P)
        s5_v = W0.take(2, S)
        s5_small = W0.take(10)
        log_dt = W0.take(G_S5)
        WA = Region(ada, 6 * D)
        qT = WA.take(4, S)
        kT = WA.take(4, S)
        v_tok = WA.take(NT, A_W)
        s_inT = WA.take(4, S)
        catT = WA.take(KD, S)
        tmp_flat = s5_tmp.rearrange("p a b -> p (a b)")
        rotA = tmp_flat[:, 0:512].rearrange("p (a b) -> p a b", a=2)
        rotB = tmp_flat[:, 512:1024].rearrange("p (a b) -> p a b", a=2)
        zbuf = tmp_flat[:, 1024:2048].rearrange("p (n a b) -> p n a b", n=2, a=2)
        post = hn.rearrange("p t (n a b) -> p t n a b", n=2, a=2)
        WU = Region(flat_uT, KD * S)
        sm = WU.take(3, KW)
        pT = WU.take(2, KW)
        phase = phase_buf[:, :, :].rearrange("p a (b c) -> p a b c", b=NCH)

        WI = Region(phase_buf[:, 1, :], SLOT)
        b_in = WI.take(2, NCH, C_S5)
        c_in = WI.take(2, 4, P_S5)
        b_bar = WI.take(2, NCH, C_S5)
        s5_t = WI.take(NCH, C_S5)
        b_pad = tmp_flat[:, 0:1024].rearrange("p (a b c) -> p a b c", a=2, b=4)
        c_pad = tmp_flat[:, 1024:2048].rearrange("p (a b c) -> p a b c", a=2, b=4)
        rows_at, n_rows = {}, 0
        for name, n in (("c", KD), ("a_re", NCH), ("a_im", NCH), ("b01", 2 * KD), ("b34", 2 * KD), ("g_mix", 2 * KD),
                        ("g_ffn", 2 * KD), ("g_kv", 2), ("d", 4), ("b_glu", 4)):
            rows_at[name] = (n_rows, n)
            n_rows += n
        vec_rows = flat_uT[:, 0:P]
        acc0 = catT.rearrange("p k s -> p (k s)")

        (LR, LI, LDT, DT, X1, ANG, MAG, KK, TT, RR, RH, SN, SH, CS, AR, AI, NR, DEN, RDEN, FR, FI,
         ER, EI, T2) = range(24)

        consts_in = sem("consts_in")
        x_in = sem("x_in")
        rows_in, ident_in, dt_in = sem("rows_in"), sem("ident_in"), sem("dt_in")
        rows_done = sem("rows_done")
        cols_ready = sem("cols_ready")
        gate_zeroed = sem("gate_zeroed")
        bbar_ready = sem("bbar_ready")
        s5_in = sem("s5_in")
        bias_in = sem("bias_in")
        late_in = sem("late_in")
        fill = [sem(f"slot{i}_filled") for i in range(NS1)]
        weights_used = sem("weights_used")
        ada_scaled = sem("ada_scaled")
        ada_used = sem("ada_used")
        ada_added = sem("ada_added")
        hi_ready, lo_ready, chunk_done = sem("hi_ready"), sem("lo_ready"), sem("chunk_done")
        dve_steps, act_steps, pool_steps = sem("dve_steps"), sem("act_steps"), sem("pool_steps")
        c_ready = sem("c_ready")
        ada_zeroed = sem("ada_zeroed")
        mod_summed = sem("mod_summed")
        mod_ready = sem("mod_ready")
        gate_ready = sem("gate_ready")
        h_ready = sem("h_ready")
        rms_ready = sem("rms_ready")
        hn_ready = sem("hn_ready")
        hnT_done = sem("hnT_done")
        uT_ready = sem("uT_ready")
        mix_out_done = sem("mix_out_done")
        out_stored = sem("out_stored")

        tables_ready = sem("tables_ready")
        y_final = sem("y_final")
        ckv_ready = sem("ckv_ready")
        ckvT_done = sem("ckvT_done")
        ckvT_ready = sem("ckvT_ready")
        kv_done = sem("kv_done")
        kn_ready = sem("kn_ready")
        v_ready = sem("v_ready")
        idxT_done = sem("idxT_done")
        idxT_ready = sem("idxT_ready")
        logit_done = sem("logit_done")
        relu_ready = sem("relu_ready")
        score_added = sem("score_added")
        mask_ready = sem("mask_ready")
        router_done = sem("router_done")
        gap_ready = sem("gap_ready")
        gap_exp = sem("gap_exp")
        member_ready = sem("member_ready")
        pos_done = sem("pos_done")
        sel_ready = sem("sel_ready")
        gather_done = sem("gather_done")
        info_done = sem("info_done")
        x_e_ready = sem("x_e_ready")
        e_hi_ready = sem("e_hi_ready")
        e_ready = sem("e_ready")
        x_hi_ready = sem("x_hi_ready")
        x_ready = sem("x_ready")
        midT_hi_ready = sem("midT_hi_ready")
        gate_bias_in = sem("gate_bias_in")
        experts_done = sem("experts_done")
        selT_ready = sem("selT_ready")
        y_sb_ready = sem("y_sb_ready")
        scatter_done = sem("scatter_done")
        scatter_added = sem("scatter_added")
        eps_ready = sem("eps_ready")
        final_steps = sem("final_steps")
        stat_ready = sem("stat_ready")

        W1 = Region(work, WORK - 256)
        q_tok = W1.take(NT, C_HEADS, HD)
        ctxT = q_tok.rearrange("p t h d -> p (t h d)").rearrange("p (k s) -> p k s", k=KD)
        AT_X = AT_WORK + W1.at
        kcat = W1.take(NT, C_HEADS, HD)
        ckvT = W1.take(2, S)
        qiT = W1.take(4, S)
        kiT = W1.take(S)
        score = W1.take(KW)
        assert W1.at >= NT * D + 2 * KD * S
        x_hi = at("x_hi", AT_X, [P, KD, S], F32R)
        x_lo = at("x_lo", AT_X + KD * S, [P, KD, S], F32R)
        ckr = W1.take(NT, LAT + ROPE)
        q_i = W1.take(NT, IH, HD)
        k_iw = W1.take(NT, 2 * HD + IH)
        selneg = W1.take(KW)
        kr_t = W1.take(ROPE)
        top8 = W1.take(NT, 8)
        WA1 = Region(ada, 6 * D)
        qT1 = WA1.take(8, S)
        kT1 = WA1.take(8, S)
        v1 = WA1.take(NT, D)
        W2 = Region(work, WORK, NT * D + 2 * KD * S)
        mid = W2.take(NT, FW)
        AT_M = AT_WORK + W2.at
        mT_hi = at("mT_hi", AT_M, [P, NT, 3, P], F32R)
        mT_lo = at("mT_lo", AT_M + NT * 3 * P, [P, NT, 3, P], F32R)
        W2.take(2 * NT * 3 * P)
        ada_acc = W2.take(2, ADA1)
        W3 = Region(work, WORK, NT * D)
        e_hi = at("e_hi", AT_WORK + W3.at, [P, KD, P], F32R)
        e_lo = at("e_lo", AT_WORK + W3.at + KD * P, [P, KD, P], F32R)
        W3.take(2 * KD * P)
        eT_hi = at("eT_hi", AT_WORK + W3.at, [P, 4, P], F32R)
        eT_lo = at("eT_lo", AT_WORK + W3.at + 4 * P, [P, 4, P], F32R)
        W3.take(2 * 4 * P)
        x_e = W3.take(KD, P)
        y_sb = W3.take(D)
        mid_e = W3.take(512)
        sel = W3.take(NT, P)
        selT = W3.take(S)
        info = W3.take(NT, 2)
        slot_info = W3.take(2)
        cur = W3.take(NT, 2)
        lg = W3.take(NT, E)
        top = W3.take(NT, E)
        rt = W3.take(NT, 48)
        possel = W3.take(NT, E + 1)
        comb = W3.take(NT, E + 1)
        jobs = W3.take(3 * E)
        final_y = hn

        w_ada, b_ada = A["w_ada"], A["b_ada"]
        kp = lambda ap: ap.rearrange("(k p) n -> p k n", p=P)
        stream = []
        fills = [0] * NS1
        users = {"weights": 0, "ada": 0, "split": 0}
        last = [None] * NS1

        def slot_ap(s):
            return ring[:, s, :] if s < NS0 else ring_more[:, s - NS0, :]

        def push(slot, pieces, user):
            before = last[slot]
            fills[slot] += 16 * len(pieces)
            chunks = users["split"]
            users[user] += NCI if user == "split" else 1
            last[slot] = (user, users[user])
            stream.append((slot, pieces, before))
            return slot, fills[slot], chunks

        def block_ap(slot, k, n):
            return slot_ap(slot)[:, 0:k * n].rearrange("p (k n) -> p k n", k=k)

        n_item = [0]

        def item(srcs, k, n, user):
            s = n_item[0] % NS0
            n_item[0] += 1
            got = push(s, [(block_ap(s, k, n), kp(srcs))], user)
            return (block_ap(s, k, n), got)

        def ada_item0(sec, half):
            return item(w_ada[0, :, sec * D + half * 512:sec * D + (half + 1) * 512], KD, 512, "ada")

        def e_in_item(i):
            return item(A["e_w_in"][0, :, i * 512:(i + 1) * 512], KD, 512, "weights")

        ada0 = [ada_item0(sec, half) for sec in (0, 1) for half in range(2)]
        e_in = []
        for i in range(4):
            e_in.append(e_in_item(i))
            ada0.append(ada_item0(3 + i // 2, i % 2))
        ada0 += [ada_item0(sec, half) for sec, half in ((2, 0), (2, 1), (5, 0))]
        NA0 = len(ada0)
        ada0.append(item(w_ada[0, :, 5 * D + 512:6 * D], KD, 512, "weights"))
        glu_w = item(A["s5_w_glu"][0], 4, 512, "weights")
        e_out = [item(A["e_w_out"][0, :, i * 512:(i + 1) * 512], KD, 512, "weights") for i in range(2)]

        def ff_pieces(kind, b, slot):
            if kind in ("gate", "up"):
                return [(block_ap(slot, KD, FW), kp(A["ff_w_" + kind][0])[:, :, bass.ds(b * FW, FW)])]
            if kind == "down":
                dst = block_ap(slot, 3, D)
                rows = A["ff_w_down"][0, bass.ds(b * FW, FW), :]
                return [(dst[:, 0:2, :], rows[0:2 * P, :].rearrange("(k p) n -> p k n", p=P)),
                        (dst[0:FW - 2 * P, 2, :], rows[2 * P:FW, :])]
            i = b * 2 + int(kind[-1])
            return [(block_ap(slot, KD, ADA1), kp(w_ada[1])[:, :, bass.ds(i * ADA1, ADA1)])]

        def ff_user(kind):
            return "ada" if kind.startswith("ada") else "split"

        def ff_static(kinds, b):
            got = {}
            for kind in kinds:
                s = n_item[0] % NS0
                n_item[0] += 1
                got[kind] = push(s, ff_pieces(kind, b, s), ff_user(kind))
            return got

        ff_first = ff_static(("gate", "up", "ada0", "ada1"), 0)
        static_before = list(stream)
        FFK = ("gate", "down", "up", "ada0", "ada1")
        ff_slot = {k: (n_item[0] + j) % NS0 for j, k in enumerate(FFK)}
        ff_inc = {k: 32 if k == "down" else 16 for k in FFK}
        ff_fill1 = {k: fills[ff_slot[k]] for k in FFK}
        ff_last1 = {k: last[ff_slot[k]] for k in FFK}
        ff_chunks1, ff_ada1 = users["split"], users["ada"]
        ff_chunk = {k: NCI * j for j, k in enumerate(("gate", "down", "up"))}
        CB = 3 * NCI
        for k in FFK:
            fills[ff_slot[k]] += ff_inc[k] * (FB - 1)
        users["split"] += CB * (FB - 1)
        users["ada"] += 2 * (FB - 1)
        n_item[0] += 5 * (FB - 1)
        for k in FFK:
            last[ff_slot[k]] = (("ada", users["ada"] - 1 + int(k[-1])) if k.startswith("ada")
                                else ("split", users["split"] - CB + ff_chunk[k] + NCI))
        stream.clear()
        ff_last = ff_static(("down",), FB - 1)
        o_cols = [(0, 256), (256, 384), (640, 384), (1024, 272), (1296, 512), (1808, 72)]
        o_in = [item(A["o_w_in"][0, :, a:a + n], KD, n, "split") for a, n in o_cols]
        s = n_item[0] % NS0
        n_item[0] += 1
        uk_ap = slot_ap(s)[:, 0:2 * 768].rearrange("p (k n) -> p k n", k=2)
        uv_ap = slot_ap(s)[:, 2 * 768:2 * 1792].rearrange("p (k n) -> p k n", k=2)
        ukv = push(s, [(uk_ap, A["mla_w_uk"][0].rearrange("(k p) a b -> p k (a b)", p=P)),
                       (uv_ap, A["mla_w_uv"][0].rearrange("(k p) a b -> p k (a b)", p=P))], "weights")
        o_out = [item(A["o_w_out"][0, :, i * 512:(i + 1) * 512], KD, 512, "weights") for i in range(2)]
        static_after = list(stream)
        moe_last0 = list(last)
        moe_c0 = users["split"]
        moe_fill0 = list(fills)
        moe_items = [("gate", 0), ("up", 0)]
        for b in range(1, MB):
            moe_items += [("gate", b), ("up", b), ("down", b - 1)]
        moe_items += [("down", MB - 1)]
        NI = len(moe_items)
        assert NI % NS1 == 0
        PER = NI // NS1
        CE = NCI * NI
        moe_at = {it: i for i, it in enumerate(moe_items)}

        def ff_chunk_of(n):
            return lambda slot, c: (slot_ap(slot)[:, 2 * c * n:(2 * c + 2) * n], P)

        def ff_down_chunk(slot, c):
            if c < 2:
                return slot_ap(slot)[:, c * D:(c + 1) * D], P
            n = FT[2][1]
            return slot_ap(slot)[0:n, 2 * D + (c - 2) * 512:2 * D + (c - 1) * 512], n

        def moe_chunk(slot, c):
            return slot_ap(slot)[:, c * CHUNK:(c + 1) * CHUNK], P

        used = {"weights": weights_used, "ada": ada_used, "split": lo_ready}

        block = ctx.enter_context(nc.Block())
        x_tok = A["x"].rearrange("o (t p) d -> p (o t) d", p=P)
        out_tok = out.rearrange("o (t p) d -> p (o t) d", p=P)

        s5_dt = sem("s5_dt")
        s5_x = sem("s5_x")
        s5_mag = sem("s5_mag")
        s5_r = sem("s5_r")
        s5_sin = sem("s5_sin")
        s5_den = sem("s5_den")
        s5_rden = sem("s5_rden")
        s5_pads = sem("s5_pads")
        s5_padT = sem("s5_padT")
        s5_wT_ready = sem("s5_wT_ready")
        phase_ready = sem("phase_ready")
        bu_done = sem("bu_done")
        bu_used = sem("bu_used")
        z_ready = sem("z_ready")
        post_ready = sem("post_ready")
        y_part_done = sem("y_part_done")
        y_pre = sem("y_pre")
        y_ready = sem("y_ready")
        glu_done = sem("glu_done")
        glu_tanh = sem("glu_tanh")
        proj_done = sem("proj_done")
        rope_done = sem("rope_done")
        nope_done = sem("nope_done")
        vs_ready = sem("vs_ready")
        qkT_done = sem("qkT_done")
        qkT_ready = sem("qkT_ready")
        score_done = sem("score_done")
        max_ready = sem("max_ready")
        exp_ready = sem("exp_ready")
        rden_ready = sem("rden_ready")
        p_ready = sem("p_ready")
        pT_done = sem("pT_done")
        pT_ready = sem("pT_ready")
        o_done = sem("o_done")
        cat_ready = sem("cat_ready")
        gate_done = sem("gate_done")
        silu_done = sem("silu_done")
        up_done = sem("up_done")
        mid_ready = sem("mid_ready")
        midT_done = sem("midT_done")
        midT_ready = sem("midT_ready")
        down_done = sem("down_done")

        @block.sync
        def _(sp):
            def load(entry):
                slot, pieces, before = entry
                if before is not None:
                    sp.wait_ge(used[before[0]], before[1])
                for dst, src in pieces:
                    sp.dma_start(dst, src).then_inc(fill[slot], 16)

            def small(name, src):
                at_, n = rows_at[name]
                sp.dma_start(vec_rows[at_:at_ + n, :], src.rearrange("o (k p) -> (o k) p", p=P)).then_inc(rows_in, 16)

            flat = lambda ap: ap.rearrange("o a b -> o (a b)")
            small("c", A["c"])
            small("a_re", flat(A["s5_a_re"]))
            small("a_im", flat(A["s5_a_im"]))
            small("b01", A["b_ada"][0:1, 0:2 * D])
            small("b34", A["b_ada"][0:1, 3 * D:5 * D])
            for e in static_before:
                load(e)

            def ff_load(k, b):
                for dst, src in ff_pieces(k, b - 1 if k == "down" else b, ff_slot[k]):
                    sp.dma_start(dst, src).then_inc(fill[ff_slot[k]], 16)

            for k in FFK:
                sp.wait_ge(used[ff_last1[k][0]], ff_last1[k][1])
                ff_load(k, 1)
            with sp.Fori(0, FB - 2) as i:
                for k in FFK:
                    if k.startswith("ada"):
                        sp.wait_ge(ada_used, i * 2 + (ff_ada1 + 1 + int(k[-1])))
                    else:
                        sp.wait_ge(lo_ready, i * CB + (ff_chunks1 + ff_chunk[k] + NCI))
                    ff_load(k, i + 2)
            for e in static_after:
                load(e)

            def moe_load(m, e):
                kind, b = moe_items[m]
                s = m % NS1
                if kind == "down":
                    src = A["moe_w_down"][0, bass.ds(e, 1), b * 512:(b + 1) * 512, :]
                    sp.dma_start(block_ap(s, 4, D), src.rearrange("e (k p) n -> p (e k) n", p=P)).then_inc(fill[s], 16)
                else:
                    src = A["moe_w_" + kind][0, bass.ds(e, 1), :, b * 512:(b + 1) * 512]
                    sp.dma_start(block_ap(s, KD, 512), src.rearrange("e (k p) n -> p (e k) n", p=P)).then_inc(fill[s], 16)

            for m in range(NS0):
                sp.wait_ge(used[moe_last0[m][0]], moe_last0[m][1])
                moe_load(m, 0)
            sp.wait_ge(router_done, 1)
            for m in range(NS0, NS1):
                moe_load(m, 0)

            def moe_wait(m, e):
                sp.wait_ge(lo_ready, e * CE + (moe_c0 + NCI * (m - NS1 + 1)))

            with sp.Fori(0, E - 1) as e:
                for m in range(NS1, NI):
                    moe_wait(m, e)
                    moe_load(m, e)
                for m in range(NS1):
                    moe_wait(NI + m, e)
                    moe_load(m, e + 1)
            for m in range(NS1, NI):
                moe_wait(m, E - 1)
                moe_load(m, E - 1)
            sp.wait_ge(tables_ready, 1)
            with sp.If(sp.value_load(job_tab[0:1, 2 * E:2 * E + 1], min_val=0, max_val=E) > 0):
                with sp.Fori(0, E) as e:
                    n_e = sp.value_load(job_tab[0:1, bass.ds(e, 1)], min_val=0, max_val=S)
                    with sp.If(n_e > OVER):
                        job = sp.value_load(job_tab[0:1, bass.ds(e + E, 1)], min_val=E, max_val=2 * E)
                        for m in range(NI):
                            moe_wait(m, job)
                            moe_load(m, e)
            sp.wait_ge(y_final, 2)
            sp.dma_start(out_tok, final_y).then_inc(out_stored, 16)
            sp.wait_ge(out_stored, 16)

        @block.gpsimd
        def _(pool):
            step = Steps(pool, pool_steps)
            par = lambda i: s5_p[:, i, :]

            def mul(o, a, b):
                step.wait()
                return step(nc.gpsimd.tensor_tensor(o, a, b, ALU.mult))

            def add(o, a, b):
                step.wait()
                return step(nc.gpsimd.tensor_tensor(o, a, b, ALU.add))

            def sub(o, a, b):
                step.wait()
                return step(nc.gpsimd.tensor_tensor(o, a, b, ALU.subtract))

            def affine(o, a, m, b):
                step.wait()
                return step(nc.gpsimd.tensor_scalar(o, a, m, b, ALU.mult, ALU.add))

            with nc.allow_non_contiguous_dma(reason="small parameters"):
                pool.dma_start(w_r[:, :, :], A["moe_w_router"][0].rearrange("(k p) e -> p k e", p=P)).then_inc(late_in, 16)
                pool.dma_start(b_r[:, :], A["moe_b_router"].broadcast_to([P, E])).then_inc(late_in, 16)
            pool.memset(gate_row[:, :, :], 0.0).then_inc(gate_zeroed, 1)
            pool.wait_ge(gate_zeroed, 1)
            for i, sec in enumerate((2, 5)):
                pool.dma_start(gate_row[0:1, i, :], A["b_ada"][0:1, sec * D:(sec + 1) * D]).then_inc(gate_bias_in, 16)
            step(pool.memset(b_pad, 0.0))
            pool.wait_ge(cols_ready, 1)
            pool.wait_ge(s5_dt, 1)
            step(nc.gpsimd.tensor_tensor(par(X1), par(LR), par(DT), ALU.mult))
            step.wait()
            nc.gpsimd.tensor_tensor(par(ANG), par(LI), par(DT), ALU.mult).then_inc(s5_x, 1)
            pool.wait_ge(s5_x, 1)
            affine(par(KK), par(ANG), 1 / (2 * np.pi), ROUND)
            affine(par(KK), par(KK), 1.0, -ROUND)
            sub(par(RR), par(ANG), par(ANG))
            add(par(RR), par(RR), par(ANG))
            for c in TWO_PI:
                affine(par(TT), par(KK), c, 0.0)
                sub(par(RR), par(RR), par(TT))
            step.wait()
            step(nc.gpsimd.tensor_scalar(par(RR), par(RR), PI, -PI, ALU.min, ALU.max))
            step.wait()
            nc.gpsimd.tensor_scalar(par(RH), par(RR), 0.5, 0.0, ALU.mult, ALU.add).then_inc(s5_r, 1)
            mul(par(DEN), par(LR), par(LR))
            mul(par(T2), par(LI), par(LI))
            step.wait()
            nc.gpsimd.tensor_tensor(par(DEN), par(DEN), par(T2), ALU.add).then_inc(s5_den, 1)
            pool.wait_ge(s5_sin, 1)
            pool.wait_ge(s5_r, 1)
            pool.wait_ge(s5_den, 1)
            mul(par(TT), par(SH), par(SH))
            affine(par(CS), par(TT), -2.0, 1.0)
            pool.wait_ge(s5_mag, 1)
            mul(par(AR), par(MAG), par(CS))
            mul(par(AI), par(MAG), par(SN))
            affine(par(NR), par(AR), 1.0, -1.0)
            pool.wait_ge(s5_rden, 1)
            for o, a, b, c, d, last_op in ((FR, NR, LR, AI, LI, add), (FI, AI, LR, NR, LI, sub)):
                mul(par(TT), par(a), par(b))
                mul(par(T2), par(c), par(d))
                last_op(par(o), par(TT), par(T2))
                mul(par(o), par(o), par(RDEN))
            pool.wait_ge(s5_in, 16 * 4)
            f = lambda i: par(i).unsqueeze(2).broadcast_to([P, NCH, C_S5])
            for i, (x, y, op) in enumerate(((0, 1, ALU.subtract), (1, 0, ALU.add))):
                mul(s5_t, f(FI), b_in[:, y, :, :])
                mul(b_bar[:, i, :, :], f(FR), b_in[:, x, :, :])
                step.wait()
                nc.gpsimd.tensor_tensor(b_bar[:, i, :, :], b_bar[:, i, :, :], s5_t, op).then_inc(bbar_ready, 1)
                pool.wait_ge(bbar_ready, i + 1)
            pool.wait_ge(s5_padT, 4)
            step(pool.memset(phase[:, 0, :, 0:1], 1.0))
            step(pool.memset(phase[:, 1, :, 0:1], 0.0))
            affine(par(ER), par(CS), 1.0, 0.0)
            affine(par(EI), par(SN), 1.0, 0.0)
            m = 1
            while m < S:
                er = par(ER).unsqueeze(2).broadcast_to([P, NCH, m])
                ei = par(EI).unsqueeze(2).broadcast_to([P, NCH, m])
                c0, s0 = phase[:, 0, :, 0:m], phase[:, 1, :, 0:m]
                c1, s1 = phase[:, 0, :, m:2 * m], phase[:, 1, :, m:2 * m]
                t = s5_tmp[:, :, 0:m]
                mul(t, s0, ei)
                mul(c1, c0, er)
                sub(c1, c1, t)
                mul(t, c0, ei)
                mul(s1, s0, er)
                add(s1, s1, t)
                mul(par(TT), par(EI), par(EI))
                mul(par(T2), par(ER), par(EI))
                mul(par(ER), par(ER), par(ER))
                sub(par(ER), par(ER), par(TT))
                affine(par(EI), par(T2), 2.0, 0.0)
                m *= 2
            step.wait()
            pool.memset(s5_small[:, 0:1], 0.0).then_inc(phase_ready, 1)
            for j in range(NCH):
                pool.wait_ge(z_ready, j + 1)
                if j >= 2:
                    pool.wait_ge(y_part_done, j - 1)
                z = zbuf[:, j % 2]
                o = post[:, j % 2]
                if j == 0:
                    pool.wait_ge(phase_ready, 1)
                    pool.wait_ge(qkT_done, 4)
                for i in range(2):
                    w = nc.gpsimd.tensor_tensor(o[:, i], z, phase[:, i, j, :].unsqueeze(1).broadcast_to([P, 2, S]), ALU.mult)
                w.then_inc(post_ready, 1)
            pool.wait_ge(h_ready, 4)
            pool.memset(ada[:, :], 0.0).then_inc(ada_zeroed, 1)
            pool.wait_ge(ada_zeroed, 1)
            pool.dma_start(ada[0:1, :], A["b_ada"][1:2, :]).then_inc(bias_in, 16)

            def ada_item(ap, j):
                if j == 0:
                    step(nc.gpsimd.tensor_tensor(ap, ap, c_col[:, :].unsqueeze(2).broadcast_to([P, KD, ADA1]), ALU.mult))
                    step.wait()
                half = KD // 2
                step(nc.gpsimd.tensor_tensor(ap[:, 0:half, :], ap[:, 0:half, :], ap[:, half:, :], ALU.add))
                half = KD // 4
                add(ap[:, 0:half, :], ap[:, 0:half, :], ap[:, half:2 * half, :])
                step.wait()
                nc.gpsimd.tensor_tensor(ada_acc[:, j, :], ap[:, 0, :], ap[:, 1, :], ALU.add).then_inc(ada_used, 1)

            for i in range(2):
                slot, value, _ = ff_first[f"ada{i}"]
                pool.wait_ge(*((ada_scaled, 1) if i else (fill[slot], value)))
                ada_item(block_ap(slot, KD, ADA1), i)
            with pool.Fori(0, FB - 1) as i:
                step.enter(i, 0, 2 * 2 + 1)
                for j in range(2):
                    k = f"ada{j}"
                    if j == 0:
                        pool.wait_ge(fill[ff_slot[k]], i * 16 + (ff_fill1[k] + 16))
                    else:
                        pool.wait_ge(ada_scaled, i + 2)
                    pool.wait_ge(ada_added, i * 2 + (j + 1))
                    ada_item(block_ap(ff_slot[k], KD, ADA1), j)
            step.leave(0, FB - 1)
            pool.wait_ge(h_ready, 12)
            pool.dma_start(gate_row[:, 0, :], A["g_final"].unsqueeze(0).broadcast_to([P, D])).then_inc(late_in, 16)

        @block.tensor
        def _(pe):
            mm = nc.tensor.matmul
            pending = [False]

            def release(w):
                if pending[0]:
                    w.then_inc(weights_used, 1)
                    pending[0] = False

            def mm3(o, xh, xl, wh, wl, start, stop):
                mm(o, xh, wh, start=start, stop=False)
                mm(o, xh, wl, start=False, stop=False)
                return mm(o, xl, wh, start=False, stop=stop)

            def tr(o, i):
                n = i.shape[0]
                return nc.tensor.transpose(o, i, ident[0:n, 0:n])

            def s5_transposes():
                pe.wait_ge(s5_pads, 8)
                for i, bank in enumerate((5, 6, 7, 4)):
                    pad = (b_pad, c_pad)[i // 2]
                    for t in range(4):
                        w = tr(ps[bank][:, t * P:(t + 1) * P], pad[:, i % 2, t, :])
                    w.then_inc(s5_padT, 1)

            def mod0_columns(bank):
                for k in range(2 * KD):
                    w = mm(ps[bank][:, k:k + 1], acc0[:, k * P:(k + 1) * P], ones[:, 0:1], start=True, stop=True)
                w.then_inc(mod_summed, 1)

            def mod1():
                pe.wait_ge(ada_added, NA1)
                pe.wait_ge(h_ready, 8)
                for i, sec in enumerate((0, 1, 3, 4)):
                    for k in range(KD):
                        w = mm(ps[4][:, i * KD + k:i * KD + k + 1], ada[:, sec * D + k * P:sec * D + (k + 1) * P],
                               ones[:, 0:1], start=True, stop=True)
                w.then_inc(mod_summed, 1)
                for i, (sec, half, bank) in enumerate(((2, 0, 5), (2, 1, 6), (5, 0, 7), (5, 1, 5))):
                    if i == 3:
                        pe.wait_ge(gate_ready, 5)
                    a = sec * D + half * 512
                    mm(ps[bank][:, :], ones, ada[:, a:a + 512], start=True, stop=True).then_inc(mod_summed, 1)

            def norm(n):
                for t in range(NT):
                    pe.wait_ge(hn_ready, NT * n + t + 1)
                    for k in range(KD):
                        c = (k % 2) * S + t * P
                        w = tr(ps[k // 2][:, c:c + P], hn[:, t, k * P:(k + 1) * P])
                        if t == 0 and k == 0:
                            release(w)
                        if t == NT - 1 and k % 2:
                            w.then_inc(hnT_done, 1)

            def arrived(got):
                pe.wait_ge(fill[got[0]], got[1])

            def project(w_item, n, banks, xT, waits=(), last_sem=None):
                ap, got = w_item
                arrived(got)
                for t in range(NT):
                    if waits:
                        pe.wait_ge(*waits[t])
                    for k in range(KD):
                        w = mm(ps[banks[t]][:, 0:n], xT[:, k, t * P:(t + 1) * P], ap[:, k, 0:n],
                               start=k == 0, stop=k == KD - 1)
                        if t == 0 and k == 0 and pending[0]:
                            w.then_inc(weights_used, 1)
                            pending[0] = False
                    w.then_inc(last_sem, 1)
                pending[0] = True

            def scores(n, qT_, kT_, hh):
                r = slice(HD * (hh % 2), HD * (hh % 2) + HD)
                if n >= 2:
                    pe.wait_ge(max_ready, n - 1)
                for t in range(NT):
                    w = mm(ps[n % 2][:, KOFF[t]:KOFF[t] + KEYS[t]], qT_[r, hh // 2, t * P:(t + 1) * P],
                           kT_[r, hh // 2, 0:KEYS[t]], start=True, stop=True)
                    if t == 0:
                        release(w)
                w.then_inc(score_done, 1)

            def probsT(n):
                pe.wait_ge(p_ready, n + 1)
                if n >= 2:
                    pe.wait_ge(pT_ready, n - 1)
                for i in range(3):
                    w = tr(ps[2 + n % 2][:, i * P:(i + 1) * P], sm[:, n % 3, i * P:(i + 1) * P])
                w.then_inc(pT_done, 1)

            def weigh(n, v, hh, cat0):
                pe.wait_ge(pT_ready, n + 1)
                pair = hh // 2
                if pair >= 2 and hh % 2 == 0:
                    pe.wait_ge(cat_ready, cat0 + pair - 1)
                r = slice(HD * (hh % 2), HD * (hh % 2) + HD)
                o = ps[4 + pair % 2]
                p_ = pT[:, n % 2, :]
                hc = slice(hh * HD, (hh + 1) * HD)
                mm(o[r, 0:P], v[:, 0, hc], p_[:, 0:P], start=True, stop=True)
                mm(o[r, P:2 * P], v[:, 0, hc], p_[:, P:2 * P], start=True, stop=False)
                mm(o[r, P:2 * P], v[:, 1, hc], p_[:, 2 * P:3 * P], start=False, stop=True).then_inc(o_done, 1)

            pe.wait_ge(rows_in, 16 * len(rows_at))
            pe.wait_ge(ident_in, 16)
            tr(ps[7][:, 0:n_rows], vec_rows[0:n_rows, :]).then_inc(rows_done, 1)
            pe.wait_ge(consts_in, 16)
            norm(0)
            pe.wait_ge(ada_used, 4)
            mod0_columns(4)
            pe.wait_ge(cols_ready, 1)
            pe.wait_ge(mod_ready, 1)
            s5_transposes()
            pe.wait_ge(uT_ready, 8)
            project(e_in[0], 512, (0, 1), uT, (), proj_done)
            project(e_in[1], 512, (2, 3), uT, (), proj_done)
            pe.wait_ge(s5_wT_ready, 5)
            project(e_in[2], 512, (4, 5), uT, (), proj_done)
            ap, got = e_in[3]
            arrived(got)
            for c in range(4):
                for k in range(KD):
                    w = mm(ps[6 + c // 2][:, (c % 2) * S:(c % 2 + 1) * S], ap[:, k, c * P:(c + 1) * P], uT[:, k, :],
                           start=k == 0, stop=k == KD - 1)
                    release(w)
                if c % 2:
                    w.then_inc(proj_done, 1)
            pending[0] = True
            pe.wait_ge(rope_done, 4)
            pe.wait_ge(nope_done, 4)
            for i in range(2):
                for pr in range(4):
                    for t in range(NT):
                        w = tr(ps[2 * i + pr // 2][:, (pr % 2) * S + t * P:(pr % 2) * S + (t + 1) * P],
                               qk_tok[:, t, i * 512 + pr * P:i * 512 + (pr + 1) * P])
                        release(w)
                    if pr % 2:
                        w.then_inc(qkT_done, 1)
            pe.wait_ge(qkT_ready, 4)
            scores(0, qT, kT, 0)
            scores(1, qT, kT, 1)
            pe.wait_ge(vs_ready, 4)
            pe.wait_ge(ada_used, 8)
            mod0_columns(7)
            ap, got = ada0[NA0]
            arrived(got)
            for k in range(KD):
                w = mm(ps[4][:, :], c_col[:, k:k + 1].broadcast_to([P, P]), ap[:, k, :], start=k == 0, stop=False)
                release(w)
            pending[0] = True
            pe.wait_ge(gate_bias_in, 16 * 2)
            mm(ps[4][:, :], ones, gate_row[:, 1, 512:1024], start=False, stop=True).then_inc(mod_summed, 1)
            for i in range(3):
                pe.wait_ge(ada_used, 9 + i)
                if i == 2:
                    pe.wait_ge(mod_ready, 2)
                mm(ps[5 + i][:, :], ones, gate_row[:, i // 2, (i % 2) * 512:(i % 2 + 1) * 512], start=True,
                   stop=True).then_inc(mod_summed, 1)
            pe.wait_ge(gate_ready, 4)

            def drive(j):
                if j == 0:
                    pe.wait_ge(s5_wT_ready, 5)
                else:
                    pe.wait_ge(bu_used, j)
                r = slice(32 * (j % 4), 32 * (j % 4) + 32)
                for i in range(2):
                    w = mm(ps[6][:, i * S:(i + 1) * S], s5_bT[r, i, j // 4, :], s_inT[r, j // 4, :], start=True, stop=True,
                           tile_position=(32 * (j % 4), 0))
                w.then_inc(bu_done, 1)

            def read_out(j):
                pe.wait_ge(post_ready, j + 1)
                t = j // 4
                if j % 4 == 0 and t >= 1:
                    pe.wait_ge(y_pre, t)
                r = slice(32 * (j % 4), 32 * (j % 4) + 32)
                o = ps[7][r, (t % 2) * S:(t % 2 + 1) * S]
                x = post[:, j % 2]
                for i, (c, a, b) in enumerate(((0, 0, 0), (1, 1, 1), (2, 1, 0), (2, 0, 1))):
                    w = mm(o, s5_cT[:, c, t, r], x[:, a, b, :], start=i == 0, stop=i == 3,
                           tile_position=(0, 32 * (j % 4)))
                w.then_inc(y_part_done, 1)

            for hh in range(A_HEADS):
                drive(2 * hh)
                if hh + 2 < A_HEADS:
                    scores(hh + 2, qT, kT, hh + 2)
                if hh:
                    weigh(hh - 1, v_tok, hh - 1, 0)
                drive(2 * hh + 1)
                if hh:
                    read_out(2 * hh - 2)
                probsT(hh)
                if hh:
                    read_out(2 * hh - 1)
            read_out(NCH - 2)
            weigh(A_HEADS - 1, v_tok, A_HEADS - 1, 0)
            read_out(NCH - 1)
            pe.wait_ge(y_ready, 4)
            pe.wait_ge(max_ready, A_HEADS)
            ap, got = glu_w
            arrived(got)
            for c in range(4):
                for k in range(4):
                    w = mm(ps[c // 2][:, (c % 2) * S:(c % 2 + 1) * S], ap[:, k, c * P:(c + 1) * P], s5_y[:, k, :],
                           start=k == 0, stop=k == 3)
                w.then_inc(glu_done, 1)
            pending[0] = True
            pe.wait_ge(cat_ready, 8)
            for n in range(2):
                project(e_out[n], 512, (4 + 2 * n, 5 + 2 * n), catT, (), mix_out_done)

            norm(1)

            def chunk_mm(q, c, outs, xh, xl, ks, rhs, n, first, final, signal=True):
                pe.wait_ge(lo_ready, q + 1)
                for t, o in enumerate(outs):
                    for j, k in enumerate(ks):
                        w = mm3(o, xh(k, t), xl(k, t), rhs(w_hi, c, j), rhs(w_lo, c, j),
                                first and j == 0, final and j == len(ks) - 1)
                w.then_inc(chunk_done, 1)

            def halves(n):
                return lambda buf, c, j: buf[:, c, j * n:(j + 1) * n]

            xh = lambda k, t: x_hi[:, k, t * P:(t + 1) * P]
            xl = lambda k, t: x_lo[:, k, t * P:(t + 1) * P]

            def rows(q, banks, n, chunks, norm_n=None):
                for c in chunks:
                    if norm_n is not None:
                        pe.wait_ge(x_ready, KD * norm_n + 2 * c + 2)
                    chunk_mm(q + c, c, [ps[i][:, 0:n] for i in banks], xh, xl, (2 * c, 2 * c + 1), halves(n), n,
                             c == 0, c == NCI - 1)

            def ff_T(u0):
                for t in range(NT):
                    pe.wait_ge(mid_ready, u0 + t + 1)
                    for i, (a, n) in enumerate(FT):
                        w = tr(ps[2 + t][0:n, i * P:(i + 1) * P], mid[:, t, a:a + n])
                    w.then_inc(midT_done, 1)

            def ff_down(q, u0, first, final):
                pe.wait_ge(midT_ready, u0 + 2)
                for c in range(NCI):
                    i = min(c, 2)
                    n = FT[i][1]
                    pe.wait_ge(lo_ready, q + c + 1)
                    for half in ((0, 1), (0, 1), (0,), (1,))[c]:
                        a = half * 512 if c < 2 else 0
                        for t in range(NT):
                            w = mm3(ps[4 + 2 * t + half][:, :], mT_hi[0:n, t, i, :], mT_lo[0:n, t, i, :],
                                    w_hi[0:n, c, a:a + 512], w_lo[0:n, c, a:a + 512], first and c == 0, final and c >= 2)
                    w.then_inc(chunk_done, 1)

            def ff_block(i, first):
                q = i * CB + ff_chunks1
                u0 = i * NT
                pe.wait_ge(silu_done, u0 + 2)
                rows(q, (0, 1), FW, (0, 1))
                ff_T(u0)
                rows(q, (0, 1), FW, (2, 3))
                ff_down(q + NCI, u0, first, False)
                rows(q + 2 * NCI, (2, 3), FW, range(NCI))

            rows(ff_first["gate"][2], (0, 1), FW, range(NCI), 0)
            rows(ff_first["up"][2], (2, 3), FW, range(NCI))
            ff_block(0, True)
            with pe.Fori(1, FB - 1) as i:
                ff_block(i, False)
            ff_T((FB - 1) * NT)
            ff_down(ff_last["down"][2], (FB - 1) * NT, False, True)

            mod1()
            norm(2)
            pe.wait_ge(mod_ready, 3)
            pe.wait_ge(gate_ready, 8)
            for j, banks in enumerate(((0, 1), (2, 3), (4, 5), (6, 7), (0, 1), (2, 3))):
                if j == 4:
                    pe.wait_ge(rope_done, 6)
                if j == 5:
                    pe.wait_ge(nope_done, 6)
                rows(o_in[j][1][2], banks, o_cols[j][1], range(NCI), 1 if j == 0 else None)
            pe.wait_ge(nope_done, 8)
            for t in range(NT):
                pe.wait_ge(ckv_ready, t + 1)
                for k in range(2):
                    w = tr(ps[4][:, k * S + t * P:k * S + (t + 1) * P], ckr[:, t, k * P:(k + 1) * P])
            w.then_inc(ckvT_done, 1)
            pe.wait_ge(ckvT_ready, 2)
            pe.wait_ge(nope_done, 10)
            arrived(ukv[:2])
            for i in range(4):
                t, half = i // 2, i % 2
                for k in range(2):
                    w = mm(ps[4 + i][:, 0:384], ckvT[:, k, t * P:(t + 1) * P], uk_ap[:, k, half * 384:(half + 1) * 384],
                           start=k == 0, stop=k == 1)
                    release(w)
                w.then_inc(kv_done, 1)
            pe.wait_ge(rope_done, 10)
            pe.wait_ge(nope_done, 12)
            for i in range(4):
                t, half = i // 2, i % 2
                for k in range(2):
                    w = mm(ps[i][:, :], ckvT[:, k, t * P:(t + 1) * P], uv_ap[:, k, half * 512:(half + 1) * 512],
                           start=k == 0, stop=k == 1)
                w.then_inc(kv_done, 1)
            pending[0] = True
            pe.wait_ge(kn_ready, 4)
            for pr in range(4):
                for t in range(NT):
                    w = tr(ps[4 + pr // 2][:, (pr % 2) * S + t * P:(pr % 2) * S + (t + 1) * P],
                           q_i[:, t, 2 * pr:2 * pr + 2, :].rearrange("p h d -> p (h d)"))
                    release(w)
                if pr % 2:
                    w.then_inc(idxT_done, 1)
            for t in range(NT):
                w = tr(ps[6][:, t * P:(t + 1) * P], k_iw[:, t, 0:2 * HD])
            w.then_inc(idxT_done, 1)
            pe.wait_ge(idxT_ready, 3)
            pe.wait_ge(v_ready, 4)
            for i in range(IH):
                r = slice(HD * (i % 2), HD * (i % 2) + HD)
                if i >= 2:
                    pe.wait_ge(relu_ready, i - 1)
                for t in range(NT):
                    w = mm(ps[i % 2][:, KOFF[t]:KOFF[t] + KEYS[t]], qiT[r, i // 2, t * P:(t + 1) * P], kiT[r, 0:KEYS[t]],
                           start=True, stop=True)
                w.then_inc(logit_done, 1)
            pe.wait_ge(rope_done, 12)
            for i, src in enumerate((q_tok, kcat)):
                for pr in range(8):
                    if i and pr % 2 == 0:
                        pe.wait_ge(qkT_ready, 4 + pr // 2 + 1)
                    for t in range(NT):
                        w = tr(ps[4 + pr // 2][:, (pr % 2) * S + t * P:(pr % 2) * S + (t + 1) * P],
                               src[:, t, 2 * pr:2 * pr + 2, :].rearrange("p h d -> p (h d)"))
                    if pr % 2:
                        w.then_inc(qkT_done, 1)
            pe.wait_ge(qkT_ready, 12)
            pe.wait_ge(relu_ready, IH)
            scores(A_HEADS, qT1, kT1, 0)
            scores(A_HEADS + 1, qT1, kT1, 1)
            for hh in range(C_HEADS):
                n = A_HEADS + hh
                if hh + 2 < C_HEADS:
                    scores(n + 2, qT1, kT1, hh + 2)
                if hh:
                    weigh(n - 1, v1, hh - 1, 8)
                probsT(n)
            weigh(A_HEADS + C_HEADS - 1, v1, C_HEADS - 1, 8)
            pe.wait_ge(cat_ready, 16)
            for n in range(2):
                project(o_out[n], 512, (4 + 2 * n, 5 + 2 * n), ctxT, (), mix_out_done)

            norm(3)
            pe.wait_ge(uT_ready, 32)
            pe.wait_ge(late_in, 16 * 2)
            for t in range(NT):
                for k in range(KD):
                    w = mm(ps[4][:, t * E:(t + 1) * E], uT[:, k, t * P:(t + 1) * P], w_r[:, k, :],
                           start=k == 0, stop=k == KD - 1)
                    release(w)
            w.then_inc(router_done, 1)
            pe.wait_ge(member_ready, 1)
            member = lambda t: rt[:, t, 16:24]
            mm(ps[5][:, 0:E], tri, member(0), start=True, stop=True)
            mm(ps[5][:, E:2 * E], tri, member(1), start=True, stop=False)
            mm(ps[5][:, E:2 * E], ones, member(0), start=False, stop=True)
            mm(ps[5][:, 2 * E:3 * E], ones, member(0), start=True, stop=False)
            mm(ps[5][:, 2 * E:3 * E], ones, member(1), start=False, stop=True).then_inc(pos_done, 1)

            def gather(g):
                pe.wait_ge(sel_ready, g + 1)
                for bank in range(2):
                    for k in range(4):
                        kk = 4 * bank + k
                        for t in range(NT):
                            w = mm(ps[6 + bank][:, k * P:(k + 1) * P], hn[:, t, kk * P:(kk + 1) * P], sel[:, t, :],
                                   start=t == 0, stop=t == NT - 1)
                    w.then_inc(gather_done, 1)
                for t in range(NT):
                    w = mm(ps[3][:, 0:2], sel[:, t, :], info[:, t, :], start=t == 0, stop=t == NT - 1)
                w.then_inc(info_done, 1)

            eh = lambda k, t: e_hi[:, k, :]
            el = lambda k, t: e_lo[:, k, :]
            UF = FB * NT

            def expert(job, g, gather_next):
                def unit(b):
                    return job * MB + (UF + b)

                def chunks(kind, b):
                    return job * CE + (moe_c0 + NCI * moe_at[kind, b])

                def project(kind, b, bank):
                    for c in range(NCI):
                        chunk_mm(chunks(kind, b) + c, c, [ps[bank][:, :]], eh, el, (2 * c, 2 * c + 1), halves(512), 512,
                                 c == 0, c == NCI - 1)

                def transposes(b):
                    pe.wait_ge(mid_ready, unit(b) + 1)
                    for i in range(4):
                        w = tr(ps[2][:, i * P:(i + 1) * P], mid_e[:, i * P:(i + 1) * P])
                    w.then_inc(midT_done, 1)

                def down(b):
                    pe.wait_ge(midT_ready, unit(b) + 1)
                    for c in range(NCI):
                        pe.wait_ge(lo_ready, chunks("down", b) + (c + 1))
                        for half in range(2):
                            n = slice(half * 512, (half + 1) * 512)
                            w = mm3(ps[4 + half][:, :], eT_hi[:, c, :], eT_lo[:, c, :], w_hi[:, c, n], w_lo[:, c, n],
                                    b == 0 and c == 0, b == MB - 1 and c == NCI - 1)
                        w.then_inc(chunk_done, 1)

                pe.wait_ge(e_ready, g * 2 + 2)
                for b in range(MB):
                    pe.wait_ge(silu_done, unit(b))
                    project("gate", b, 0)
                    if b:
                        transposes(b - 1)
                    else:
                        pe.wait_ge(mid_ready, unit(0))
                    project("up", b, 1)
                    if b:
                        down(b - 1)
                if gather_next:
                    gather(g + 1)
                transposes(MB - 1)
                down(MB - 1)
                pe.wait_ge(y_sb_ready, job * 2 + 2)
                pe.wait_ge(selT_ready, job + 1)
                if gather_next:
                    pe.wait_ge(e_ready, g * 2 + 4)
                for i in range(4):
                    t, half = i // 2, i % 2
                    mm(ps[4 + i][:, :], selT[:, t * P:(t + 1) * P], y_sb[:, half * 512:(half + 1) * 512],
                       start=True, stop=True).then_inc(scatter_done, 1)
                pe.wait_ge(scatter_added, job * 4 + 4)

            gather(0)
            with pe.Fori(0, E) as e:
                expert(e, e, True)
            pe.wait_ge(tables_ready, 1)
            with pe.If(pe.value_load(job_tab[0:1, 2 * E:2 * E + 1], min_val=0, max_val=E) > 0):
                with pe.Fori(0, E) as e:
                    n_e = pe.value_load(job_tab[0:1, bass.ds(e, 1)], min_val=0, max_val=S)
                    with pe.If(n_e > OVER):
                        job = pe.value_load(job_tab[0:1, bass.ds(e + E, 1)], min_val=E, max_val=2 * E)
                        gather(job + 1)
                        expert(job, job + 1, False)

        @block.scalar
        def _(act):
            fn = nc.scalar.activation
            par = lambda i: s5_p[:, i, :]
            step = Steps(act, act_steps)

            def small(name, src):
                at_, n = rows_at[name]
                act.dma_start(vec_rows[at_:at_ + n, :], src.rearrange("o (k p) -> (o k) p", p=P)).then_inc(rows_in, 16)

            act.dma_start(ident, A["consts"][:, C_ID:C_ID + P]).then_inc(ident_in, 16)
            small("g_mix", A["g_mix"].rearrange("l (o d) -> o (l d)", o=1))
            small("g_ffn", A["g_ffn"].rearrange("l (o d) -> o (l d)", o=1))
            small("g_kv", A["mla_g_kv"])
            small("d", A["s5_d"].rearrange("o g c -> o (g c)"))
            small("b_glu", A["s5_b_glu"])
            act.dma_start(log_dt, A["s5_log_dt"].broadcast_to([P, G_S5])).then_inc(dt_in, 16)
            act.dma_start(h[:, :, :], x_tok).then_inc(x_in, 16)
            with nc.allow_non_contiguous_dma(reason="small parameters"):
                for i, n in enumerate(("re", "im")):
                    act.dma_start(b_in[:, i, :, :], A["s5_b_" + n].rearrange("o (j g) p c -> (g p) (o j) c", g=2)).then_inc(s5_in, 16)
                    act.dma_start(c_in[:, i, :, :], A["s5_c_" + n].rearrange("o (t g) c p -> (g c) (o t) p", t=4)).then_inc(s5_in, 16)
            act.dma_start(cst[:, P:], A["consts"][:, P:]).then_inc(consts_in, 16)
            act.wait_ge(rows_done, 1)
            turned = lambda name, n=None: ps[7][:, rows_at[name][0]:rows_at[name][0] + (n or rows_at[name][1])]
            fn(c_col[:, :], turned("c"), ACT.Silu).then_inc(c_ready, 1)
            fn(s5_p[:, LR:LI + 1, :], turned("a_re", 2 * NCH).rearrange("p (a j) -> p a j", a=2), ACT.Copy)
            fn(bg_col[:, :, :], turned("b01", 8 * KD).rearrange("p (a k) -> p a k", a=8), ACT.Copy)
            fn(g_kv[:, :], turned("g_kv"), ACT.Copy)
            fn(s5_d[:, :], turned("d"), ACT.Copy)
            fn(s5_bg[:, :], turned("b_glu"), ACT.Copy, scale=0.5).then_inc(cols_ready, 1)
            act.wait_ge(dt_in, 16)
            for g in range(2):
                rows_g = slice(g * P_S5, (g + 1) * P_S5)
                w = fn(s5_p[rows_g, DT, :], log_dt[rows_g, :].rearrange("p (j g) -> p g j", g=2)[:, g, :], ACT.Exp)
            w.then_inc(s5_dt, 1)
            act.wait_ge(s5_x, 1)
            fn(par(MAG), par(X1), ACT.Exp).then_inc(s5_mag, 1)
            act.wait_ge(s5_r, 1)
            fn(par(SN), par(RR), ACT.Sin)
            fn(par(SH), par(RH), ACT.Sin).then_inc(s5_sin, 1)

            def pads():
                act.wait_ge(s5_in, 16 * 4)
                act.wait_ge(consts_in, 16)
                for i in range(2):
                    for g in range(2):
                        fn(c_pad[:, i, :, g * P_S5:(g + 1) * P_S5], c_in[:, i, :, :], ACT.Copy,
                           scale=cst[:, C_HM + g:C_HM + g + 1]).then_inc(s5_pads, 1)
                for i in range(2):
                    act.wait_ge(bbar_ready, i + 1)
                    for g in range(2):
                        rows_g = slice(g * P_S5, (g + 1) * P_S5)
                        fn(b_pad[rows_g, i, :, :].rearrange("p t (j x) -> p (t j) x", x=2 * C_S5)[:, :, g * C_S5:(g + 1) * C_S5],
                           b_bar[rows_g, i, :, :], ACT.Copy).then_inc(s5_pads, 1)

            def s5_weights():
                for i, (dst, scale) in enumerate(((s5_bT[:, 0], 1.0), (s5_bT[:, 1], 1.0), (s5_cT[:, 0], 1.0),
                                                  (s5_cT[:, 1], -1.0), (s5_cT[:, 2], -1.0))):
                    bank = ps[(5, 6, 7, 7, 4)[i]]
                    act.wait_ge(s5_padT, (1, 2, 3, 3, 4)[i])
                    fn(dst, bank[:, :].rearrange("p (t q) -> p t q", t=4), ACT.Copy, scale=scale).then_inc(s5_wT_ready, 1)

            def gates0():
                for i, g in enumerate((3, 0, 1, 2)):
                    act.wait_ge(mod_summed, 3 + i)
                    fn(gate_row[:, g // 2, (g % 2) * 512:(g % 2 + 1) * 512], ps[4 + i][:, :], ACT.Copy).then_inc(gate_ready, 1)

            def gates1():
                for i, (row, half, bank) in enumerate(((0, 0, 5), (0, 1, 6), (1, 0, 7), (1, 1, 5))):
                    act.wait_ge(mod_summed, 8 + i)
                    fn(gate_row[:, row, half * 512:(half + 1) * 512], ps[bank][:, :], ACT.Copy).then_inc(gate_ready, 1)

            def rms(src, junk, width, n):
                for t in range(NT):
                    w = fn(junk(t), src(t), ACT.Square, accum_out=stat[:, t:t + 1])
                    step(w)
                step.wait()
                fn(stat[:, 2:4], stat[:, 0:2], ACT.Sqrt, bias=eps[:, 0:1], scale=1.0 / width).then_inc(rms_ready, 1)

            def norm_stats(n):
                if n == 0:
                    act.wait_ge(x_in, 16)
                elif n < 4:
                    act.wait_ge(h_ready, 4 * n)
                else:
                    act.wait_ge(experts_done, 1)
                act.wait_ge(eps_ready, 1)
                rms(lambda t: h[:, t, :], lambda t: hn[:, t, :], D, n)

            def norm_out(n):
                m = n % 2
                act.wait_ge(mod_ready, (1, 2, 3, 3)[n])
                for k in (0, 1, 4, 5):
                    act.wait_ge(hnT_done, 4 * n + k // 2 + 1)
                    fn(uT[:, k, :], ps[k // 2][:, (k % 2) * S:(k % 2 + 1) * S], ACT.Identity, scale=mod_a[:, m, k:k + 1],
                       bias=mod_b[:, m, k:k + 1]).then_inc(uT_ready, 1)

            def norm_hi(n):
                for k in range(KD):
                    act.wait_ge(uT_ready, KD * n + k + 1)
                    fn(x_hi[:, k, :], uT[:, k, :], ACT.Copy).then_inc(x_hi_ready, 1)

            def high(q, c, src, n=P):
                if not isinstance(q, int) or q >= NB:
                    act.wait_ge(chunk_done, q + 1 - NB)
                w = w_hi[0:n, c, 0:src.free_size()]
                fn(w, src, ACT.Copy).then_inc(hi_ready, 1)

            def arrived(slot, value):
                act.wait_ge(fill[slot], value)

            def heads(ap, n, width=HD):
                return ap.rearrange("p (h d) -> p h d", h=n)

            def exps(n, l1):
                act.wait_ge(max_ready, n + 1)
                q = n % 3
                for t in range(NT):
                    x = sm[:, q, KOFF[t]:KOFF[t] + KEYS[t]]
                    w = fn(x, x, ACT.Exp, scale=SC, bias=stat[:, 12 + 2 * q + t:13 + 2 * q + t],
                           **({"accum_out": stat[:, 18 + 2 * q + t:19 + 2 * q + t]} if l1 else {}))
                w.then_inc(exp_ready, 1)

            def probs(n):
                act.wait_ge(rden_ready, n + 1)
                q = n % 3
                for t in range(NT):
                    x = sm[:, q, KOFF[t]:KOFF[t] + KEYS[t]]
                    w = fn(x, x, ACT.Copy, scale=stat[:, 24 + 2 * q + t:25 + 2 * q + t])
                w.then_inc(p_ready, 1)

            def head_out(n, dst, pair):
                act.wait_ge(o_done, n + 1)
                fn(dst[:, pair, :], ps[4 + pair % 2][:, 0:S], ACT.Copy).then_inc(cat_ready, 1)

            def probsT_out(n):
                act.wait_ge(pT_done, n + 1)
                if n >= 2:
                    act.wait_ge(o_done, n - 1)
                fn(pT[:, n % 2, :], ps[2 + n % 2][:, 0:KW], ACT.Copy).then_inc(pT_ready, 1)

            norm_stats(0)
            pads()
            norm_out(0)
            s5_weights()
            for i in range(4):
                act.wait_ge(proj_done, i + 1)
                t, a = i % 2, (i // 2) * 512
                fn(heads(qk_tok[:, t, a:a + 512], 8)[:, :, ROPE:], heads(ps[i][:, :], 8)[:, :, ROPE:],
                   ACT.Copy).then_inc(nope_done, 1)
            for t in range(NT):
                act.wait_ge(proj_done, 5 + t)
                fn(v_tok[:, t, :], ps[4 + t][:, :], ACT.Copy).then_inc(vs_ready, 1)
            for i in range(2):
                act.wait_ge(proj_done, 7 + i)
                fn(s_inT[:, 2 * i:2 * i + 2, :], ps[6 + i][:, :].rearrange("p (c s) -> p c s", c=2), ACT.Copy).then_inc(vs_ready, 1)
            for i, dst in ((1, qT), (3, kT)):
                act.wait_ge(qkT_done, i + 1)
                fn(dst[:, 2:4, :], ps[i][:, :].rearrange("p (c s) -> p c s", c=2), ACT.Copy).then_inc(qkT_ready, 1)
            exps(0, False)
            gates0()
            for hh in range(A_HEADS):
                if hh + 1 < A_HEADS:
                    exps(hh + 1, False)
                probs(hh)
                if hh and hh % 2 == 0:
                    head_out(hh - 1, catT, hh // 2 - 1)
                probsT_out(hh)
            head_out(A_HEADS - 1, catT, A_HEADS // 2 - 1)
            act.wait_ge(y_pre, 4)
            for t in range(4):
                fn(s5_y[:, t, :], s5_y[:, t, :], ACT.Gelu_apprx_tanh).then_inc(y_ready, 1)
            th = lambda c: hn.rearrange("p t d -> p (t d)")[:, c * S:(c + 1) * S]
            act.wait_ge(y_part_done, NCH)
            for c in range(4):
                act.wait_ge(glu_done, 2 * (c // 2) + 2)
                fn(th(c), ps[c // 2][:, (c % 2) * S:(c % 2 + 1) * S], ACT.Tanh, scale=0.5,
                   bias=s5_bg[:, c:c + 1]).then_inc(glu_tanh, 1)

            def item_high(q, slot, value, chunk, chunks=range(NCI)):
                arrived(slot, value)
                for c in chunks:
                    high(q + c, c, *chunk(slot, c))

            def silus(u0):
                for t in range(NT):
                    fn(mid[:, t, :], ps[t][:, 0:FW], ACT.Silu).then_inc(silu_done, 1)

            def midT_high(u0):
                for t in range(NT):
                    act.wait_ge(midT_done, u0 + t + 1)
                    fn(mT_hi[:, t, 0:2, :], ps[2 + t][:, 0:2 * P].rearrange("p (i t) -> p i t", i=2), ACT.Copy)
                    n = FT[2][1]
                    fn(mT_hi[0:n, t, 2, :], ps[2 + t][0:n, 2 * P:3 * P], ACT.Copy).then_inc(midT_hi_ready, 1)

            norm_stats(1)
            act.wait_ge(h_ready, 4)
            item_high(ff_first["gate"][2], *ff_first["gate"][:2], ff_chunk_of(FW))
            norm_hi(1)
            item_high(ff_first["up"][2], *ff_first["up"][:2], ff_chunk_of(FW))
            act.wait_ge(chunk_done, NCI)
            silus(0)
            with act.Fori(0, FB - 1) as i:
                q = i * CB + ff_chunks1
                v = lambda k: (ff_slot[k], i * ff_inc[k] + (ff_fill1[k] + ff_inc[k]))
                item_high(q, *v("gate"), ff_chunk_of(FW))
                midT_high(i * NT)
                item_high(q + NCI, *v("down"), ff_down_chunk)
                act.wait_ge(chunk_done, q + NCI)
                silus(i * NT + NT)
                item_high(q + 2 * NCI, *v("up"), ff_chunk_of(FW))
            midT_high((FB - 1) * NT)
            item_high(ff_last["down"][2], *ff_last["down"][:2], ff_down_chunk)

            norm_stats(2)
            gates1()
            proj_end = lambda j: o_in[j][1][2] + NCI

            def evac(j):
                if j in (1, 2):
                    act.wait_ge(chunk_done, proj_end(j))
                    for t in range(NT):
                        fn(q_tok[:, t, 8 * j - 8:8 * j, ROPE:], heads(ps[2 * j + t][:, 0:384], 8), ACT.Copy).then_inc(nope_done, 1)
                if j == 3:
                    act.wait_ge(chunk_done, proj_end(j))
                    for t in range(NT):
                        fn(ckr[:, t, :], ps[6 + t][:, 0:LAT + ROPE], ACT.Copy).then_inc(nope_done, 1)
                if j == 4:
                    act.wait_ge(chunk_done, proj_end(j))
                    for t in range(NT):
                        fn(q_i[:, t, :, ROPE:], heads(ps[t][:, :], 8)[:, :, ROPE:], ACT.Copy).then_inc(nope_done, 1)

            for j in range(6):
                q, (slot, value, _) = o_in[j][1][2], o_in[j][1]
                chunk = ff_chunk_of(o_cols[j][1])
                item_high(q, slot, value, chunk, (0, 1))
                if j == 0:
                    item_high(q, slot, value, chunk, (2, 3))
                    norm_hi(2)
                else:
                    evac(j - 1)
                    item_high(q, slot, value, chunk, (2, 3))
            act.wait_ge(nope_done, 10)
            act.wait_ge(x_ready, 2 * KD)
            rms(lambda t: ckr[:, t, 0:LAT], lambda t: flat_uT[:, t * LAT:(t + 1) * LAT], LAT, 0)
            step.wait()
            act.wait_ge(chunk_done, proj_end(5))
            for i in range(4):
                t, half = i // 2, i % 2
                act.wait_ge(kv_done, i + 1)
                fn(kcat[:, t, 8 * half:8 * half + 8, ROPE:], heads(ps[4 + i][:, 0:384], 8), ACT.Copy).then_inc(kn_ready, 1)
            for i in range(2):
                act.wait_ge(idxT_done, i + 1)
                fn(qiT[:, 2 * i:2 * i + 2, :], ps[4 + i][:, :].rearrange("p (c s) -> p c s", c=2), ACT.Copy).then_inc(idxT_ready, 1)
            for i in range(IH):
                act.wait_ge(logit_done, i + 1)
                if i >= 2:
                    act.wait_ge(score_added, i - 1)
                fn(sm[:, i % 2, :], ps[i % 2][:, 0:KW], ACT.Relu, scale=SC).then_inc(relu_ready, 1)
            for i in range(8):
                act.wait_ge(qkT_done, 5 + i)
                dst = (qT1, kT1)[i // 4]
                fn(dst[:, 2 * (i % 4):2 * (i % 4) + 2, :], ps[4 + i % 4][:, :].rearrange("p (c s) -> p c s", c=2),
                   ACT.Copy).then_inc(qkT_ready, 1)
            exps(A_HEADS, True)
            for hh in range(C_HEADS):
                n = A_HEADS + hh
                if hh + 1 < C_HEADS:
                    exps(n + 1, True)
                probs(n)
                if hh and hh % 2 == 0:
                    head_out(n - 1, ctxT, hh // 2 - 1)
                probsT_out(n)
            head_out(A_HEADS + C_HEADS - 1, ctxT, C_HEADS // 2 - 1)

            norm_stats(3)
            norm_out(3)
            act.wait_ge(gap_ready, 1)
            fn(rt[:, :, 40:41], rt[:, :, 41:42], ACT.Exp).then_inc(gap_exp, 1)

            UF = FB * NT

            def slots_high(g):
                for i in range(2):
                    act.wait_ge(x_e_ready, g * 2 + (i + 1))
                    fn(e_hi[:, 4 * i:4 * i + 4, :], x_e[:, 4 * i:4 * i + 4, :], ACT.Copy).then_inc(e_hi_ready, 1)

            def expert(job, g, gather_next):
                def convert(kind, b, cs=range(NCI)):
                    m = moe_at[kind, b]
                    item_high(job * CE + (moe_c0 + NCI * m), m % NS1,
                              job * (16 * PER) + (moe_fill0[m % NS1] + 16 * (m // NS1 + 1)), moe_chunk, cs)

                def silu_of(b):
                    act.wait_ge(chunk_done, job * CE + (moe_c0 + NCI * (moe_at["gate", b] + 1)))
                    act.wait_ge(midT_done, job * MB + (UF + b))
                    fn(mid_e[:, :], ps[0][:, :], ACT.Silu).then_inc(silu_done, 1)

                def midT_high_of(b):
                    act.wait_ge(midT_done, job * MB + (UF + b + 1))
                    fn(eT_hi[:, :, :], ps[2][:, :].rearrange("p (i t) -> p i t", i=4), ACT.Copy).then_inc(midT_hi_ready, 1)

                for b in range(MB):
                    convert("gate", b, (0,))
                    if b == 1:
                        silu_of(0)
                    convert("gate", b, (1, 2, 3))
                    convert("up", b)
                    if b:
                        midT_high_of(b - 1)
                        convert("down", b - 1, (0, 1))
                        silu_of(b)
                        convert("down", b - 1, (2, 3))
                convert("down", MB - 1, (0, 1))
                if gather_next:
                    slots_high(g + 1)
                midT_high_of(MB - 1)
                convert("down", MB - 1, (2, 3))

            slots_high(0)
            with act.Fori(0, E) as e:
                expert(e, e, True)
            act.wait_ge(tables_ready, 1)
            with act.If(act.value_load(job_tab[0:1, 2 * E:2 * E + 1], min_val=0, max_val=E) > 0):
                with act.Fori(0, E) as e:
                    n_e = act.value_load(job_tab[0:1, bass.ds(e, 1)], min_val=0, max_val=S)
                    with act.If(n_e > OVER):
                        job = act.value_load(job_tab[0:1, bass.ds(e + E, 1)], min_val=E, max_val=2 * E)
                        slots_high(job + 1)
                        expert(job, job + 1, False)
            norm_stats(4)

        @block.vector
        def _(dve):
            V = nc.vector
            par = lambda i: s5_p[:, i, :]
            step = Steps(dve, dve_steps)

            def chained(ins):
                step(ins)
                step.wait()

            V.memset(eps[:, :], EPS).then_inc(eps_ready, 1)

            def columns(i, psum, j, mods):
                a = psum
                chained(V.tensor_tensor(b_col[:, 2 * i:2 * i + 2, :], a, b_col[:, 2 * i:2 * i + 2, :], ALU.add))
                step(V.tensor_copy(mod_b[:, i, :], b_col[:, 2 * i, :]))
                V.scalar_tensor_tensor(mod_a[:, i, :], b_col[:, 2 * i + 1, :], 1.0, g_col[:, j, :], ALU.add,
                                       ALU.mult).then_inc(mod_ready, 1)

            def ada0_item(n, o, first):
                ap, (slot, value, _) = ada0[n]
                dve.wait_ge(fill[slot], value)
                for k in range(KD):
                    if k == 0 and first:
                        w = V.tensor_scalar(o, ap[:, k, :], c_col[:, k:k + 1], None, ALU.mult)
                    else:
                        w = V.scalar_tensor_tensor(o, ap[:, k, :], c_col[:, k:k + 1], o, ALU.mult, ALU.add)
                    if k < KD - 1:
                        chained(w)
                w.then_inc(ada_used, 1)

            def columns(i, bank):
                a = ps[bank][:, 0:2 * KD].rearrange("p (a k) -> p a k", a=2)
                chained(V.tensor_tensor(b_col[:, 2 * i:2 * i + 2, :], a, b_col[:, 2 * i:2 * i + 2, :], ALU.add))
                step(V.tensor_copy(mod_b[:, i, :], b_col[:, 2 * i, :]))
                V.scalar_tensor_tensor(mod_a[:, i, :], b_col[:, 2 * i + 1, :], 1.0, g_col[:, 2 * i, :], ALU.add,
                                       ALU.mult).then_inc(mod_ready, 1)

            def mod1():
                dve.wait_ge(mod_summed, 7)
                m = lambda i: ps[4][:, i * KD:(i + 1) * KD]
                for j in range(2):
                    V.tensor_copy(mod_b[:, j, :], m(2 * j))
                    w = V.scalar_tensor_tensor(mod_a[:, j, :], m(2 * j + 1), 1.0, g_col[:, 2 * j + 1, :], ALU.add, ALU.mult)
                w.then_inc(mod_ready, 1)

            def low(q, c, src, n=P):
                dve.wait_ge(hi_ready, q + 1)
                f = src.free_size()
                V.tensor_tensor(w_lo[0:n, c, 0:f], src, w_hi[0:n, c, 0:f].bitcast(F32), ALU.subtract).then_inc(lo_ready, 1)

            def item_low(q, slot, chunk, chunks=range(NCI)):
                for c in chunks:
                    low(q + c, c, *chunk(slot, c))

            def norm_scale(n, count):
                dve.wait_ge(rms_ready, count)
                chained(V.reciprocal(stat[:, 4:6], stat[:, 2:4]))
                for t in range(NT):
                    V.tensor_scalar(hn[:, t, :], h[:, t, :], stat[:, 4 + t:5 + t], None, ALU.mult).then_inc(hn_ready, 1)

            def norm_out(n):
                m = n % 2
                for k in (2, 3, 6, 7):
                    dve.wait_ge(hnT_done, 4 * n + k // 2 + 1)
                    V.tensor_scalar(uT[:, k, :], ps[k // 2][:, (k % 2) * S:(k % 2 + 1) * S], mod_a[:, m, k:k + 1], mod_b[:, m, k:k + 1],
                                    ALU.mult, ALU.add).then_inc(uT_ready, 1)

            def norm_split(n):
                m = n % 2
                for k in range(KD):
                    dve.wait_ge(hnT_done, 4 * n + k // 2 + 1)
                    V.tensor_scalar(uT[:, k, :], ps[k // 2][:, (k % 2) * S:(k % 2 + 1) * S], mod_a[:, m, k:k + 1],
                                    mod_b[:, m, k:k + 1], ALU.mult, ALU.add).then_inc(uT_ready, 1)
                for k in range(KD):
                    dve.wait_ge(x_hi_ready, KD * (n - 1) + k + 1)
                    V.tensor_tensor(x_lo[:, k, :], uT[:, k, :], x_hi[:, k, :].bitcast(F32), ALU.subtract).then_inc(x_ready, 1)

            def rope(dst, src, t, n, sem_):
                x1, x2 = src[:, :, 0:HALF], src[:, :, HALF:ROPE]
                a, b = rope_buf[:, 0, 0:n, :], rope_buf[:, 1, 0:n, :]
                step(V.tensor_tensor(a, x1, cos(t, n), ALU.mult))
                chained(V.tensor_tensor(b, x2, sin(t, n), ALU.mult))
                chained(V.tensor_tensor(dst[:, :, 0:HALF], a, b, ALU.subtract))
                step(V.tensor_tensor(a, x2, cos(t, n), ALU.mult))
                chained(V.tensor_tensor(b, x1, sin(t, n), ALU.mult))
                V.tensor_tensor(dst[:, :, HALF:ROPE], a, b, ALU.add).then_inc(sem_, 1)

            def heads(ap, n):
                return ap.rearrange("p (h d) -> p h d", h=n)

            def mask_max(n, neg):
                dve.wait_ge(score_done, n + 1)
                if n >= 3:
                    dve.wait_ge(pT_done, n - 2)
                q = n % 3
                for t in range(NT):
                    c = slice(KOFF[t], KOFF[t] + KEYS[t])
                    step(V.tensor_tensor_reduce(out=sm[:, q, c], in0=ps[n % 2][:, c], in1=neg[:, c], scale=1.0, scalar=NEG,
                                                op0=ALU.add, op1=ALU.max, accum_out=stat[:, 6 + 2 * q + t:7 + 2 * q + t]))
                step.wait()
                V.tensor_scalar(stat[:, 12 + 2 * q:14 + 2 * q], stat[:, 6 + 2 * q:8 + 2 * q], -SC, None,
                                ALU.mult).then_inc(max_ready, 1)

            def weights_sum(n, l1):
                dve.wait_ge(exp_ready, n + 1)
                q = n % 3
                den, rden = stat[:, 18 + 2 * q:20 + 2 * q], stat[:, 24 + 2 * q:26 + 2 * q]
                if not l1:
                    for t in range(NT):
                        x = sm[:, q, KOFF[t]:KOFF[t] + KEYS[t]]
                        c = cst[:, C_CNT + KOFF[t]:C_CNT + KOFF[t] + KEYS[t]]
                        step(V.tensor_tensor_reduce(out=x, in0=x, in1=c, scale=1.0, scalar=0.0, op0=ALU.mult, op1=ALU.add,
                                                    accum_out=den[:, t:t + 1]))
                    step.wait()
                V.reciprocal(rden, den).then_inc(rden_ready, 1)

            def residual(count, m, base, in0=None, h0=0):
                for i in range(4):
                    n, t = i // 2, i % 2
                    if in0 is None:
                        dve.wait_ge(mix_out_done, base + i + 1)
                        y = ps[4 + 2 * n + t][:, :]
                    else:
                        y = in0(n, t)
                    tmp = flat_uT[:, i * 512:(i + 1) * 512]
                    chained(V.tensor_tensor(tmp, y, gate_row[:, m, n * 512:(n + 1) * 512], ALU.mult))
                    x = h[:, t, n * 512:(n + 1) * 512]
                    V.tensor_tensor(x, x, tmp, ALU.add).then_inc(h_ready, 1)

            def ada_scale(slot, ks):
                for k in ks:
                    x = block_ap(slot, KD, ADA1)[:, k, :]
                    w = V.tensor_scalar(x, x, c_col[:, k:k + 1], None, ALU.mult)
                if k == KD - 1:
                    w.then_inc(ada_scaled, 1)

            dve.wait_ge(c_ready, 1)
            ada0_item(0, acc0[:, 0:512], True)
            dve.wait_ge(s5_den, 1)
            V.reciprocal(par(RDEN), par(DEN)).then_inc(s5_rden, 1)
            ada0_item(1, acc0[:, 512:1024], True)
            norm_scale(0, 1)
            for n in (2, 3):
                ada0_item(n, acc0[:, n * 512:(n + 1) * 512], True)
            dve.wait_ge(mod_summed, 1)
            dve.wait_ge(cols_ready, 1)
            columns(0, 4)
            dve.wait_ge(mod_ready, 1)
            norm_out(0)

            def rope0(i):
                dve.wait_ge(nope_done, i + 1)
                t, a = i % 2, (i // 2) * 512
                rope(heads(qk_tok[:, t, a:a + 512], 8), heads(ps[i][:, :], 8), t, 8, rope_done)
                dve.wait_ge(rope_done, i + 1)

            for n in range(4):
                ada0_item(4 + n, acc0[:, n * 512:(n + 1) * 512], True)
                if n in (1, 2):
                    rope0(2 * n - 2)
                    rope0(2 * n - 1)
            dve.wait_ge(gate_bias_in, 16 * 2)
            for n in range(2):
                ada0_item(8 + n, gate_row[:, 0, n * 512:(n + 1) * 512], False)
            for i, dst in ((0, qT), (2, kT)):
                dve.wait_ge(qkT_done, i + 1)
                V.tensor_copy(dst[:, 0:2, :], ps[i][:, :].rearrange("p (c s) -> p c s", c=2)).then_inc(qkT_ready, 1)
            neg0 = cst[:, C_NEG:C_NEG + KW]
            mask_max(0, neg0)
            mask_max(1, neg0)
            dve.wait_ge(mod_summed, 2)
            columns(1, 7)
            ada0_item(10, gate_row[:, 1, 0:512], False)

            def turn(j):
                dve.wait_ge(bu_done, j + 1)
                if j == 0:
                    dve.wait_ge(phase_ready, 1)
                bu = ps[6][:, :].rearrange("p (a s) -> p a s", a=2)
                c = lambda i: phase[:, i, j, :].unsqueeze(1).broadcast_to([P, 2, S])
                step.wait()
                step(V.tensor_tensor(rotA, bu, c(0), ALU.mult))
                V.tensor_tensor(rotB, bu, c(1), ALU.mult).then_inc(bu_used, 1)
                dve.wait_ge(bu_used, j + 1)
                step(V.tensor_tensor(s5_v[:, 0, :], rotA[:, 0, :], rotB[:, 1, :], ALU.add))
                chained(V.tensor_tensor(s5_v[:, 1, :], rotA[:, 1, :], rotB[:, 0, :], ALU.subtract))
                if j >= 2:
                    dve.wait_ge(post_ready, j - 1)
                z = zbuf[:, j % 2]
                for i in range(2):
                    w = V.tensor_tensor_scan(z[:, i, :], s5_p[:, MAG, j:j + 1].broadcast_to([P, S]), s5_v[:, i, :],
                                             0.0, ALU.mult, ALU.add)
                    if i == 0:
                        step(w)
                w.then_inc(z_ready, 1)
                dve.wait_ge(z_ready, j + 1)

            def y_before_gelu(t):
                dve.wait_ge(y_part_done, 4 * t + 4)
                V.scalar_tensor_tensor(s5_y[:, t, :], s_inT[:, t, :], s5_d[:, t:t + 1], ps[7][:, (t % 2) * S:(t % 2 + 1) * S],
                                       ALU.mult, ALU.add).then_inc(y_pre, 1)

            dve.wait_ge(vs_ready, 4)
            for hh in range(A_HEADS):
                turn(2 * hh)
                if hh % 2 and hh >= 3:
                    y_before_gelu((hh - 3) // 2)
                weights_sum(hh, False)
                turn(2 * hh + 1)
                if hh + 2 < A_HEADS:
                    mask_max(hh + 2, neg0)
            y_before_gelu(3)
            for c in range(4):
                dve.wait_ge(glu_tanh, c + 1)
                t = hn.rearrange("p t d -> p (t d)")[:, c * S:(c + 1) * S]
                chained(V.tensor_scalar(t, t, 0.5, 0.5, ALU.mult, ALU.add))
                V.tensor_tensor(catT[:, 4 + c, :], t, s5_y[:, c, :], ALU.mult).then_inc(cat_ready, 1)
            residual(0, 0, 0)

            norm_scale(1, 2)
            dve.wait_ge(mod_ready, 2)
            item_low(ff_first["gate"][2], ff_first["gate"][0], ff_chunk_of(FW))
            norm_split(1)
            item_low(ff_first["up"][2], ff_first["up"][0], ff_chunk_of(FW))
            dve.wait_ge(fill[ff_first["ada1"][0]], ff_first["ada1"][1])
            ada_scale(ff_first["ada1"][0], range(KD))

            def mids(u0, q):
                dve.wait_ge(chunk_done, q)
                for t in range(NT):
                    dve.wait_ge(silu_done, u0 + t + 1)
                    V.tensor_tensor(mid[:, t, :], mid[:, t, :], ps[2 + t][:, 0:FW], ALU.mult).then_inc(mid_ready, 1)

            def midT_low(u0):
                for t in range(NT):
                    dve.wait_ge(midT_hi_ready, u0 + t + 1)
                    V.tensor_tensor(mT_lo[:, t, 0:2, :], ps[2 + t][:, 0:2 * P].rearrange("p (i t) -> p i t", i=2),
                                    mT_hi[:, t, 0:2, :].bitcast(F32), ALU.subtract)
                    n = FT[2][1]
                    V.tensor_tensor(mT_lo[0:n, t, 2, :], ps[2 + t][0:n, 2 * P:3 * P], mT_hi[0:n, t, 2, :].bitcast(F32),
                                    ALU.subtract).then_inc(midT_ready, 1)

            def add_ada(i):
                for j in range(2):
                    dve.wait_ge(ada_used, i * 2 + (NA0 + j + 1))
                    o = ada[:, bass.ds(i * (2 * ADA1) + j * ADA1, ADA1)]
                    V.tensor_tensor(o, o, ada_acc[:, j, :], ALU.add).then_inc(ada_added, 1)

            dve.wait_ge(bias_in, 16)

            def scale_ada(i, ks):
                if isinstance(i, int) and i == 0:
                    return
                if ks[0] == 0:
                    dve.wait_ge(fill[ff_slot["ada1"]], (i - 1) * 16 + (ff_fill1["ada1"] + 16))
                ada_scale(ff_slot["ada1"], ks)

            def ff_block(i):
                q = i * CB + ff_chunks1
                item_low(q, ff_slot["gate"], ff_chunk_of(FW), (0, 1))
                mids(i * NT, q)
                item_low(q, ff_slot["gate"], ff_chunk_of(FW), (2,))
                scale_ada(i, range(0, KD // 2))
                item_low(q, ff_slot["gate"], ff_chunk_of(FW), (3,))
                midT_low(i * NT)
                scale_ada(i, range(KD // 2, KD))
                item_low(q + NCI, ff_slot["down"], ff_down_chunk)
                item_low(q + 2 * NCI, ff_slot["up"], ff_chunk_of(FW))
                add_ada(i)

            ff_block(0)
            with dve.Fori(1, FB - 1) as i:
                ff_block(i)
            mids((FB - 1) * NT, ff_last["down"][2])
            scale_ada(FB - 1, range(0, KD))
            midT_low((FB - 1) * NT)
            item_low(ff_last["down"][2], ff_last["down"][0], ff_down_chunk)
            add_ada(FB - 1)
            dve.wait_ge(chunk_done, ff_last["down"][2] + NCI)
            residual(0, 1, 0, lambda n, t: ps[4 + 2 * t + n][:, :])

            mod1()
            norm_scale(2, 3)
            dve.wait_ge(mod_ready, 3)
            proj_end = lambda j: o_in[j][1][2] + NCI

            def rope_out(j):
                if j == 0:
                    for t in range(NT):
                        dve.wait_ge(chunk_done, proj_end(0))
                        rope(q_tok[:, t], heads(ps[t][:, 0:256], 16), t, 16, rope_done)
                        dve.wait_ge(rope_done, 5 + t)
                if j == 4:
                    for t in range(NT):
                        dve.wait_ge(nope_done, 11 + t)
                        rope(q_i[:, t], heads(ps[t][:, :], 8), t, 8, rope_done)
                        dve.wait_ge(rope_done, 7 + t)

            for j in range(6):
                q, slot = o_in[j][1][2], o_in[j][1][0]
                chunk = ff_chunk_of(o_cols[j][1])
                item_low(q, slot, chunk, (0, 1))
                if j == 0:
                    item_low(q, slot, chunk, (2, 3))
                    norm_split(2)
                else:
                    rope_out(j - 1)
                    item_low(q, slot, chunk, (2, 3))
            dve.wait_ge(rms_ready, 4)
            chained(V.reciprocal(stat[:, 4:6], stat[:, 2:4]))
            for t in range(NT):
                V.tensor_scalar(ckr[:, t, 0:LAT], ckr[:, t, 0:LAT], stat[:, 4 + t:5 + t], None, ALU.mult).then_inc(ckv_ready, 1)
            for t in range(NT):
                dve.wait_ge(chunk_done, proj_end(5))
                kk = k_iw[:, t, :]
                step(V.tensor_copy(kk[:, ROPE:HD], ps[2 + t][:, ROPE:HD]))
                step(V.tensor_scalar(kk[:, 2 * HD:], ps[2 + t][:, HD:HD + IH], IH ** -0.5, None, ALU.mult))
                rope(kk[:, 0:HD].unsqueeze(1), ps[2 + t][:, 0:HD].unsqueeze(1), t, 1, rope_done)
                dve.wait_ge(rope_done, 9 + t)
                step.wait()
                step(V.tensor_copy(kk[:, HD:2 * HD], kk[:, 0:HD]))
            for k in range(2):
                dve.wait_ge(ckvT_done, 1)
                V.tensor_scalar(ckvT[:, k, :], ps[4][:, k * S:(k + 1) * S], g_kv[:, k:k + 1], None, ALU.mult).then_inc(ckvT_ready, 1)
            for t in range(NT):
                kr = kr_t[:, :].unsqueeze(1)
                rope(kr, ckr[:, t, LAT:].unsqueeze(1), t, 1, dve_steps)
                step.n += 1
                step.wait()
                V.tensor_copy(kcat[:, t, :, 0:ROPE], kr.broadcast_to([P, C_HEADS, ROPE])).then_inc(rope_done, 1)
                dve.wait_ge(rope_done, 11 + t)
            for i in range(4):
                t, half = i // 2, i % 2
                dve.wait_ge(kv_done, 5 + i)
                V.tensor_copy(v1[:, t, half * 512:(half + 1) * 512], ps[i][:, :]).then_inc(v_ready, 1)
            dve.wait_ge(idxT_done, 3)
            V.tensor_copy(kiT[:, :], ps[6][:, 0:S]).then_inc(idxT_ready, 1)
            for i in range(IH):
                dve.wait_ge(relu_ready, i + 1)
                for t in range(NT):
                    c = slice(KOFF[t], KOFF[t] + KEYS[t])
                    wi = k_iw[:, t, 2 * HD + i:2 * HD + i + 1]
                    if i == 0:
                        w = V.tensor_scalar(score[:, c], sm[:, 0, c], wi, None, ALU.mult)
                    else:
                        w = V.scalar_tensor_tensor(score[:, c], sm[:, i % 2, c], wi, score[:, c], ALU.mult, ALU.add)
                w.then_inc(score_added, 1)
                dve.wait_ge(score_added, i + 1)
            chained(V.tensor_tensor(score, score, cst[:, C_CB:C_CB + KW], ALU.add))
            for i in range(TOPK // 8):
                for t in range(NT):
                    step(V.max(top8[:, t, :], score[:, KOFF[t]:KOFF[t] + KEYS[t]]))
                step.wait()
                for t in range(NT):
                    x = score[:, KOFF[t]:KOFF[t] + KEYS[t]]
                    step(V.match_replace(x, top8[:, t, :], x, NEG))
                step.wait()
            chained(V.tensor_scalar(selneg, score, NEG / 3, BIG, ALU.is_le, ALU.mult))
            chained(V.tensor_tensor(selneg, selneg, cst[:, C_CAU:C_CAU + KW], ALU.mult))
            chained(V.tensor_scalar(selneg, selneg, BIG, None, ALU.subtract))
            mask_max(A_HEADS, selneg)
            mask_max(A_HEADS + 1, selneg)
            for hh in range(C_HEADS):
                n = A_HEADS + hh
                weights_sum(n, True)
                if hh + 2 < C_HEADS:
                    mask_max(n + 2, selneg)
            residual(0, 0, 4)

            norm_scale(3, 5)
            dve.wait_ge(late_in, 16 * 2)
            norm_out(3)
            dve.wait_ge(router_done, 1)
            for t in range(NT):
                step(V.tensor_tensor(lg[:, t, :], ps[4][:, t * E:(t + 1) * E], b_r[:, :], ALU.add))
            step(V.memset(possel[:, :, E:E + 1], -1.0))
            step(V.memset(comb[:, :, E:E + 1], 0.0))
            step.wait()
            for t in range(NT):
                step(V.max(top[:, t, :], lg[:, t, :]))
            step.wait()
            for t in range(NT):
                step(V.max_index(top_i[:, t, :], top[:, t, :], lg[:, t, :]))
            step.wait()
            step(V.tensor_copy(rt[:, :, 24:26], top_i[:, :, 0:2]))
            V.tensor_tensor(rt[:, :, 41:42], top[:, :, 1:2], top[:, :, 0:1], ALU.subtract).then_inc(gap_ready, 1)
            step.wait()
            for t in range(NT):
                for i in range(2):
                    step(V.tensor_scalar(rt[:, t, 8 * i:8 * i + 8], iota(E), rt[:, t, 24 + i:25 + i], None, ALU.is_equal))
            step.wait()
            V.tensor_tensor(rt[:, :, 16:24], rt[:, :, 0:8], rt[:, :, 8:16], ALU.add).then_inc(member_ready, 1)
            dve.wait_ge(gap_exp, 1)
            chained(V.tensor_scalar(rt[:, :, 42:43], rt[:, :, 40:41], 1.0, None, ALU.add))
            chained(V.reciprocal(rt[:, :, 43:44], rt[:, :, 42:43]))
            chained(V.tensor_tensor(rt[:, :, 44:45], rt[:, :, 40:41], rt[:, :, 43:44], ALU.mult))
            for t in range(NT):
                chained(V.tensor_scalar(comb[:, t, 0:E], rt[:, t, 0:8], rt[:, t, 43:44], None, ALU.mult))
                chained(V.scalar_tensor_tensor(comb[:, t, 0:E], rt[:, t, 8:16], rt[:, t, 44:45], comb[:, t, 0:E], ALU.mult, ALU.add))
            dve.wait_ge(pos_done, 1)
            dve.wait_ge(member_ready, 1)
            for t in range(NT):
                chained(V.scalar_tensor_tensor(possel[:, t, 0:E], ps[5][:, t * E:(t + 1) * E], 1.0, rt[:, t, 16:24], ALU.add, ALU.mult))
            chained(V.tensor_scalar(possel[:, :, 0:E], possel[:, :, 0:E], -1.0, None, ALU.add))
            cnt, rnd, over = jobs[:, 0:E], jobs[:, E:2 * E], jobs[:, 2 * E:3 * E]
            chained(V.tensor_copy(cnt, ps[5][:, 2 * E:3 * E]))
            chained(V.tensor_scalar(over, cnt, OVER + 0.5, None, ALU.is_gt))
            chained(V.tensor_tensor_scan(rnd, ones[:, 0:E], over, 0.0, ALU.mult, ALU.add))
            step(V.tensor_copy(job_tab[:, 0:E], cnt))
            step(V.tensor_copy(job_tab[:, 2 * E:2 * E + 1], rnd[:, E - 1:E]))
            step.wait()
            chained(V.tensor_tensor(rnd, rnd, over, ALU.subtract))
            chained(V.tensor_scalar(rnd, rnd, float(E), None, ALU.add))
            V.tensor_copy(job_tab[:, E:2 * E], rnd).then_inc(tables_ready, 1)
            for t in range(NT):
                step(V.tensor_copy(info[:, t, 0:1], cst[:, C_TOK + t:C_TOK + t + 1]))

            UF = FB * NT

            def select(e, g, rnd_):
                step.wait()
                for t in range(NT):
                    step(V.tensor_scalar(cur[:, t, 0:1], possel[:, t, bass.ds(e, 1)], float(-P * rnd_), None, ALU.add))
                    step(V.tensor_copy(info[:, t, 1:2], comb[:, t, bass.ds(e, 1)]))
                step.wait()
                for t in range(NT):
                    w = V.tensor_scalar(sel[:, t, :], iota(P), cur[:, t, 0:1], None, ALU.is_equal)
                    if t == 0:
                        step(w)
                w.then_inc(sel_ready, 1)

            def slots_in(g):
                for i in range(2):
                    dve.wait_ge(gather_done, g * 2 + (i + 1))
                    for k in range(4 * i, 4 * i + 4):
                        w = V.tensor_scalar(x_e[:, k, :], ps[6 + i][:, (k % 4) * P:(k % 4 + 1) * P], mod_a[:, 1, k:k + 1],
                                            mod_b[:, 1, k:k + 1], ALU.mult, ALU.add)
                    w.then_inc(x_e_ready, 1)
                for i in range(2):
                    dve.wait_ge(e_hi_ready, g * 2 + (i + 1))
                    k = slice(4 * i, 4 * i + 4)
                    V.tensor_tensor(e_lo[:, k, :], x_e[:, k, :], e_hi[:, k, :].bitcast(F32), ALU.subtract).then_inc(e_ready, 1)

            def back(g, job):
                dve.wait_ge(info_done, g + 1)
                chained(V.tensor_copy(slot_info, ps[3][:, 0:2]))
                V.tensor_scalar(selT, iota(S), slot_info[:, 0:1], slot_info[:, 1:2], ALU.is_equal,
                                ALU.mult).then_inc(selT_ready, 1)

            def expert(job, e_next, g, gather_next):
                def convert(kind, b, cs=range(NCI)):
                    m = moe_at[kind, b]
                    item_low(job * CE + (moe_c0 + NCI * m), m % NS1, moe_chunk, cs)

                def mids_of(b):
                    dve.wait_ge(chunk_done, job * CE + (moe_c0 + NCI * (moe_at["up", b] + 1)))
                    dve.wait_ge(silu_done, job * MB + (UF + b + 1))
                    V.tensor_tensor(mid_e[:, :], mid_e[:, :], ps[1][:, :], ALU.mult).then_inc(mid_ready, 1)

                def midT_low_of(b):
                    dve.wait_ge(midT_hi_ready, job * MB + (UF + b + 1))
                    V.tensor_tensor(eT_lo[:, :, :], ps[2][:, :].rearrange("p (i t) -> p i t", i=4),
                                    eT_hi[:, :, :].bitcast(F32), ALU.subtract).then_inc(midT_ready, 1)

                for b in range(MB):
                    convert("gate", b, (0,))
                    if b:
                        mids_of(b - 1)
                    convert("gate", b, (1, 2, 3))
                    convert("up", b)
                    if b == 0:
                        back(g, job)
                        if gather_next:
                            select(e_next, g + 1, 0)
                    else:
                        midT_low_of(b - 1)
                        convert("down", b - 1)
                convert("down", MB - 1, (0, 1))
                mids_of(MB - 1)
                if gather_next:
                    slots_in(g + 1)
                midT_low_of(MB - 1)
                convert("down", MB - 1, (2, 3))
                dve.wait_ge(chunk_done, job * CE + (moe_c0 + CE))
                for half in range(2):
                    n = slice(half * 512, (half + 1) * 512)
                    V.tensor_tensor(y_sb[:, n], ps[4 + half][:, :], gate_row[:, 1, n], ALU.mult).then_inc(y_sb_ready, 1)
                for i in range(4):
                    t, half = i // 2, i % 2
                    dve.wait_ge(scatter_done, job * 4 + (i + 1))
                    y = h[:, t, half * 512:(half + 1) * 512]
                    V.tensor_tensor(y, y, ps[4 + i][:, :], ALU.add).then_inc(scatter_added, 1)

            select(0, 0, 0)
            slots_in(0)
            with dve.Fori(0, E) as e:
                step.enter(e, 0, 6)
                expert(e, e + 1, e, True)
            step.leave(0, E)
            n_over = dve.value_load(job_tab[0:1, 2 * E:2 * E + 1], min_val=0, max_val=E)
            with dve.If(n_over > 0):
                with dve.Fori(0, E) as e:
                    n_e = dve.value_load(job_tab[0:1, bass.ds(e, 1)], min_val=0, max_val=S)
                    with dve.If(n_e > OVER):
                        job = dve.value_load(job_tab[0:1, bass.ds(e + E, 1)], min_val=E, max_val=2 * E)
                        step.enter(job, E, 6)
                        select(e, job + 1, 1)
                        slots_in(job + 1)
                        expert(job, None, job + 1, False)
            step.sem, step.n, step.reg = final_steps, 0, None
            dve.wait_ge(scatter_added, n_over * 4 + 4 * E)
            V.memset(eps[:, :], EPS).then_inc(experts_done, 1)

            dve.wait_ge(rms_ready, 6)
            V.reciprocal(stat[:, 4:6], stat[:, 2:4]).then_inc(stat_ready, 1)
            dve.wait_ge(stat_ready, 1)
            dve.wait_ge(late_in, 16 * 3)
            for t in range(NT):
                V.scalar_tensor_tensor(final_y[:, t, :], h[:, t, :], stat[:, 4 + t:5 + t], gate_row[:, 0, :],
                                       ALU.mult, ALU.mult).then_inc(y_final, 1)


_INS = ["x", "c", "w_ada", "b_ada", "g_mix", "g_ffn", "g_final", "e_w_in", "e_w_out", "s5_a_re", "s5_a_im",
        "s5_log_dt", "s5_b_re", "s5_b_im", "s5_c_re", "s5_c_im", "s5_d", "s5_w_glu", "s5_b_glu",
        "ff_w_gate", "ff_w_up", "ff_w_down", "o_w_in", "o_w_out", "mla_g_kv", "mla_w_uk", "mla_w_uv",
        "moe_w_router", "moe_b_router", "moe_w_gate", "moe_w_up", "moe_w_down"]


def kernel(**inputs):
    import concourse.bacc as bacc
    from concourse.bass_utils import run_bass_kernel_spmd as run

    nc = bacc.Bacc("TRN2", target_bir_lowering=False, num_devices=1)
    arrays, aps = {}, {}
    for name in _INS:
        a = np.ascontiguousarray(inputs[name])
        arrays[f"in_{name}"] = a
        aps[name] = nc.dram_tensor(f"in_{name}", a.shape, mybir.dt.from_np(a.dtype), kind="ExternalInput").ap()
    consts = constants()
    arrays["in_consts"] = consts
    aps["consts"] = nc.dram_tensor("in_consts", consts.shape, F32, kind="ExternalInput").ap()
    out = nc.dram_tensor("out_0", (1, S, D), F32, kind="ExternalOutput").ap()
    trunk(nc, aps, out)
    r = run(nc, [arrays], core_ids=[0])
    return r.results[0]["out_0"]
```
